# Optimizing a Trainium2 kernel written in Bass

```python
import jax, jax.numpy as jnp
from jax import lax
import numpy as np

D_MODEL = 1024
BATCH = 1
SEQ = 512
DEPTH = 1

GRID_W = 64
CTX_LEN = 256
N_HEADS = 8
N_KV_HEADS = 2
HEAD_DIM = 64
GQA_GROUP = N_HEADS // N_KV_HEADS
ATT_WIDTH = N_HEADS * HEAD_DIM
KV_WIDTH = N_KV_HEADS * HEAD_DIM
CONV_WIDTH = D_MODEL - ATT_WIDTH
CONV_GROUPS = 8
CONV_K = 3
WINDOW = 128
BLOCK = 128
ROPE_THETA = 10000.0
N_EXPERTS = 16
EC_CAPACITY_FACTOR = 2
D_EXPERT = 1024
EPS = 1e-6
IN_WIDTH = ATT_WIDTH + 2 * KV_WIDTH + 3 * CONV_WIDTH
SPLIT_POINTS = [ATT_WIDTH, ATT_WIDTH + KV_WIDTH, ATT_WIDTH + 2 * KV_WIDTH,
                ATT_WIDTH + 2 * KV_WIDTH + CONV_WIDTH, ATT_WIDTH + 2 * KV_WIDTH + 2 * CONV_WIDTH]


def rmsnorm(x, g):
    xf = x.astype(jnp.float32)
    r = xf * lax.rsqrt(jnp.mean(xf * xf, axis=-1, keepdims=True) + EPS)
    return (r * g.astype(jnp.float32)).astype(x.dtype)

def modulate(h, shift, scale):
    return h * (1 + scale) + shift

def axial_rope_tables(seq_len):
    rows = seq_len // GRID_W
    row = jnp.repeat(jnp.arange(rows), GRID_W, total_repeat_length=rows * GRID_W)
    col = jnp.tile(jnp.arange(GRID_W), rows)
    n_freq = HEAD_DIM // 4
    inv = ROPE_THETA ** (-jnp.arange(n_freq, dtype=jnp.float32) / n_freq)
    ang = jnp.concatenate([row.astype(jnp.float32)[:, None] * inv,
                           col.astype(jnp.float32)[:, None] * inv], axis=-1)
    return jnp.cos(ang), jnp.sin(ang)

def apply_rope(x, cos, sin):
    xf = x.astype(jnp.float32)
    half = HEAD_DIM // 2
    x1, x2 = xf[..., :half], xf[..., half:]
    cs, sn = cos[None, :, None, :], sin[None, :, None, :]
    return jnp.concatenate([x1 * cs - x2 * sn, x1 * sn + x2 * cs], axis=-1).astype(x.dtype)

def windowed_attention(q, k, v, k_ctx, v_ctx, sink):
    bsz, seq, _, hd = q.shape
    nb = seq // BLOCK
    scale = hd ** -0.5
    qb = q.reshape(bsz, nb, BLOCK, N_KV_HEADS, GQA_GROUP, hd)
    pad = ((0, 0), (BLOCK, BLOCK), (0, 0), (0, 0))
    kp = jnp.pad(k, pad).reshape(bsz, nb + 2, BLOCK, N_KV_HEADS, hd)
    vp = jnp.pad(v, pad).reshape(bsz, nb + 2, BLOCK, N_KV_HEADS, hd)
    kb = jnp.concatenate([kp[:, :-2], kp[:, 1:-1], kp[:, 2:]], axis=2)
    vb = jnp.concatenate([vp[:, :-2], vp[:, 1:-1], vp[:, 2:]], axis=2)
    s_loc = jnp.einsum('bnqkgd,bnjkd->bnkgqj', qb, kb).astype(jnp.float32) * scale
    s_ctx = jnp.einsum('bnqkgd,bjkd->bnkgqj', qb, k_ctx).astype(jnp.float32) * scale
    i = jnp.arange(BLOCK)[None, :, None]
    j = jnp.arange(3 * BLOCK)[None, None, :]
    kpos = jnp.arange(nb)[:, None, None] * BLOCK + j - BLOCK
    valid = (jnp.abs(j - BLOCK - i) <= WINDOW) & (kpos >= 0) & (kpos < seq)
    s_loc = jnp.where(valid[None, :, None, None], s_loc, -jnp.inf)
    sk = jnp.broadcast_to(sink.astype(jnp.float32).reshape(N_KV_HEADS, GQA_GROUP)[None, None, :, :, None, None],
                          s_loc.shape[:-1] + (1,))
    p = jax.nn.softmax(jnp.concatenate([sk, s_ctx, s_loc], axis=-1), axis=-1)
    n_ctx = k_ctx.shape[1]
    p_ctx = p[..., 1:1 + n_ctx].astype(v.dtype)
    p_loc = p[..., 1 + n_ctx:].astype(v.dtype)
    out = (jnp.einsum('bnkgqj,bjkd->bnqkgd', p_ctx, v_ctx)
           + jnp.einsum('bnkgqj,bnjkd->bnqkgd', p_loc, vb))
    return out.reshape(bsz, seq, N_HEADS * hd)

def context_attention(q, k, v, sink):
    bsz, n, _, hd = q.shape
    qg = q.reshape(bsz, n, N_KV_HEADS, GQA_GROUP, hd)
    s = jnp.einsum('bqkgd,bjkd->bkgqj', qg, k).astype(jnp.float32) * hd ** -0.5
    sk = jnp.broadcast_to(sink.astype(jnp.float32).reshape(N_KV_HEADS, GQA_GROUP)[None, :, :, None, None],
                          s.shape[:-1] + (1,))
    p = jax.nn.softmax(jnp.concatenate([sk, s], axis=-1), axis=-1)[..., 1:].astype(v.dtype)
    return jnp.einsum('bkgqj,bjkd->bqkgd', p, v).reshape(bsz, n, N_HEADS * hd)

def short_conv_mixer(bg, cg, hv, conv_w):
    u = cg * hv
    up = jnp.pad(u, ((0, 0), (1, 1), (0, 0)))
    y = conv_w[0] * up[:, :-2] + conv_w[1] * up[:, 1:-1] + conv_w[2] * up[:, 2:]
    return bg * y

def expert_choice_ffn(h, w_router, w_gate, w_up, w_down):
    bsz, n, d = h.shape
    cap = EC_CAPACITY_FACTOR * n // N_EXPERTS
    aff = jax.nn.softmax((h @ w_router).astype(jnp.float32), axis=-1)
    g, idx = lax.top_k(jnp.swapaxes(aff, 1, 2), cap)
    xs = jax.vmap(lambda hb, ib: hb[ib])(h, idx)
    a = jnp.einsum('becd,edf->becf', xs, w_gate)
    u = jnp.einsum('becd,edf->becf', xs, w_up)
    y = jnp.einsum('becf,efd->becd', jax.nn.silu(a) * u, w_down) * g[..., None].astype(h.dtype)
    flat = (idx + (jnp.arange(bsz) * n)[:, None, None]).reshape(-1)
    out = jax.ops.segment_sum(y.reshape(-1, d), flat, num_segments=bsz * n)
    return out.reshape(bsz, n, d)

def first_inputs(seed: int = 0) -> dict:
    key = jax.random.key(seed)
    ks = jax.random.split(key, 17)
    D = D_MODEL
    nrm = jax.random.normal
    f32 = jnp.float32
    return {
        "x": nrm(ks[0], (BATCH, SEQ, D), f32),
        "c": nrm(ks[1], (BATCH, D), f32),
        "ctx": nrm(ks[2], (BATCH, CTX_LEN, D), f32),
        "c_ctx": nrm(ks[3], (D,), f32),
        "w_ada": nrm(ks[4], (DEPTH, D, 6 * D), f32) * (0.5 * D ** -0.5),
        "b_ada": nrm(ks[5], (DEPTH, 6 * D), f32) * 0.01,
        "g_mix": 1.0 + 0.1 * nrm(ks[6], (DEPTH, D), f32),
        "w_in": nrm(ks[7], (DEPTH, D, IN_WIDTH), f32) * D ** -0.5,
        "conv_w": nrm(ks[8], (DEPTH, CONV_K, CONV_WIDTH), f32) * CONV_K ** -0.5,
        "sink": nrm(ks[9], (DEPTH, N_HEADS), f32),
        "w_out": nrm(ks[10], (DEPTH, D, D), f32) * D ** -0.5,
        "g_ffn": 1.0 + 0.1 * nrm(ks[11], (DEPTH, D), f32),
        "w_router": nrm(ks[12], (DEPTH, D, N_EXPERTS), f32) * D ** -0.5,
        "w_gate": nrm(ks[13], (DEPTH, N_EXPERTS, D, D_EXPERT), f32) * D ** -0.5,
        "w_up": nrm(ks[14], (DEPTH, N_EXPERTS, D, D_EXPERT), f32) * D ** -0.5,
        "w_down": nrm(ks[15], (DEPTH, N_EXPERTS, D_EXPERT, D), f32) * D_EXPERT ** -0.5,
        "g_final": 1.0 + 0.1 * nrm(ks[16], (D,), f32),
    }

def first_block(x, c, ctx, c_ctx, w_ada, b_ada, g_mix, w_in, conv_w, sink, w_out, g_ffn,
              w_router, w_gate, w_up, w_down, g_final):
    bsz, seq, _ = x.shape
    cos, sin = axial_rope_tables(seq)
    for l in range(DEPTH):
        last = l == DEPTH - 1
        mod = jax.nn.silu(c) @ w_ada[l] + b_ada[l]
        sh1, sc1, gt1, sh2, sc2, gt2 = [m[:, None, :] for m in jnp.split(mod, 6, axis=-1)]
        mod_c = jax.nn.silu(c_ctx) @ w_ada[l] + b_ada[l]
        csh1, csc1, cgt1, csh2, csc2, cgt2 = jnp.split(mod_c, 6, axis=-1)

        hc = modulate(rmsnorm(ctx, g_mix[l]), csh1, csc1)
        n_ctx = ctx.shape[1]
        if last:
            kv_c = hc @ w_in[l][:, ATT_WIDTH:ATT_WIDTH + 2 * KV_WIDTH]
            k_c, v_c = jnp.split(kv_c, 2, axis=-1)
            k_c = k_c.reshape(bsz, n_ctx, N_KV_HEADS, HEAD_DIM)
            v_c = v_c.reshape(bsz, n_ctx, N_KV_HEADS, HEAD_DIM)
        else:
            q_c, k_c, v_c, bg_c, cg_c, hv_c = jnp.split(hc @ w_in[l], SPLIT_POINTS, axis=-1)
            q_c = q_c.reshape(bsz, n_ctx, N_HEADS, HEAD_DIM)
            k_c = k_c.reshape(bsz, n_ctx, N_KV_HEADS, HEAD_DIM)
            v_c = v_c.reshape(bsz, n_ctx, N_KV_HEADS, HEAD_DIM)
            att_c = context_attention(q_c, k_c, v_c, sink[l])
            conv_c = short_conv_mixer(bg_c, cg_c, hv_c, conv_w[l])
            ctx_new = ctx + cgt1 * (jnp.concatenate([att_c, conv_c], axis=-1) @ w_out[l])
            hc2 = modulate(rmsnorm(ctx_new, g_ffn[l]), csh2, csc2)
            ctx_new = ctx_new + cgt2 * expert_choice_ffn(hc2, w_router[l], w_gate[l], w_up[l], w_down[l])

        h = modulate(rmsnorm(x, g_mix[l]), sh1, sc1)
        q, k, v, bg, cg, hv = jnp.split(h @ w_in[l], SPLIT_POINTS, axis=-1)
        q = apply_rope(q.reshape(bsz, seq, N_HEADS, HEAD_DIM), cos, sin)
        k = apply_rope(k.reshape(bsz, seq, N_KV_HEADS, HEAD_DIM), cos, sin)
        v = v.reshape(bsz, seq, N_KV_HEADS, HEAD_DIM)
        att = windowed_attention(q, k, v, k_c, v_c, sink[l])
        conv = short_conv_mixer(bg, cg, hv, conv_w[l])
        x = x + gt1 * (jnp.concatenate([att, conv], axis=-1) @ w_out[l])

        h2 = modulate(rmsnorm(x, g_ffn[l]), sh2, sc2)
        x = x + gt2 * expert_choice_ffn(h2, w_router[l], w_gate[l], w_up[l], w_down[l])

        if not last:
            ctx = ctx_new
    return rmsnorm(x, g_final)


DEPTH_2 = 2

N_MIXERS = 2
N_POOL_LAYERS = (DEPTH_2 + 1) // 2
N_MLA_LAYERS = DEPTH_2 // 2
POOL_WINDOWS = (2, 4, 8, 16)
N_POOL_GROUPS = len(POOL_WINDOWS)
POOL_GROUP = D_MODEL // N_POOL_GROUPS
N_HEADS_2 = D_MODEL // 128
QK_NOPE = 128
QK_ROPE = 64
QK_HEAD = QK_NOPE + QK_ROPE
V_HEAD = 128
Q_LORA = 3 * D_MODEL // 4
KV_LORA = D_MODEL // 4
Q_BLOCK = 128
D_FF = 2816
FFN_HALF = 0.5


def rmsnorm_2(x, gain):
    x32 = x.astype(jnp.float32)
    y = x32 * lax.rsqrt(jnp.mean(x32 * x32, axis=-1, keepdims=True) + EPS)
    return (y * gain.astype(jnp.float32)).astype(x.dtype)

def swiglu(h, w_gate, w_up, w_down):
    return (jax.nn.silu(h @ w_gate) * (h @ w_up)) @ w_down

def pool_mixer(h, w, scale):
    B, S, D = h.shape
    u = h.astype(jnp.float32).reshape(B, S, N_POOL_GROUPS, POOL_GROUP)
    cs = jnp.pad(jnp.cumsum(u, axis=1), ((0, 0), (1, 0), (0, 0), (0, 0)))
    sums = []
    for g, w_len in enumerate(POOL_WINDOWS):
        c = cs[:, :, g]
        lower = jnp.pad(c[:, :S + 1 - w_len], ((0, 0), (w_len - 1, 0), (0, 0)))
        sums.append(c[:, 1:] - lower)
    window_sum = jnp.stack(sums, axis=2)
    t = jnp.arange(S)
    count = jnp.minimum(t[:, None] + 1, jnp.array(POOL_WINDOWS, jnp.int32)[None, :])
    pooled = window_sum / count.astype(jnp.float32)[None, :, :, None] - u
    y = jnp.einsum('bsgc,gcd->bsgd', pooled.astype(h.dtype), w).reshape(B, S, D)
    return y * scale

def rope_tail(x, cos, sin):
    x_nope, x_pe = jnp.split(x, [QK_NOPE], axis=-1)
    x1, x2 = jnp.split(x_pe, 2, axis=-1)
    c = cos[:, :, None, :].astype(x.dtype)
    s = sin[:, :, None, :].astype(x.dtype)
    return jnp.concatenate([x_nope, x1 * c - x2 * s, x2 * c + x1 * s], axis=-1)

def causal_attention(q, k, v):
    B, S, H, Dq = q.shape
    nb = S // Q_BLOCK
    qb = q.reshape(B, nb, Q_BLOCK, H, Dq).transpose(1, 0, 3, 2, 4)
    kt = k.transpose(0, 2, 1, 3)
    vt = v.transpose(0, 2, 1, 3)
    kpos = jnp.arange(S)
    scale = QK_HEAD ** -0.5

    def one_block(args):
        q_blk, blk = args
        s = jnp.einsum('bhqd,bhkd->bhqk', q_blk, kt,
                       preferred_element_type=jnp.float32) * scale
        qpos = blk * Q_BLOCK + jnp.arange(Q_BLOCK)
        s = jnp.where(kpos[None, :] <= qpos[:, None], s, -jnp.inf)
        p = jax.nn.softmax(s, axis=-1).astype(vt.dtype)
        return jnp.einsum('bhqk,bhkv->bhqv', p, vt)

    out = lax.map(one_block, (qb, jnp.arange(nb)))
    return out.transpose(1, 0, 3, 2, 4).reshape(B, S, H, V_HEAD)

def mla_mixer(h, cos, sin, w_in, q_norm, w_q_up, kv_norm, w_kv_up,
              q_head_norm, k_head_norm, w_out):
    B, S, _ = h.shape
    lat = h @ w_in
    cq, ckv, k_pe = jnp.split(lat, [Q_LORA, Q_LORA + KV_LORA], axis=-1)
    q = (rmsnorm_2(cq, q_norm) @ w_q_up).reshape(B, S, N_HEADS_2, QK_HEAD)
    kv = (rmsnorm_2(ckv, kv_norm) @ w_kv_up).reshape(B, S, N_HEADS_2, QK_NOPE + V_HEAD)
    k_nope, v = jnp.split(kv, [QK_NOPE], axis=-1)
    k = jnp.concatenate(
        [k_nope, jnp.broadcast_to(k_pe[:, :, None, :], (B, S, N_HEADS_2, QK_ROPE))], axis=-1)
    q = rope_tail(rmsnorm_2(q, q_head_norm), cos, sin)
    k = rope_tail(rmsnorm_2(k, k_head_norm), cos, sin)
    o = causal_attention(q, k, v)
    return o.reshape(B, S, N_HEADS_2 * V_HEAD) @ w_out

def second_inputs(seed: int = 0) -> dict:
    key = jax.random.key(seed)
    ks = jax.random.split(key, 24)
    f32 = jnp.float32

    def dense(k, shape, fan_in):
        return jax.random.normal(k, shape, f32) * fan_in ** -0.5

    def gain(k, shape):
        return 1.0 + 0.05 * jax.random.normal(k, shape, f32)

    x = jax.random.normal(ks[0], (BATCH, SEQ, D_MODEL), f32)
    offsets = jax.random.randint(ks[1], (BATCH, 1), 0, 4096, dtype=jnp.int32)
    positions = (jnp.arange(SEQ, dtype=jnp.int32)[None, :] + offsets).astype(jnp.int32)
    return {
        "x": x,
        "positions": positions,
        "ffn1_norm": gain(ks[2], (DEPTH_2, D_MODEL)),
        "ffn1_w_gate": dense(ks[3], (DEPTH_2, D_MODEL, D_FF), D_MODEL),
        "ffn1_w_up": dense(ks[4], (DEPTH_2, D_MODEL, D_FF), D_MODEL),
        "ffn1_w_down": dense(ks[5], (DEPTH_2, D_FF, D_MODEL), D_FF),
        "mix_norm": gain(ks[6], (DEPTH_2, D_MODEL)),
        "pool_w": dense(ks[7], (N_POOL_LAYERS, N_POOL_GROUPS, POOL_GROUP, POOL_GROUP), POOL_GROUP),
        "pool_scale": gain(ks[8], (N_POOL_LAYERS, D_MODEL)),
        "mla_w_in": dense(ks[9], (N_MLA_LAYERS, D_MODEL, Q_LORA + KV_LORA + QK_ROPE), D_MODEL),
        "mla_q_norm": gain(ks[10], (N_MLA_LAYERS, Q_LORA)),
        "mla_w_q_up": dense(ks[11], (N_MLA_LAYERS, Q_LORA, N_HEADS_2 * QK_HEAD), Q_LORA),
        "mla_kv_norm": gain(ks[12], (N_MLA_LAYERS, KV_LORA)),
        "mla_w_kv_up": dense(ks[13], (N_MLA_LAYERS, KV_LORA, N_HEADS_2 * (QK_NOPE + V_HEAD)), KV_LORA),
        "mla_q_head_norm": gain(ks[14], (N_MLA_LAYERS, QK_HEAD)),
        "mla_k_head_norm": gain(ks[15], (N_MLA_LAYERS, QK_HEAD)),
        "mla_w_out": dense(ks[16], (N_MLA_LAYERS, N_HEADS_2 * V_HEAD, D_MODEL), N_HEADS_2 * V_HEAD),
        "ffn2_norm": gain(ks[17], (DEPTH_2, D_MODEL)),
        "ffn2_w_gate": dense(ks[18], (DEPTH_2, D_MODEL, D_FF), D_MODEL),
        "ffn2_w_up": dense(ks[19], (DEPTH_2, D_MODEL, D_FF), D_MODEL),
        "ffn2_w_down": dense(ks[20], (DEPTH_2, D_FF, D_MODEL), D_FF),
    }

def second_block(x, positions, ffn1_norm, ffn1_w_gate, ffn1_w_up, ffn1_w_down, mix_norm,
              pool_w, pool_scale, mla_w_in, mla_q_norm, mla_w_q_up, mla_kv_norm,
              mla_w_kv_up, mla_q_head_norm, mla_k_head_norm, mla_w_out,
              ffn2_norm, ffn2_w_gate, ffn2_w_up, ffn2_w_down):
    inv_freq = 1.0 / (ROPE_THETA ** (jnp.arange(0, QK_ROPE, 2, dtype=jnp.float32) / QK_ROPE))
    ang = positions.astype(jnp.float32)[..., None] * inv_freq
    cos, sin = jnp.cos(ang), jnp.sin(ang)

    for i in range(DEPTH_2):
        h = rmsnorm_2(x, ffn1_norm[i])
        x = x + FFN_HALF * swiglu(h, ffn1_w_gate[i], ffn1_w_up[i], ffn1_w_down[i])
        h = rmsnorm_2(x, mix_norm[i])
        j = i // N_MIXERS
        if i % N_MIXERS == 0:
            x = x + pool_mixer(h, pool_w[j], pool_scale[j])
        else:
            x = x + mla_mixer(h, cos, sin, mla_w_in[j], mla_q_norm[j], mla_w_q_up[j],
                              mla_kv_norm[j], mla_w_kv_up[j], mla_q_head_norm[j],
                              mla_k_head_norm[j], mla_w_out[j])
        h = rmsnorm_2(x, ffn2_norm[i])
        x = x + FFN_HALF * swiglu(h, ffn2_w_gate[i], ffn2_w_up[i], ffn2_w_down[i])
    return x


def setup_inputs(seed=0):
    out = dict(first_inputs(seed))
    for name, value in second_inputs(seed + 1).items():
        if name != "x":
            out[name + "_2"] = value
    return out


def reference(
    x, c, ctx, c_ctx, w_ada, b_ada, g_mix, w_in, conv_w, sink, w_out, g_ffn, w_router, w_gate,
    w_up, w_down, g_final, positions_2, ffn1_norm_2, ffn1_w_gate_2, ffn1_w_up_2, ffn1_w_down_2,
    mix_norm_2, pool_w_2, pool_scale_2, mla_w_in_2, mla_q_norm_2, mla_w_q_up_2, mla_kv_norm_2,
    mla_w_kv_up_2, mla_q_head_norm_2, mla_k_head_norm_2, mla_w_out_2, ffn2_norm_2,
    ffn2_w_gate_2, ffn2_w_up_2, ffn2_w_down_2,
):
    x = first_block(
        x, c, ctx, c_ctx, w_ada, b_ada, g_mix, w_in, conv_w, sink, w_out, g_ffn, w_router,
        w_gate, w_up, w_down, g_final,
    )
    return second_block(
        x, positions_2, ffn1_norm_2, ffn1_w_gate_2, ffn1_w_up_2, ffn1_w_down_2, mix_norm_2,
        pool_w_2, pool_scale_2, mla_w_in_2, mla_q_norm_2, mla_w_q_up_2, mla_kv_norm_2,
        mla_w_kv_up_2, mla_q_head_norm_2, mla_k_head_norm_2, mla_w_out_2, ffn2_norm_2,
        ffn2_w_gate_2, ffn2_w_up_2, ffn2_w_down_2,
    )


_drawn_inputs = setup_inputs


def setup_inputs(seed=0):
    import zlib

    import numpy as np

    out = dict(_drawn_inputs(seed))
    spreads = {}
    factors = {'ctx': 3.254,
     'b_ada': 4.1,
     'sink': 8.0,
     'g_ffn': 2.806,
     'mla_q_norm_2': 8.0,
     'mla_kv_norm_2': 7.184,
     'mla_q_head_norm_2': 8.0,
     'mla_k_head_norm_2': 8.0}
    for name, (base, spread) in spreads.items():
        noise = np.random.default_rng([zlib.crc32(name.encode()), seed]).standard_normal(out[name].shape)
        drawn = base * np.exp(spread * noise) if base else spread * noise
        out[name] = __import__('jax').numpy.asarray(drawn.astype(out[name].dtype))
    for name, factor in factors.items():
        out[name] = (out[name] * factor).astype(out[name].dtype)
    return out
```

```python
from contextlib import ExitStack

import numpy as np

import concourse.bass as bass
from concourse import mybir

F32 = mybir.dt.float32
F32R = mybir.dt.float32r
I32 = mybir.dt.int32
ALU = mybir.AluOpType
ACT = mybir.ActivationFunctionType
AX_X = mybir.AxisListType.X

P = 128
T = 512
C = 256
D = 1024
KD = D // P
H, HD = 8, 64
NB = T // P
E, SLOTS = 16, 64
PAIRS = E // 2
F2 = 2816
KF = F2 // P
HALF_KF = KF // 2
MH, NOPE, ROPE = 8, 128, 64
KQ, KKV = 6, 2
EPS = 1e-6
MASKED = -1e30
STAGE = 4
WIDE = HALF_KF * P
RING = 16

_names = [("c", KD), ("cctx", KD), ("b_ada", 48), ("g_mix", KD), ("g_ffn", KD), ("conv_w", 12), ("sink", H),
          ("ffn1a", KD), ("ffn2a", KD), ("ffn1b", KD), ("ffn2b", KD), ("mixa", KD), ("mixb", KD),
          ("pool_scale", KD), ("q_norm", KQ), ("kv_norm", KKV), ("qh_nope", 1), ("qh_rope", 1),
          ("kh_nope", 1), ("kh_rope", 1), ("g_final", KD)]
COL, NCOLS = {}, 0
for _n, _k in _names:
    COL[_n] = (NCOLS, _k)
    NCOLS += _k

_tables = [("ident", P), ("turn", P), ("lower", H), ("one_row", 15), ("two_rows", 14), ("slot", SLOTS), ("inv_freq", 1), ("rcount", 15)]
TAB, NTAB = {}, 0
for _n, _k in _tables:
    TAB[_n] = (NTAB, _k)
    NTAB += _k


def shape_tables():
    t = np.zeros((P, NTAB), np.float32)

    def put(name, v):
        t[:, TAB[name][0]:TAB[name][0] + TAB[name][1]] = v

    put("ident", np.eye(P))
    turn = np.zeros((P, P), np.float32)
    for g in range(0, P, 64):
        for d in range(32):
            turn[g + 32 + d, g + d] = -1.0
            turn[g + d, g + 32 + d] = 1.0
    put("turn", turn)
    put("lower", np.repeat((np.arange(P) < 64)[:, None], H, 1))
    one, two = np.zeros((P, 15), np.float32), np.zeros((P, 14), np.float32)
    one[:, 7] = 1
    two[:64, 6], two[64:, 7] = 1, 1
    put("one_row", one)
    put("two_rows", two)
    put("slot", np.arange(1, SLOTS + 1))
    inv = (np.float32(1) / np.power(np.float32(10000), np.arange(0, 64, 2, dtype=np.float32) / np.float32(64))).astype(np.float32)
    bits = inv.view(np.int32).copy()
    bits[[5, 27]] -= 2
    put("inv_freq", np.tile(bits.view(np.float32), 4)[:, None])
    put("rcount", 1.0 / np.arange(1, 16, dtype=np.float32))
    i, j = np.arange(P)[:, None], np.arange(P)[None, :]
    zero = np.zeros((P, P), np.float32)
    window = np.concatenate([np.where(j >= i, 0, MASKED), zero, np.where(j <= i, 0, MASKED)], 1).astype(np.float32)
    causal = np.concatenate([zero, zero, zero, np.where(j <= i, 0, MASKED)], 1).astype(np.float32)
    inv16 = (np.float32(10000.0) ** (-np.arange(16, dtype=np.float32) / np.float32(16))).astype(np.float32)
    tok = np.arange(T)
    ang = np.concatenate([(tok // 64).astype(np.float32)[:, None] * inv16, (tok % 64).astype(np.float32)[:, None] * inv16], -1)
    rope = np.concatenate([np.tile(np.cos(ang).T, (4, 1)), np.tile(np.sin(ang).T, (4, 1))], 1).astype(np.float32)
    select = np.zeros((MH, MH + MH // 2, P), np.float32)
    for h in range(MH):
        select[h, h] = 1
        select[h, MH + h // 2, 64 * (h % 2):64 * (h % 2) + 64] = 1
    return t, window, causal, rope, select.reshape(MH, -1)


def build(nc, A, out):
    st = ExitStack()
    with st:
        sem_names = []

        def sem(name):
            sem_names.append(name)
            return st.enter_context(nc.semaphore(name))

        base = 16512

        def place(name, shape, dt, at):
            return nc.alloc_sbuf_tensor_at(name, shape, dt, offset=base + at)

        def up(n):
            return (n + 31) // 32 * 32

        KB = 1024
        TILE = T * 4
        X0, HH, HL, G = 0, 16 * KB, 32 * KB, 48 * KB
        ST = G + KF * 2 * TILE
        WH = ST + STAGE * WIDE * 4
        WL = WH + 2 * WIDE * 4
        TM = WL + 2 * WIDE * 4
        CO = TM + 11 * TILE
        x = place("x", [P, KD, T], F32, X0)
        hH = place("hH", [P, KD, T], F32R, HH)
        hL = place("hL", [P, KD, T], F32R, HL)
        stage = place("stage", [P, STAGE, WIDE], F32, ST)
        wH = place("wH", [P, 2, WIDE], F32R, WH)
        wL = place("wL", [P, 2, WIDE], F32R, WL)
        std = place("std", [P, T], F32, TM)
        rstd = place("rstd", [P, T], F32, TM + TILE)
        ssq = place("ssq", [P, T], F32, TM + 2 * TILE)
        sq = place("sq", [P, 2, T], F32, TM + 3 * TILE)
        hraw = place("hraw", [P, 2, T], F32, TM + 5 * TILE)
        sg = place("sg", [P, 2, T], F32, TM + 7 * TILE)
        gf = place("gf", [P, 2, T], F32, TM + 9 * TILE)
        cols = place("cols", [P, NCOLS], F32, CO)
        tabs = place("tabs", [P, NTAB], F32, CO + up(NCOLS * 4))
        c2 = CO + up(NCOLS * 4) + up(NTAB * 4)
        ones = place("ones", [P, P], F32, c2)
        eps = place("eps", [P, 1], F32, c2 + 512)
        mod = place("mod", [P, 64], F32, c2 + 544)
        gain1 = place("gain1", [P, 3 * KD], F32, c2 + 544 + 256)
        stat = place("stat", [P, 64], F32, c2 + 544 + 256 + 96)
        assert base + c2 + 544 + 256 + 96 + 256 <= 229368, base + c2 + 1152

        ctx = place("ctx", [P, KD, C], F32, G)
        cH = place("cH", [P, KD, C], F32R, G + 8 * KB)
        cL = place("cL", [P, KD, C], F32R, G + 16 * KB)
        PT = place("PT", [P, 2, 5, T], F32, G)
        adaw = place("adaw", [P, 4, 1024], F32, G + 24 * KB)
        prob = place("prob", [P, 4, 648], F32, G + 24 * KB)
        acc = place("acc", [P, 2, 1024], F32, G + 40 * KB)
        accc = place("accc", [P, 2, 1024], F32, G + 48 * KB)
        qT = place("qT", [P, 4, T], F32, G + 56 * KB)
        kT = place("kT", [P, T + C], F32, G + 64 * KB)
        vT = place("vT", [P, T + C], F32, G + 67 * KB)
        V = place("V", [P, 6, P], F32, G + 70 * KB)
        conv = place("conv", [P, 4, T], F32, G + 73 * KB)
        rope = place("rope", [P, 2, T], F32, G + 81 * KB)
        window = place("window", [P, 3 * P], F32, G + 85 * KB)
        catH, catL = hH, hL
        ring = place("ring", [P, RING, 1024], F32, G)
        h2 = place("h2", [P, KD, T], F32, HH)
        h2t = place("h2t", [P, NB, D], F32, HL)
        pos = place("pos", [E, T], F32, G + 64 * KB)
        afT = place("afT", [E, T], F32, G + 66 * KB)
        work = place("work", [E, 2, T], F32, G + 68 * KB)
        xs = place("xs", [P, D], F32, G + 64 * KB)
        xsT = place("xsT", [P, KD, P], F32, G + 68 * KB)
        sil = place("sil", [P, 1024], F32, G + 72 * KB)
        hid = place("hid", [P, 1024], F32, G + 76 * KB)
        hidT = place("hidT", [P, 8, P], F32, G + 80 * KB)
        pick = place("pick", [P, NB, P], F32, G + 84 * KB)
        pickg = place("pickg", [P, NB, P], F32, G + 86 * KB)
        pickgT = place("pickgT", [P, T], F32, TM + 3 * TILE)
        af = place("af", [P, NB, E], F32, TM + 4 * TILE)
        posT = place("posT", [P, NB, E], F32, TM + 4 * TILE + 256)
        top = place("top", [E, 8, 8], F32, TM + 4 * TILE + 512)
        wr = place("wr", [P, KD, E], F32, TM + 7 * TILE)
        gH = place("gH", [P, KF, T], F32R, G)
        gL = place("gL", [P, KF, T], F32R, G + KF * TILE)
        s1 = place("s1", [P, 2, T], F32, G)
        s2 = place("s2", [P, 2, T], F32, G + 2 * TILE)
        hp = place("hp", [P, KD, T], F32, G + 4 * TILE)
        lat = place("lat", [P, 9, T], F32, G)
        kr = place("kr", [P, MH, T], F32, G)
        nH = place("nH", [P, KD, T], F32R, G + 18 * KB)
        nL = place("nL", [P, KD, T], F32R, G + 34 * KB)
        oH, oL = nH, nL
        qn = place("qn", [P, MH, T], F32, G + 50 * KB)
        qr = place("qr", [P, 4, T], F32, G + 66 * KB)
        pT2 = [place("pT2a", [P, NB, T], F32, G + 74 * KB), place("pT2b", [P, NB, T], F32, TM)]
        select = place("select", [MH, MH + MH // 2, P], F32, TM + 7 * TILE)
        rstd_q = place("rstd_q", [P, T], F32, TM + 10 * TILE)
        head_std = place("head_std", [MH, T], F32, TM)
        head_rstd = [place("head_rstd_q", [MH, T], F32, TM + TILE), place("head_rstd_k", [MH, T], F32, TM + 2 * TILE)]
        rope_tmp = place("rope_tmp", [P, T], F32, G + 78 * KB)
        rope2 = place("rope2", [P, 2, T], F32, G + 82 * KB)
        krope = place("krope", [P, T], F32, G + 86 * KB)
        kn = place("kn", [P, MH, T], F32, HH)
        V2 = place("V2", [P, NB, D], F32, HL)
        prob2 = place("prob2", [P, 4, T], F32, TM + 7 * TILE)
        cmask = place("cmask", [P, T], F32, TM + 6 * TILE)
        posi = place("posi", [P, T], I32, G + 74 * KB)
        posf = place("posf", [P, T], F32, G + 76 * KB)
        ang = place("ang", [P, T], F32, G + 78 * KB)
        turns = place("turns", [P, T], F32, G + 80 * KB)

        pb = [st.enter_context(nc.psum_tensor(f"pb{i}", [P, 512], F32)) for i in range(8)]

        def col(name, k=0):
            return cols[:, COL[name][0] + k:COL[name][0] + k + 1]

        def tab(name, n=None):
            a, k = TAB[name]
            return tabs[:, a:a + (n or k)]


        small_loaded, x_loaded, ctx_loaded = sem("small_loaded"), sem("x_loaded"), sem("ctx_loaded")
        ones_set = sem("ones_set")
        ada_landed = [sem(f"ada_landed{i}") for i in range(4)]
        cond_ready, adac_added, ada_added = sem("cond_ready"), sem("adac_added"), sem("ada_added")
        mod_summed, mod_ready, gain_ready = sem("mod_summed"), sem("mod_ready"), sem("gain_ready")
        strip_landed = [sem(f"strip_landed{i}") for i in range(STAGE)]
        strip_hi, strip_lo, strip_used = sem("strip_hi"), sem("strip_lo"), sem("strip_used")
        out_taken = sem("out_taken")
        sq_done, ssq_done, norm_summed = sem("sq_done"), sem("ssq_done"), sem("norm_summed")
        std_done, rstd_done = sem("std_done"), sem("rstd_done")
        h_raw, h_hi, h_lo = sem("h_raw"), sem("h_hi"), sem("h_lo")
        gate_ready, g_raw = sem("gate_ready"), sem("g_raw")
        silu_done, g_hi, g_lo = sem("silu_done"), sem("g_hi"), sem("g_lo")
        turned, rope_part, rope_done = sem("turned"), sem("rope_part"), sem("rope_done")
        v_turned, v_ready, conv_part = sem("v_turned"), sem("v_ready"), sem("conv_part")
        cat_hi, cat_lo = sem("cat_hi"), sem("cat_lo")
        scored, row_max, masked, bias_ready = sem("scored"), sem("row_max"), sem("masked"), sem("bias_ready")
        ctx_copied, exp_done, inv_ready, p_ready = sem("ctx_copied"), sem("exp_done"), sem("inv_ready"), sem("p_ready")
        p_turned, pt_act, pt_dve, pv_done = sem("p_turned"), sem("pt_act"), sem("pt_dve"), sem("pv_done")
        att_hi, att_lo = sem("att_hi"), sem("att_lo")
        wr_loaded, logits_done, lmax, aff_exp, aff_ready = sem("wr_loaded"), sem("logits_done"), sem("lmax"), sem("aff_exp"), sem("aff_ready")
        aff_turned, top_step, pos_turned, posT_ready = sem("aff_turned"), sem("top_step"), sem("pos_turned"), sem("posT_ready")
        h2_turned, h2t_ready = sem("h2_turned"), sem("h2t_ready")
        exp_landed = [sem(f"exp_landed{i}") for i in range(RING // 2)]
        exp_used = sem("exp_used")
        pick_ready, pickg_ready, pg_turned, pgT_ready = sem("pick_ready"), sem("pickg_ready"), sem("pg_turned"), sem("pgT_ready")
        gathered, xs_act, xs_dve, xs_turned = sem("gathered"), sem("xs_act"), sem("xs_dve"), sem("xs_turned")
        xsT_act, xsT_dve, sil_done, hid_done = sem("xsT_act"), sem("xsT_dve"), sem("sil_done"), sem("hid_done")
        hid_turned, hidT_act, hidT_dve = sem("hid_turned"), sem("hidT_act"), sem("hidT_dve")
        y_act, y_dve, scattered, x_added = sem("y_act"), sem("y_dve"), sem("scattered"), sem("x_added")
        pool_step, pool_hi, pool_lo = sem("pool_step"), sem("pool_hi"), sem("pool_lo")
        pos_loaded, mask_loaded, angle, sines = sem("pos_loaded"), sem("mask_loaded"), sem("angle"), sem("sines")
        hq_sq, hq_summed, hq_std, hq_rstd, hq_out = sem("hq_sq"), sem("hq_summed"), sem("hq_std"), sem("hq_rstd"), sem("hq_out")
        kr_cleared, gained, select_loaded, spread = sem("kr_cleared"), sem("gained"), sem("select_loaded"), sem("spread")
        out_stored = sem("out_stored")

        W_IN, W_OUT, FFN1A = 0, 18, 26
        NFFN = 2 * KF + 2 * KD
        POOL = FFN1A + NFFN
        FFN2A = POOL + 4
        FFN1B = FFN2A + NFFN
        M_IN = FFN1B + NFFN
        M_Q = M_IN + 9
        M_K = M_Q + 12
        M_V = M_K + 2
        M_OUT = M_V + 2
        FFN2B = M_OUT + KD
        N_STRIPS = FFN2B + NFFN
        width = [KD * P] * FFN1A
        ffn_width = [KD * P] * (2 * KF) + [WIDE] * (2 * KD)
        width += ffn_width + [4 * P] * 4 + ffn_width + ffn_width
        width += [KD * P] * 9 + [KQ * P] * 12 + [KD * P] * 4 + [KD * P] * KD + ffn_width
        assert len(width) == N_STRIPS
        T_IN, T_OUT, T_FFN1A = 0, 18, 26
        T_POOL = T_FFN1A + KF + KD
        T_FFN2A = T_POOL + KD
        T_FFN1B = T_FFN2A + KF + KD
        T_MIN = T_FFN1B + KF + KD
        T_MQ = T_MIN + 9
        T_MK = T_MQ + 12
        T_MV = T_MK + 8
        T_MOUT = T_MV + 8
        T_FFN2B = T_MOUT + KD
        NCTX, NX, NH2, NFIN, N1A, NMA, N2A, N1B, NMB, NQL, NKL, N2B = range(12)
        KT = [KD] * 9 + [KQ, KKV, KD]
        WID = [C] + [T] * 11
        SQ0 = [sum(KT[:q]) for q in range(12)]
        SS0 = [sum(KT[:q]) + q for q in range(12)]
        IS_SPLIT = [q not in (NH2, NFIN, NMA) for q in range(12)]
        FOLDED = [q in (N1A, N2A, N1B, NMB, NQL, N2B) for q in range(12)]
        RAW0 = [sum(k for r, k in enumerate(KT[:q]) if not FOLDED[r]) for q in range(12)]
        HI0 = [sum(k for r, k in enumerate(KT[:q]) if r not in (NFIN, NMA)) for q in range(12)]
        LO0 = [sum(k for r, k in enumerate(KT[:q]) if IS_SPLIT[r]) for q in range(12)]
        SCALE1 = float(HD) ** -0.5
        SCALE2 = float(NOPE + ROPE) ** -0.5
        UNITS = [(n, a, j) for n in range(NB) for a in range(4) for j in range(2)]

        def keys(n):
            return max(0, n - 1) * P, min(NB, n + 2) * P

        def block_at(u):
            return u // 8 if 0 <= u < len(UNITS) and u % 8 == 7 else None

        GAIN = {N1A: "ffn1a", N2A: "ffn2a", N1B: "ffn1b", NMB: "mixb", N2B: "ffn2b"}

        OUTS = [n if n <= 12 else 12 + 2 * (n - 12) for n in range(21)]

        def head_at(u):
            return u // NB if 0 <= u < MH * NB and u % NB == NB - 1 else None

        def count(it, before, per, n):
            return before * per + n if it is None else it * per + (before * per + n)

        def bank(tile):
            return 2 * (tile % 2)

        def shifted(n, it, by=4):
            return n if it is None else it * by + n

        S2 = (0, 1, 6, 7)
        LAG = 3
        POOL_STEPS = []
        for _g in range(4):
            POOL_STEPS.append((POOL_STEPS[-1] if _g else 0) + 2 * (_g + 1) + 1 + 4)
        ROT_AT = {1: 0, 3: 1, 4: 2, 5: 3, 6: 4}

        def b_units(u):
            return min(max(u - 8, 0), 16)

        rstd_of = [sg[:, 0, :]] + [rstd[:, :]] * 11
        rstd_of[NQL] = rstd_q[:, :]
        kv_tiles = {n: [4, 5] + list(range(keys(n)[0] // P, keys(n)[1] // P)) for n in range(NB)}
        ffns = [(FFN1A, T_FFN1A, 0, N1A), (FFN2A, T_FFN2A, 1, N2A), (FFN1B, T_FFN1B, 2, N1B), (FFN2B, T_FFN2B, 3, N2B)]

        block = st.enter_context(nc.Block())

        @block.sync
        def _(sp):
            sp.dma_start(cols[:, :], A["cols"]).then_inc(small_loaded, 16)
            sp.dma_start(tabs[:, :], A["tabs"]).then_inc(small_loaded, 16)
            sp.dma_start(ctx[:, :, :], A["ctx"].rearrange("p (k t) -> p k t", k=KD)).then_inc(ctx_loaded, 16)
            sp.dma_start(x[:, :, :], A["x"].rearrange("p (k t) -> p k t", k=KD)).then_inc(x_loaded, 16)
            sp.dma_start(rope[:, :, :], A["rope"].rearrange("p (k t) -> p k t", k=2)).then_inc(small_loaded, 16)
            sp.dma_start(window[:, :], A["window"]).then_inc(small_loaded, 16)

            def ada(a):
                if a >= 4:
                    sp.wait_ge(ada_added, a - 3)
                sp.dma_start(adaw[:, a % 4, :], A["w_ada"][(a % 8) * P:(a % 8) * P + P, (a // 8) * 1024:(a // 8) * 1024 + 1024])\
                  .then_inc(ada_landed[a % 4], 16)

            def strip(n, src, it=None):
                if n >= STAGE:
                    sp.wait_ge(strip_lo, shifted(n - STAGE + 1, it))
                sp.dma_start(stage[:, n % STAGE, 0:width[n]], src).then_inc(strip_landed[n % STAGE], 16)

            def ffn_tiles(n0, f, it):
                for j in range(2):
                    g = j if it is None else it * 2 + j
                    strip(n0 + 2 * j, A["gate"][f][g], it)
                    strip(n0 + 2 * j + 1, A["up"][f][g], it)

            def ffn(n0, f, start=0):
                down = A["down"][f]
                with sp.Fori(start, KF // 2) as i:
                    ffn_tiles(n0, f, i)
                d0 = n0 + 2 * KF
                with sp.Fori(0, KD // 2) as i:
                    for j in range(4):
                        strip(d0 + j, down[i * 4 + j], i)

            for a in range(16):
                ada(a)
            for n in range(18):
                strip(W_IN + n, A["w_in"][n])
                if n < 16:
                    ada(16 + 2 * n)
                    ada(17 + 2 * n)
            for n in range(8):
                strip(W_OUT + n, A["w_out"][n])
                if n == 3:
                    sp.wait_ge(rope_done, 5)
                    sp.wait_ge(cat_lo, 4)
                    sp.dma_start(wr[:, :, :], A["w_router"].rearrange("p (k e) -> p k e", k=KD)).then_inc(wr_loaded, 16)

            def experts(d, it):
                w = 2 * (d % 8)
                sp.dma_start(ring[:, w:w + 2, :], A["experts"][it, d].rearrange("p (e f) -> p e f", e=2)).then_inc(exp_landed[d % 8], 16)

            sp.wait_ge(pv_done, NB)
            sp.wait_ge(pt_act, 32)
            sp.wait_ge(att_lo, NB)
            sp.wait_ge(cat_lo, 4)
            for d in range(8):
                experts(d, 0)
            ffn_tiles(FFN1A, 0, None)
            with sp.Fori(0, PAIRS - 1) as i:
                for d in range(24):
                    sp.wait_ge(exp_used, i * 24 + (d + 1))
                    experts((d + 8) % 24, i + (d + 8) // 24)
            for d in range(16):
                sp.wait_ge(exp_used, (PAIRS - 1) * 24 + d + 1)
                experts(d + 8, PAIRS - 1)

            ffn(FFN1A, 0, start=1)
            for n in range(4):
                strip(POOL + n, A["pool_w"][n])
            ffn(FFN2A, 1)
            ffn(FFN1B, 2)
            for n in range(9):
                strip(M_IN + n, A["mla_in"][n])
            sp.wait_ge(strip_used, M_IN)
            sp.dma_start(posi[:, :], A["positions"]).then_inc(pos_loaded, 16)
            sp.dma_start(select[:, :, :], A["select"].rearrange("h (k p) -> h k p", p=P)).then_inc(select_loaded, 16)
            for n in range(12):
                strip(M_Q + n, A["q_up"][n])
            for n in range(4):
                strip(M_K + n, A["kv_up"][n])
            sp.wait_ge(h_lo, LO0[N2B])
            sp.dma_start(cmask[:, :], A["causal"]).then_inc(mask_loaded, 16)
            for n in range(8):
                strip(M_OUT + n, A["mla_out"][n])
            ffn(FFN2B, 3)
            sp.wait_ge(out_taken, T_FFN2B + KF + KD)
            sp.dma_start(out, x[:, :, :].rearrange("p k t -> p (k t)")).then_inc(out_stored, 16)
            sp.wait_ge(out_stored, 16)

        @block.gpsimd
        def _(pool):
            pool.memset(ones[:, :], 1.0).then_inc(ones_set, 1)
            pool.memset(eps[:, :], EPS).then_inc(ones_set, 1)
            pool.wait_ge(h_lo, LO0[N2B])
            pool.wait_ge(sq_done, SQ0[N2B])
            pool.memset(kr[:, :, :], 0.0).then_inc(kr_cleared, 1)

        @block.scalar
        def _(act):
            def hi(n, it=None):
                if n >= N_STRIPS:
                    return
                landed = 16 * (n // STAGE + 1)
                act.wait_ge(strip_landed[n % STAGE], shifted(landed, it, 16))
                if n >= 2:
                    act.wait_ge(strip_used, shifted(n - 1, it))
                act.activation(wH[:, n % 2, 0:width[n]], stage[:, n % STAGE, 0:width[n]], ACT.Copy).then_inc(strip_hi, 1)

            def square(q, k, src, seen=None):
                if SS0[q] + k >= 2:
                    act.wait_ge(ssq_done, SS0[q] + (k if k >= 2 else 0))
                act.activation(sq[:, (SQ0[q] + k) % 2, 0:WID[q]], src, ACT.Square).then_inc(sq_done, 1)

            def root(q, features):
                act.wait_ge(norm_summed, q + 1)
                act.wait_ge(ones_set, 2)
                if q:
                    act.wait_ge(rstd_done, q)
                act.activation(std[:, 0:WID[q]], pb[6][:, 0:WID[q]], ACT.Sqrt, bias=eps[:, 0:1], scale=1.0 / features)\
                   .then_inc(std_done, 1)

            def norm_hi(q, dst, shift=None):
                for k in range(KT[q]):
                    act.wait_ge(h_raw, RAW0[q] + k + 1)
                    src = hraw[:, (RAW0[q] + k) % 2, 0:WID[q]]
                    if shift is None:
                        ins = act.activation(dst[:, k, :], src, ACT.Copy)
                    else:
                        ins = act.activation(dst[:, k, :], src, ACT.Identity, bias=mod[:, shift + k:shift + k + 1])
                    ins.then_inc(h_hi, 1)

            def prepare(q, k, src, gain, it=None):
                g = k if it is None else it * 2 + k
                act.wait_ge(ssq_done, shifted(SS0[q] + k, it, 2) if k or it is not None else SS0[q])
                act.activation(sq[:, (SQ0[q] + k) % 2, :], src[:, g, :], ACT.Square).then_inc(sq_done, 1)
                a = COL[gain][0]
                scale = cols[:, a + k:a + k + 1] if it is None else cols[:, bass.ds(it * 2 + (a + k), 1)]
                dst = (nH if q == NQL else hH)[:, g, :]
                act.activation(dst, src[:, g, :], ACT.Copy, scale=scale).then_inc(h_hi, 1)

            def ffn(n0, t0, f, q):
                def inner(tile, it):
                    act.wait_ge(gate_ready, shifted(f * KF + tile + 1, it, 2))
                    act.activation(sg[:, tile % 2, :], hraw[:, tile % 2, :], ACT.Silu).then_inc(silu_done, 1)
                    act.wait_ge(g_raw, shifted(f * KF + tile + 1, it, 2))
                    dst = gH[:, tile, :] if it is None else gH[:, it * 2 + tile, :]
                    act.activation(dst, gf[:, tile % 2, :], ACT.Copy).then_inc(g_hi, 1)

                def tiles(e, it):
                    hi(n0 + e + 2, it)
                    hi(n0 + e + 3, it)
                    inner(e // 2, it)
                    hi(n0 + e + 4, it)
                    hi(n0 + e + 5, it)
                    inner(e // 2 + 1, it)

                root(q, D)
                with act.Fori(0, KF // 2 - 1) as i:
                    tiles(0, i)
                tiles(2 * KF - 4, None)
                d0, q1 = n0 + 2 * KF, q + 1

                def added(m, it):
                    act.wait_ge(out_taken, shifted(t0 + KF + m + 1, it, 2))
                    if FOLDED[q1]:
                        prepare(q1, m, x, GAIN[q1], it)
                    else:
                        act.wait_ge(ssq_done, shifted(SS0[q1] + m, it, 2) if m or it is not None else SS0[q1])
                        src = x[:, m, :] if it is None else x[:, it * 2 + m, :]
                        act.activation(sq[:, (SQ0[q1] + m) % 2, :], src, ACT.Square).then_inc(sq_done, 1)

                def down(e, it):
                    hi(d0 + e + 2, it)
                    hi(d0 + e + 3, it)
                    if q1 < 12:
                        added(e // 2, it)
                    hi(d0 + e + 4, it)
                    hi(d0 + e + 5, it)
                    if q1 < 12:
                        added(e // 2 + 1, it)

                with act.Fori(0, KD // 2 - 1) as i:
                    down(0, i)
                down(2 * KD - 4, None)

            act.wait_ge(small_loaded, 64)
            act.activation(stat[:, 0:16], cols[:, 0:16], ACT.Silu).then_inc(cond_ready, 1)
            act.wait_ge(ctx_loaded, 16)
            for k in range(KD):
                square(NCTX, k, ctx[:, k, :])
            act.wait_ge(x_loaded, 16)
            for k in range(KD):
                square(NX, k, x[:, k, :])
            root(NCTX, D)
            root(NX, D)
            hi(0)
            hi(1)
            act.wait_ge(mod_ready, 2)
            norm_hi(NCTX, cH, shift=48)
            norm_hi(NX, hH, shift=0)
            for s in range(18):
                hi(s + 2)
            act.wait_ge(strip_used, 18)
            for k in range(4):
                act.wait_ge(out_taken, 9 + 3 * k)
                act.activation(catH[:, 4 + k, :], conv[:, k, :], ACT.Copy).then_inc(cat_hi, 1)

            def att_context(u):
                if u >= 4:
                    act.wait_ge(p_turned, u - 3)
                act.wait_ge(scored, u + 1)
                act.activation(prob[:, u % 4, 0:C], pb[2 * (u % 2) + 1][:, 0:C], ACT.Copy).then_inc(ctx_copied, 1)

            def att_exp(u):
                lo_, hi_ = keys(UNITS[u][0])
                act.wait_ge(ctx_copied, u + 1)
                act.wait_ge(bias_ready, u + 1)
                p = prob[:, u % 4, 0:C + hi_ - lo_ + 1]
                act.activation(p, p, ACT.Exp, bias=stat[:, 16 + u % 4:17 + u % 4], scale=SCALE1,
                               accum_out=stat[:, 20 + u % 4:21 + u % 4]).then_inc(exp_done, 1)

            def att_turned(u):
                n, a, j = UNITS[u]
                act.wait_ge(p_turned, u + 1)
                if n and a == j == 0:
                    act.wait_ge(pv_done, n)
                act.activation(PT[:, j, 0:4, a * P:(a + 1) * P],
                               pb[4 + 2 * (u % 2)][:, :].rearrange("p (k q) -> p k q", k=4), ACT.Copy).then_inc(pt_act, 1)

            def att_out(n):
                act.wait_ge(pv_done, n + 1)
                act.activation(catH[:, 0:4, n * P:(n + 1) * P], pb[7][:, :].rearrange("p (k q) -> p k q", k=4), ACT.Copy)\
                   .then_inc(att_hi, 1)

            for u in range(len(UNITS) + LAG + 2):
                if u < len(UNITS):
                    att_context(u)
                if 1 <= u <= len(UNITS):
                    att_exp(u - 1)
                if 0 <= u - LAG < len(UNITS):
                    att_turned(u - LAG)
                if block_at(u - LAG - 2) is not None:
                    att_out(block_at(u - LAG - 2))

            def residual_squares(n0, t0, q, gain=None):
                for s in range(KD):
                    hi(n0 + s + 2)
                    act.wait_ge(out_taken, t0 + s + 1)
                    if gain:
                        prepare(q, s, x, gain)
                    else:
                        square(q, s, x[:, s, :])

            residual_squares(W_OUT, T_OUT, NH2)

            root(NH2, D)
            act.wait_ge(mod_ready, 6)
            norm_hi(NH2, h2, shift=24)
            for k in range(KD):
                for_half = k % 2
                act.wait_ge(h2_turned, k + 1)
                tt = k // 2
                act.activation(h2t[:, tt, for_half * 512:(for_half + 1) * 512], pb[for_half][:, :], ACT.Copy).then_inc(h2t_ready, 1)
                if k == 1:
                    act.wait_ge(lmax, 2)
                    for i in range(NB):
                        act.activation(af[:, i, :], pb[4][:, i * E:(i + 1) * E], ACT.Exp, bias=stat[:, 4 + i:5 + i], scale=1.0,
                                       accum_out=stat[:, 8 + i:9 + i]).then_inc(aff_exp, 1)

            def tokens_out(it, p):
                act.wait_ge(gathered, count(it, p, 2, 1))
                act.activation(xs[:, 0:512], pb[6][:, :], ACT.Copy).then_inc(xs_act, 1)

            def tokens_turned(it, p):
                act.wait_ge(xs_turned, count(it, p, 2, 1))
                act.activation(xsT[:, 0:4, :], pb[2][:, :].rearrange("p (k s) -> p k s", k=4), ACT.Copy).then_inc(xsT_act, 1)

            def silu(it, p):
                act.wait_ge(exp_used, count(it, p, 24, 16))
                for half in range(2):
                    act.activation(sil[:, half * 512:(half + 1) * 512], pb[half][:, :], ACT.Silu).then_inc(sil_done, 1)

            def hidden_turned(it, p):
                act.wait_ge(hid_turned, count(it, p, 2, 1))
                act.activation(hidT[:, 0:4, :], pb[0][:, :].rearrange("p (k s) -> p k s", k=4), ACT.Copy).then_inc(hidT_act, 1)

            def expert_out(it, p):
                act.wait_ge(exp_used, count(it, p, 24, 24))
                act.activation(xs[:, 0:512], pb[4][:, :], ACT.Copy).then_inc(y_act, 1)
                act.wait_ge(pg_turned, count(it, p, 1, 1))
                act.activation(pickgT[:, :], pb[6][:, :], ACT.Copy).then_inc(pgT_ready, 1)

            tokens_out(None, 0)
            tokens_turned(None, 0)
            with act.Fori(0, PAIRS - 1) as i:
                silu(i, 0)
                tokens_out(i, 1)
                hidden_turned(i, 0)
                tokens_turned(i, 1)
                expert_out(i, 0)
            silu(None, PAIRS - 1)
            hidden_turned(None, PAIRS - 1)
            expert_out(None, PAIRS - 1)

            for k in range(KD):
                act.wait_ge(x_added, 64)
                square(NFIN, k, x[:, k, :])
            root(NFIN, D)
            for k in range(KD):
                act.wait_ge(h_raw, RAW0[NFIN] + k + 1)
                prepare(N1A, k, x, "ffn1a")
            ffn(*ffns[0])

            root(NMA, D)
            for g in range(4):
                act.wait_ge(pool_step, POOL_STEPS[g])
                act.activation(hH[:, 2 * g:2 * g + 2, :], gf[:, :, :], ACT.Copy).then_inc(pool_hi, 1)
                hi(POOL + g + 2)
                for m in (2 * g, 2 * g + 1):
                    act.wait_ge(out_taken, T_POOL + m + 1)
                    square(N2A, m, x[:, m, :])
            act.wait_ge(strip_used, POOL + 4)
            for m in range(KD):
                act.activation(hH[:, m, :], x[:, m, :], ACT.Copy, scale=col("ffn2a", m)).then_inc(h_hi, 1)
            ffn(*ffns[1])
            ffn(*ffns[2])

            for s in range(9):
                hi(M_IN + s + 2)
                if s == 0:
                    root(NMB, D)
                if s == KQ + 1:
                    root(NQL, KQ * P)
                act.wait_ge(out_taken, T_MIN + s + 1)
                if s < KQ:
                    prepare(NQL, s, lat, "q_norm")
                elif s < KQ + KKV:
                    square(NKL, s - KQ, lat[:, s, :])
            for k in range(2):
                act.wait_ge(angle, 8 + 2 * k)
                act.activation(rope2[:, 1 - k, :], (ang if k == 0 else turns)[:, :], ACT.Sin).then_inc(sines, 1)

            def head_square(n, src):
                if n >= 2:
                    act.wait_ge(hq_summed, n - 1)
                act.activation(sq[:, n % 2, :], src, ACT.Square).then_inc(hq_sq, 1)

            def head_root(group):
                act.wait_ge(hq_summed, (12, 21)[group])
                act.wait_ge(hq_rstd if group else rstd_done, group or NKL + 1)
                act.activation(head_std[:, :], pb[4 + group][0:MH, :], ACT.Sqrt, bias=eps[0:MH, 0:1], scale=1.0 / (NOPE + ROPE))\
                   .then_inc(hq_std, 1)

            for s in range(12):
                hi(M_Q + s + 2)
                if s == 1:
                    root(NKL, KKV * P)
                if s == 3:
                    norm_hi(NKL, nH[:, KQ:KD, :])
                act.wait_ge(out_taken, T_MQ + s + 1)
                if s == 0:
                    act.wait_ge(ssq_done, SS0[N2B])
                head_square(s, qr[:, s, :] if s < 4 else qn[:, s - 4, :])
            head_square(12, lat[:, 8, :])
            for g in range(2):
                if g:
                    head_root(0)
                hi(M_K + g + 2)
                act.wait_ge(strip_used, M_K + g + 1)
                for h in range(4 * g, 4 * g + 4):
                    act.activation(kn[:, h, :], pb[h % 4][:, :], ACT.Copy).then_inc(out_taken, 1)
                for h in range(4 * g, 4 * g + 4):
                    act.wait_ge(out_taken, T_MK + h + 1)
                    head_square(13 + h, kn[:, h, :])
            for g in range(2):
                if g == 0:
                    head_root(1)
                hi(M_V + g + 2)
                act.wait_ge(strip_used, M_V + g + 1)
                for i in range(NB):
                    act.activation(V2[:, i, 512 * g:512 * g + 512], pb[i][:, :], ACT.Copy).then_inc(out_taken, 1)

            def soft(u):
                h, b = divmod(u, NB)
                act.wait_ge(bias_ready, 32 + u + 1)
                p = prob2[:, u % 4, 0:(b + 1) * P]
                act.activation(p, p, ACT.Exp, bias=stat[:, 16 + u % 4:17 + u % 4], scale=SCALE2,
                               accum_out=stat[:, 20 + u % 4:21 + u % 4]).then_inc(exp_done, 1)

            def turn_out(u):
                h, b = divmod(u, NB)
                act.wait_ge(p_turned, 32 + u + 1)
                if b == 0 and h >= 2:
                    act.wait_ge(pv_done, NB + h - 1)
                act.activation(pT2[h % 2][:, 0:b + 1, b * P:(b + 1) * P],
                               pb[2 + u % 2][:, 0:(b + 1) * P].rearrange("p (k q) -> p k q", q=P), ACT.Copy).then_inc(pt_act, 1)

            def head_out(h):
                act.wait_ge(pv_done, NB + h + 1)
                act.activation(oH[:, h, :], pb[4 + h % 2][:, :], ACT.Copy).then_inc(att_hi, 1)

            for u in range(MH * NB + LAG + 2):
                if u < MH * NB:
                    soft(u)
                if 0 <= u - LAG < MH * NB:
                    turn_out(u - LAG)
                if head_at(u - LAG - 2) is not None:
                    head_out(head_at(u - LAG - 2))
            residual_squares(M_OUT, T_MOUT, N2B, "ffn2b")
            ffn(*ffns[3])

        @block.tensor
        def _(pe):
            def three(ps, lhs, rhs, first, last):
                (lh, ll), (rh, rl) = lhs, rhs
                pe.matmul(ps, lh, rh, start=first, stop=False)
                pe.matmul(ps, lh, rl, start=False, stop=False)
                return pe.matmul(ps, ll, rh, start=False, stop=last)

            def weights(n, c, w=P):
                return wH[:, n % 2, c:c + w], wL[:, n % 2, c:c + w]

            def norm_sum(q):
                pe.wait_ge(ssq_done, SS0[q] + KT[q] + 1)
                if q:
                    pe.wait_ge(std_done, q)
                else:
                    pe.wait_ge(ones_set, 2)
                pe.matmul(pb[6][:, 0:WID[q]], ones[:, :], ssq[:, 0:WID[q]], start=True, stop=True).then_inc(norm_summed, 1)

            def whole(n, tile, kt, high, low, lows_of=None, c0=0, used=True, at=None):
                pe.wait_ge(strip_lo, n + 1)
                if at is None:
                    pe.wait_ge(out_taken, tile - 1)
                elif at == 0:
                    pe.wait_ge(out_taken, tile)
                for k in range(kt):
                    if lows_of is not None:
                        pe.wait_ge(h_lo, lows_of + k + 1)
                    mm = three(pb[bank(tile) if at is None else at][:, :], weights(n, c0 + k * P), (high[:, k, :], low[:, k, :]),
                               k == 0, k == kt - 1)
                if used:
                    mm.then_inc(strip_used, 1)

            def mod_sum(b):
                pe.wait_ge(ada_added, 8 * b + 8)
                if b:
                    pe.wait_ge(mod_ready, b)
                for m in range(KD):
                    mm = pe.matmul(pb[7][:, 8 * b + m:8 * b + m + 1], acc[:, b % 2, m * P:(m + 1) * P], ones[:, 0:1], start=True, stop=True)
                if b < 2:
                    for m in range(KD):
                        mm = pe.matmul(pb[7][:, 48 + 8 * b + m:49 + 8 * b + m], accc[:, b % 2, m * P:(m + 1) * P], ones[:, 0:1],
                                       start=True, stop=True)
                mm.then_inc(mod_summed, 1)

            norm_sum(NCTX)
            norm_sum(NX)
            mod_sum(0)
            mod_sum(1)
            for s in range(18):
                pe.wait_ge(strip_lo, s + 1)
                if s >= 2:
                    pe.wait_ge(out_taken, s - 1)
                for k in range(KD):
                    if s == 0:
                        pe.wait_ge(h_lo, LO0[NX] + k + 1)
                    mm = three(pb[bank(s)][:, :], weights(s, k * P), (hH[:, k, :], hL[:, k, :]), k == 0, k == KD - 1)
                if s < 2:
                    for k in range(KD):
                        mm = three(pb[bank(s) + 1][:, 0:C], weights(s, k * P), (cH[:, k, :], cL[:, k, :]), k == 0, k == KD - 1)
                mm.then_inc(strip_used, 1)
                if s in ROT_AT:
                    r = ROT_AT[s]
                    src = kT[:, 0:T] if r == 0 else qT[:, r - 1, :]
                    pe.wait_ge(out_taken, s)
                    if r >= 2:
                        pe.wait_ge(rope_done, r - 1)
                    pe.matmul(pb[4 + r % 2][:, :], tab("turn"), src, start=True, stop=True).then_inc(turned, 1)
                if s in (4, 8, 12, 16):
                    mod_sum(1 + s // 4)
                if s == 9:
                    pe.wait_ge(rope_done, 5)
                    for i in range(6):
                        mm = pe.transpose(pb[4 + i // 4][:, (i % 4) * P:(i % 4 + 1) * P], vT[:, i * P:(i + 1) * P], tab("ident"))
                        if i in (3, 5):
                            mm.then_inc(v_turned, 1)

            def att_scores(u):
                n, a, j = UNITS[u]
                lo_, hi_ = keys(n)
                if u < 2:
                    pe.wait_ge(out_taken, 18)
                    pe.wait_ge(rope_done, 5)
                else:
                    pe.wait_ge(masked, u - 1)
                    pe.wait_ge(ctx_copied, u - 1)
                q = qT[64 * j:64 * j + 64, a, n * P:(n + 1) * P]
                pe.matmul(pb[2 * j][:, 0:hi_ - lo_], q, kT[64 * j:64 * j + 64, lo_:hi_], start=True, stop=True)
                pe.matmul(pb[2 * j + 1][:, 0:C], q, kT[64 * j:64 * j + 64, T:T + C], start=True, stop=True).then_inc(scored, 1)

            def att_turn(u):
                tiles = len(kv_tiles[UNITS[u][0]])
                pe.wait_ge(p_ready, u + 1)
                if u >= 2:
                    pe.wait_ge(pt_act, u - 1)
                if tiles == 5:
                    pe.wait_ge(v_ready, 2)
                    pe.wait_ge(pt_dve, b_units(u))
                for k in range(tiles):
                    dst = pb[4 + 2 * (u % 2)][:, k * P:(k + 1) * P] if k < 4 else pb[5][:, 0:P]
                    mm = pe.transpose(dst, prob[:, u % 4, k * P:(k + 1) * P], tab("ident"))
                mm.then_inc(p_turned, 1)

            def att_values(n):
                pe.wait_ge(pt_act, 8 * n + 8)
                pe.wait_ge(pt_dve, b_units(8 * n + 8))
                pe.wait_ge(v_ready, 2)
                if n == 0:
                    pe.wait_ge(mod_ready, 6)
                else:
                    pe.wait_ge(att_lo, n)
                tiles = len(kv_tiles[n])
                for k, v in enumerate(kv_tiles[n]):
                    for j in range(2):
                        mm = pe.matmul(pb[7][64 * j:64 * j + 64, :], V[:, v, 64 * j:64 * j + 64], PT[:, j, k, :],
                                       start=(k == 0), stop=(k == tiles - 1))
                mm.then_inc(pv_done, 1)

            for u in range(len(UNITS) + LAG + 1):
                if u < len(UNITS):
                    att_scores(u)
                if 0 <= u - LAG < len(UNITS):
                    att_turn(u - LAG)
                if block_at(u - LAG - 1) is not None:
                    att_values(block_at(u - LAG - 1))

            pe.wait_ge(cat_lo, 4)
            pe.wait_ge(att_lo, NB)
            for s in range(KD):
                whole(W_OUT + s, T_OUT + s, KD, catH, catL)

            norm_sum(NH2)
            pe.wait_ge(wr_loaded, 16)
            pe.wait_ge(h_hi, HI0[NH2] + KD)
            for i in range(NB):
                for k in range(KD):
                    mm = pe.matmul(pb[4][:, i * E:(i + 1) * E], h2[:, k, i * P:(i + 1) * P], wr[:, k, :], start=(k == 0), stop=(k == KD - 1))
            mm.then_inc(logits_done, 1)
            for m in range(8):
                if m >= 2:
                    pe.wait_ge(h2t_ready, m - 1)
                for i in range(4):
                    mm = pe.transpose(pb[m % 2][:, i * P:(i + 1) * P], h2[:, 4 * (m % 2) + i, (m // 2) * P:(m // 2 + 1) * P], tab("ident"))
                mm.then_inc(h2_turned, 1)
                if m == 3:
                    pe.wait_ge(aff_ready, NB)
                    for i in range(NB):
                        mm = pe.transpose(pb[5][0:E, i * P:(i + 1) * P], af[:, i, :], tab("ident"))
                    mm.then_inc(aff_turned, 1)
            pe.wait_ge(top_step, 20)
            for i in range(NB):
                mm = pe.transpose(pb[5][:, i * E:(i + 1) * E], pos[:, i * P:(i + 1) * P], tab("ident", E)[0:E, :])
            mm.then_inc(pos_turned, 1)
            pe.wait_ge(h2t_ready, 8)

            def gather(it, p):
                pe.wait_ge(pick_ready, count(it, p, 1, 1))
                for half in range(2):
                    for k in range(NB):
                        mm = pe.matmul(pb[6 + half][:, :], pick[:, k, :], h2t[:, k, half * 512:(half + 1) * 512],
                                       start=(k == 0), stop=(k == NB - 1))
                    mm.then_inc(gathered, 1)

            def turn_tokens(it, p):
                for half, copied in enumerate((xs_act, xs_dve)):
                    pe.wait_ge(copied, count(it, p, 1, 1))
                    for k in range(4):
                        c = (4 * half + k) * P
                        mm = pe.transpose(pb[2 + half][:, k * P:(k + 1) * P], xs[:, c:c + P], tab("ident"))
                    mm.then_inc(xs_turned, 1)

            def scatter(it, p, k):
                if k == 0:
                    pe.wait_ge(pgT_ready, count(it, p, 1, 1))
                    pe.wait_ge(y_act, count(it, p, 1, 1))
                if k == 4:
                    pe.wait_ge(y_dve, count(it, p, 1, 1))
                if k >= 2:
                    pe.wait_ge(x_added, count(it, p, KD, k - 1))
                pe.matmul(pb[7 - k % 2][:, :], xs[:, k * P:(k + 1) * P], pickgT[:, :], start=True, stop=True).then_inc(scattered, 1)

            def gate_up(it, p):
                for k in range(KD):
                    if k == 0:
                        pe.wait_ge(xsT_act, count(it, p, 1, 1))
                        pe.wait_ge(xsT_dve, count(it, p, 1, 1))
                    for g in range(2):
                        d = 2 * k + g
                        pe.wait_ge(exp_landed[d % 8], count(it, p, 48, 16 * (d // 8 + 1)))
                        for half in range(2):
                            for j in range(2):
                                mm = pe.matmul(pb[2 * g + half][64 * j:64 * j + 64, :], xsT[:, k, 64 * j:64 * j + 64],
                                               ring[:, 2 * (d % 8) + j, half * 512:(half + 1) * 512],
                                               start=(k == 0), stop=(k == KD - 1))
                        mm.then_inc(exp_used, 1)
                    if it is not None and 2 <= k < 6:
                        scatter(it, p - 1, 2 * k - 4)
                        scatter(it, p - 1, 2 * k - 3)

            def turn_hidden(it, p):
                for half in range(2):
                    pe.wait_ge(hid_done, count(it, p, 2, half + 1))
                    for k in range(4):
                        c = (4 * half + k) * P
                        mm = pe.transpose(pb[half][:, k * P:(k + 1) * P], hid[:, c:c + P], tab("ident"))
                    mm.then_inc(hid_turned, 1)

            def down(it, p):
                for k in range(8):
                    if k == 0:
                        pe.wait_ge(hidT_act, count(it, p, 1, 1))
                    if k == 4:
                        pe.wait_ge(hidT_dve, count(it, p, 1, 1))
                    d = 16 + k
                    pe.wait_ge(exp_landed[d % 8], count(it, p, 48, 16 * (d // 8 + 1)))
                    for half in range(2):
                        for j in range(2):
                            mm = pe.matmul(pb[4 + half][64 * j:64 * j + 64, :], hidT[:, k, 64 * j:64 * j + 64],
                                           ring[:, 2 * (d % 8) + j, half * 512:(half + 1) * 512],
                                           start=(k == 0), stop=(k == 7))
                    mm.then_inc(exp_used, 1)
                pe.wait_ge(pickg_ready, count(it, p, 1, 1))
                for k in range(NB):
                    mm = pe.transpose(pb[6][:, k * P:(k + 1) * P], pickg[:, k, :], tab("ident"))
                mm.then_inc(pg_turned, 1)

            gather(None, 0)
            turn_tokens(None, 0)
            gate_up(None, 0)
            with pe.Fori(0, PAIRS - 1) as i:
                gather(i, 1)
                turn_hidden(i, 0)
                turn_tokens(i, 1)
                down(i, 0)
                gate_up(i, 1)
                pe.wait_ge(x_added, count(i, 0, KD, KD))
            turn_hidden(None, PAIRS - 1)
            down(None, PAIRS - 1)
            for k in range(KD):
                scatter(None, PAIRS - 1, k)

            def ffn(n0, t0, f, q):
                def inner(tile, it, waits):
                    for part in range(2):
                        n = n0 + 2 * tile + part
                        pe.wait_ge(strip_lo, shifted(n + 1, it))
                        if part == 0:
                            pe.wait_ge(out_taken, shifted(t0 + tile - 1, it, 2))
                        for k in range(KD):
                            if waits and part == 0:
                                pe.wait_ge(h_lo, LO0[q] + k + 1)
                            mm = three(pb[bank(t0 + tile) + part][:, :], weights(n, k * P), (hH[:, k, :], hL[:, k, :]), k == 0, k == KD - 1)
                        mm.then_inc(strip_used, 1)

                def outer(m, it):
                    t = t0 + KF + m
                    for half in range(2):
                        n = n0 + 2 * KF + 2 * m + half
                        pe.wait_ge(strip_lo, shifted(n + 1, it))
                        pe.wait_ge(g_lo, f * KF + HALF_KF * (half + 1))
                        if half == 0:
                            pe.wait_ge(out_taken, shifted(t - 1, it, 2))
                        for k in range(HALF_KF):
                            g = half * HALF_KF + k
                            mm = three(pb[bank(t)][:, :], weights(n, k * P), (gH[:, g, :], gL[:, g, :]), g == 0, g == KF - 1)
                        mm.then_inc(strip_used, 1)

                inner(0, None, True)
                norm_sum(q)
                inner(1, None, False)
                with pe.Fori(0, KF // 2 - 1) as i:
                    inner(2, i, False)
                    inner(3, i, False)
                with pe.Fori(0, KD // 2) as i:
                    outer(0, i)
                    outer(1, i)

            norm_sum(NFIN)
            ffn(*ffns[0])
            norm_sum(NMA)
            for g in range(4):
                pe.wait_ge(pool_lo, g + 1)
                for m in range(2):
                    whole(POOL + g, T_POOL + 2 * g + m, 2, hH[:, 2 * g:2 * g + 2, :], hL[:, 2 * g:2 * g + 2, :], c0=2 * m * P, used=(m == 1))
            ffn(*ffns[1])
            ffn(*ffns[2])

            for s in range(9):
                whole(M_IN + s, T_MIN + s, KD, hH, hL, lows_of=LO0[NMB] if s == 0 else None)
                if s == 0:
                    norm_sum(NMB)
                if s == KQ:
                    norm_sum(NQL)

            def turn(r, src):
                pe.wait_ge(gained, r + 1)
                if r >= 2:
                    pe.wait_ge(rope_done, 5 + r - 1)
                pe.matmul(pb[6 + r % 2][:, :], tab("turn"), src, start=True, stop=True).then_inc(turned, 1)

            def head_sum(n):
                pe.wait_ge(hq_sq, n + 1)
                if n < 4:
                    rows = tab("two_rows")[:, 6 - 2 * n:14 - 2 * n]
                elif n == 12:
                    rows = tab("lower")
                else:
                    h = n - 4 if n < 12 else n - 13
                    rows = tab("one_row")[:, 7 - h:15 - h]
                pe.matmul(pb[4 if n < 12 else 5][0:MH, :], rows, sq[:, n % 2, :], start=n in (0, 12), stop=n in (11, 20))\
                  .then_inc(hq_summed, 1)

            def spread_rows(n):
                if n == 0:
                    pe.wait_ge(select_loaded, 16)
                pe.wait_ge(hq_rstd, 1 if n < 12 else 2)
                if n >= 2:
                    pe.wait_ge(hq_out, OUTS[n - 1])
                pe.matmul(pb[6 + n % 2][:, :], select[:, n if n < 12 else n - 12, :], head_rstd[n >= 12][:, :], start=True, stop=True)\
                  .then_inc(spread, 1)

            for s in range(12):
                whole(M_Q + s, T_MQ + s, KQ, nH, nL, lows_of=LO0[NQL] if s == 0 else None)
                if s == 0:
                    norm_sum(NKL)
                if s == 1:
                    pe.wait_ge(std_done, NKL + 1)
                if 1 <= s <= 5:
                    r = s - 1
                    turn(r, krope[:, :] if r == 0 else qr[:, r - 1, :])
                if s:
                    head_sum(s - 1)

            def keys_of(g):
                for m in range(4):
                    whole(M_K + g, T_MK + 4 * g + m, KKV, nH[:, KQ:KD, :], nL[:, KQ:KD, :],
                          lows_of=LO0[NKL] if g == m == 0 else None, c0=2 * m * P, used=(m == 3), at=m)

            def values_of(g):
                n = M_V + g
                pe.wait_ge(strip_lo, n + 1)
                pe.wait_ge(out_taken, T_MV + 4 * g)
                for i in range(NB):
                    for k in range(KKV):
                        lhs = (nH[:, KQ + k, i * P:(i + 1) * P], nL[:, KQ + k, i * P:(i + 1) * P])
                        mm = three(pb[i][:, :], lhs, weights(n, k * 512, 512), k == 0, k == KKV - 1)
                mm.then_inc(strip_used, 1)

            keys_of(0)
            head_sum(11)
            head_sum(12)
            keys_of(1)
            for h in range(4):
                head_sum(13 + h)
            for n in range(6):
                spread_rows(n)
            for h in range(4, 8):
                head_sum(13 + h)
            values_of(0)
            for n in range(6, 12):
                spread_rows(n)
            values_of(1)
            for n in range(12, 20):
                spread_rows(n)

            def scores(u):
                h, b = divmod(u, NB)
                w = (b + 1) * P
                if u < 2:
                    pe.wait_ge(out_taken, T_MOUT)
                    pe.wait_ge(hq_out, OUTS[20])
                elif u >= 4:
                    pe.wait_ge(masked, 32 + u - 3)
                pe.matmul(pb[S2[u % 4]][:, 0:w], qn[:, h, b * P:(b + 1) * P], kn[:, h, 0:w], start=True, stop=False)
                pe.matmul(pb[S2[u % 4]][:, 0:w], qr[:, h // 2, b * P:(b + 1) * P], kr[:, h, 0:w], start=False, stop=True).then_inc(scored, 1)

            def turn_probs(u):
                h, b = divmod(u, NB)
                pe.wait_ge(p_ready, 32 + u + 1)
                pe.wait_ge(pt_act, 32 + u - 1)
                for k in range(b + 1):
                    mm = pe.transpose(pb[2 + u % 2][:, k * P:(k + 1) * P], prob2[:, u % 4, k * P:(k + 1) * P], tab("ident"))
                mm.then_inc(p_turned, 1)

            def values(h):
                pe.wait_ge(pt_act, 32 + NB * h + NB)
                if h >= 2:
                    pe.wait_ge(att_lo, NB + h - 1)
                for k in range(NB):
                    mm = pe.matmul(pb[4 + h % 2][:, k * P:T], V2[:, k, h * P:(h + 1) * P], pT2[h % 2][:, k, k * P:T],
                                   start=(k == 0), stop=(k == NB - 1))
                mm.then_inc(pv_done, 1)

            for u in range(MH * NB + LAG + 1):
                if u < MH * NB:
                    scores(u)
                if 0 <= u - LAG < MH * NB:
                    turn_probs(u - LAG)
                if head_at(u - LAG - 1) is not None:
                    values(head_at(u - LAG - 1))
            pe.wait_ge(att_lo, NB + MH)
            for s in range(KD):
                whole(M_OUT + s, T_MOUT + s, KD, oH, oL)
            ffn(*ffns[3])

        @block.vector
        def _(dve):
            def lo(n, it=None):
                if n >= N_STRIPS:
                    return
                dve.wait_ge(strip_hi, shifted(n + 1, it))
                w = width[n]
                dve.tensor_tensor(wL[:, n % 2, 0:w], stage[:, n % STAGE, 0:w], wH[:, n % 2, 0:w], ALU.subtract).then_inc(strip_lo, 1)

            def clear(q):
                if q:
                    dve.wait_ge(norm_summed, q)
                dve.memset(ssq[:, :], 0.0).then_inc(ssq_done, 1)

            def add(q, k, it=None):
                dve.wait_ge(sq_done, shifted(SQ0[q] + k + 1, it, 2))
                dve.wait_ge(ssq_done, shifted(SS0[q] + k + 1, it, 2))
                w = WID[q]
                dve.tensor_tensor(ssq[:, 0:w], ssq[:, 0:w], sq[:, (SQ0[q] + k) % 2, 0:w], ALU.add).then_inc(ssq_done, 1)

            def invert(q):
                dve.wait_ge(std_done, q + 1)
                dve.reciprocal(rstd_of[q][:, 0:WID[q]], std[:, 0:WID[q]]).then_inc(rstd_done, 1)

            def norm_low(q, src, gain, high, low, shift=None):
                w = WID[q]
                dve.wait_ge(rstd_done, q + 1)
                for k in range(KT[q] + 1):
                    if k < KT[q]:
                        if q or k >= 2:
                            dve.wait_ge(h_hi, HI0[q] + max(k - 1, 0))
                            dve.wait_ge(h_lo, LO0[q] + (max(k - 1, 0) if low is not None else 0))
                        dve.scalar_tensor_tensor(out=hraw[:, (RAW0[q] + k) % 2, 0:w], in0=src[:, k, :], scalar=gain(k),
                                                 in1=rstd_of[q][:, 0:w], op0=ALU.mult, op1=ALU.mult).then_inc(h_raw, 1)
                    if k and low is not None:
                        dve.wait_ge(h_hi, HI0[q] + k)
                        raw = hraw[:, (RAW0[q] + k - 1) % 2, 0:w]
                        if shift is None:
                            ins = dve.tensor_tensor(low[:, k - 1, :], raw, high[:, k - 1, :], ALU.subtract)
                        else:
                            ins = dve.scalar_tensor_tensor(out=low[:, k - 1, :], in0=raw, scalar=mod[:, shift + k - 1:shift + k],
                                                           in1=high[:, k - 1, :], op0=ALU.add, op1=ALU.subtract)
                        ins.then_inc(h_lo, 1)

            def lowered(q, k, src, gain, it=None):
                g = k if it is None else it * 2 + k
                a = COL[gain][0]
                scale = cols[:, a + k:a + k + 1] if it is None else cols[:, bass.ds(it * 2 + (a + k), 1)]
                high, low = (nH, nL) if q == NQL else (hH, hL)
                dve.wait_ge(h_hi, shifted(HI0[q] + k + 1, it, 2))
                dve.scalar_tensor_tensor(out=low[:, g, :], in0=src[:, g, :], scalar=scale, in1=high[:, g, :],
                                         op0=ALU.mult, op1=ALU.subtract).then_inc(h_lo, 1)

            def ada(a):
                b, k = divmod(a, KD)
                dve.wait_ge(ada_landed[a % 4], 16 * (a // 4 + 1))
                if a == 0:
                    dve.wait_ge(cond_ready, 1)
                if k == 0 and b >= 2:
                    dve.wait_ge(mod_summed, b - 1)
                for into, vec, done in ((accc, KD, adac_added), (acc, 0, ada_added)):
                    if into is accc and b >= 2:
                        continue
                    w, v = adaw[:, a % 4, :], stat[:, vec + k:vec + k + 1]
                    if k == 0:
                        dve.tensor_scalar(into[:, b % 2, :], w, v, None, ALU.mult).then_inc(done, 1)
                    else:
                        dve.wait_ge(done, a)
                        dve.scalar_tensor_tensor(out=into[:, b % 2, :], in0=w, scalar=v, in1=into[:, b % 2, :],
                                                 op0=ALU.mult, op1=ALU.add).then_inc(done, 1)

            def mod_take(b):
                dve.wait_ge(mod_summed, b + 1)
                bias = cols[:, COL["b_ada"][0] + 8 * b:COL["b_ada"][0] + 8 * b + 8]
                if b < 2:
                    dve.tensor_tensor(mod[:, 48 + 8 * b:56 + 8 * b], pb[7][:, 48 + 8 * b:56 + 8 * b], bias, ALU.add)
                dve.tensor_tensor(mod[:, 8 * b:8 * b + 8], pb[7][:, 8 * b:8 * b + 8], bias, ALU.add).then_inc(mod_ready, 1)

            def mod_gain(dst, scale_col, g, need):
                dve.wait_ge(mod_ready, need)
                dve.scalar_tensor_tensor(out=gain1[:, dst:dst + 8], in0=mod[:, scale_col:scale_col + 8], scalar=1.0,
                                         in1=cols[:, COL[g][0]:COL[g][0] + 8], op0=ALU.add, op1=ALU.mult).then_inc(gain_ready, 1)

            dve.wait_ge(small_loaded, 64)
            sink = cols[:, COL["sink"][0]:COL["sink"][0] + H]
            dve.tensor_scalar(stat[:, 40:48], sink, -1.0, None, ALU.mult).then_inc(gain_ready, 1)
            dve.tensor_scalar(stat[:, 48:56], sink, 1.0 / SCALE1, None, ALU.mult).then_inc(gain_ready, 1)
            for q in (NCTX, NX):
                clear(q)
                for k in range(KD):
                    add(q, k)
            invert(NCTX)
            invert(NX)
            for a in range(16):
                ada(a)
            mod_take(0)
            mod_take(1)
            mod_gain(0, 8, "g_mix", 2)
            mod_gain(8, 56, "g_mix", 2)
            lo(0)
            lo(1)
            dve.wait_ge(gain_ready, 4)
            norm_low(NCTX, ctx, lambda k: gain1[:, 8 + k:9 + k], cH, cL, shift=48)
            norm_low(NX, x, lambda k: gain1[:, k:k + 1], hH, hL, shift=0)

            def rope_finish(r, dst, rot, sine, cosine, tmp, r0, part0):
                dve.wait_ge(turned, r0 + 1)
                if r0:
                    dve.wait_ge(rope_done, r0)
                dve.tensor_tensor(tmp, rot, sine, ALU.mult).then_inc(rope_part, 1)
                dve.tensor_tensor(dst, dst, cosine, ALU.mult).then_inc(rope_part, 1)
                dve.wait_ge(rope_part, 2 * r0 + 2)
                dve.tensor_tensor(dst, dst, tmp, ALU.add).then_inc(rope_done, 1)

            for s in range(18):
                if s < 16:
                    ada(16 + 2 * s)
                    ada(17 + 2 * s)
                lo(s + 2)
                dve.wait_ge(strip_used, s + 1)
                ps = pb[bank(s)][:, :]
                if s < 2:
                    dst = (kT, vT)[s]
                    dve.tensor_copy(dst[:, 0:T], ps)
                    dve.tensor_copy(dst[:, T:T + C], pb[bank(s) + 1][:, 0:C]).then_inc(out_taken, 1)
                elif s < 6:
                    dve.tensor_copy(qT[:, s - 2, :], ps).then_inc(out_taken, 1)
                else:
                    i, part = divmod(s - 6, 3)
                    w3 = [cols[:, COL["conv_w"][0] + 3 * i + j:COL["conv_w"][0] + 3 * i + j + 1] for j in range(3)]
                    y, u = gf[:, 0, :], sg[:, 1, :]
                    if part == 0:
                        dve.tensor_copy(sg[:, 0, :], ps).then_inc(out_taken, 1)
                    elif part == 1:
                        dve.wait_ge(out_taken, s)
                        dve.tensor_tensor(u, ps, sg[:, 0, :], ALU.mult).then_inc(out_taken, 1)
                        dve.wait_ge(out_taken, s + 1)
                        dve.tensor_scalar(y, u, w3[1], None, ALU.mult).then_inc(conv_part, 1)
                        dve.wait_ge(conv_part, 3 * i + 1)
                        dve.scalar_tensor_tensor(out=y[:, 1:T], in0=u[:, 0:T - 1], scalar=w3[0], in1=y[:, 1:T],
                                                 op0=ALU.mult, op1=ALU.add).then_inc(conv_part, 1)
                        dve.wait_ge(conv_part, 3 * i + 2)
                        dve.scalar_tensor_tensor(out=y[:, 0:T - 1], in0=u[:, 1:T], scalar=w3[2], in1=y[:, 0:T - 1],
                                                 op0=ALU.mult, op1=ALU.add).then_inc(conv_part, 1)
                    else:
                        dve.wait_ge(conv_part, 3 * i + 3)
                        dve.tensor_tensor(conv[:, i, :], ps, y, ALU.mult).then_inc(out_taken, 1)
                if s - 1 in ROT_AT:
                    r = ROT_AT[s - 1]
                    rope_finish(r, kT[:, 0:T] if r == 0 else qT[:, r - 1, :], pb[4 + r % 2][:, :], rope[:, 1, :], rope[:, 0, :],
                                gf[:, 1, :], r, 2 * r)
                if s in (6, 10, 14):
                    mod_take(s // 4 + 1)
                if s == 11:
                    dve.wait_ge(v_turned, 2)
                    dve.tensor_copy(V[:, 0:4, :], pb[4][:, :].rearrange("p (k d) -> p k d", k=4)).then_inc(v_ready, 1)
                    dve.tensor_copy(V[:, 4:6, :], pb[5][:, 0:C].rearrange("p (k d) -> p k d", k=2)).then_inc(v_ready, 1)
            mod_take(5)
            mod_gain(16, 32, "g_ffn", 6)
            for k in range(4):
                dve.wait_ge(cat_hi, k + 1)
                dve.tensor_tensor(catL[:, 4 + k, :], conv[:, k, :], catH[:, 4 + k, :], ALU.subtract).then_inc(cat_lo, 1)

            def att_max(u):
                n, a, j = UNITS[u]
                w = keys(n)[1] - keys(n)[0]
                off = P if n == 0 else 0
                head = a + 4 * j
                m1, m2 = stat[:, 28 + u % 4:29 + u % 4], stat[:, 32 + u % 4:33 + u % 4]
                dve.wait_ge(ctx_copied, u + 1)
                if u >= 4:
                    dve.wait_ge(p_turned, u - 3)
                dve.reduce_max(m1, prob[:, u % 4, 0:C], AX_X).then_inc(row_max, 1)
                dve.tensor_copy(prob[:, u % 4, C + w:C + w + 1], stat[:, 48 + head:49 + head]).then_inc(row_max, 1)
                dve.wait_ge(row_max, 2 * u + 2)
                dve.tensor_tensor_reduce(prob[:, u % 4, C:C + w], pb[2 * j][:, 0:w], window[:, off:off + w], 1.0, m1,
                                         ALU.add, ALU.max, m2).then_inc(masked, 1)
                dve.wait_ge(masked, u + 1)
                dve.tensor_scalar(stat[:, 16 + u % 4:17 + u % 4], m2, -SCALE1, stat[:, 40 + head:41 + head],
                                  ALU.mult, ALU.min).then_inc(bias_ready, 1)

            def scale_probs(v, p):
                dve.wait_ge(exp_done, v + 1)
                dve.reciprocal(stat[:, 24 + v % 4:25 + v % 4], stat[:, 20 + v % 4:21 + v % 4]).then_inc(inv_ready, 1)
                dve.wait_ge(inv_ready, v + 1)
                dve.tensor_scalar(p, p, stat[:, 24 + v % 4:25 + v % 4], None, ALU.mult).then_inc(p_ready, 1)

            def att_fifth(u):
                n, a, j = UNITS[u]
                if len(kv_tiles[n]) == 5:
                    dve.wait_ge(p_turned, u + 1)
                    if a == j == 0:
                        dve.wait_ge(pv_done, n)
                    dve.tensor_copy(PT[:, j, 4, a * P:(a + 1) * P], pb[5][:, 0:P]).then_inc(pt_dve, 1)

            def att_low(n):
                dve.wait_ge(att_hi, n + 1)
                dve.tensor_tensor(catL[:, 0:4, n * P:(n + 1) * P], pb[7][:, :].rearrange("p (k q) -> p k q", k=4),
                                  catH[:, 0:4, n * P:(n + 1) * P], ALU.subtract).then_inc(att_lo, 1)

            for u in range(len(UNITS) + LAG + 3):
                if u < len(UNITS):
                    att_max(u)
                if 1 <= u <= len(UNITS):
                    n = UNITS[u - 1][0]
                    scale_probs(u - 1, prob[:, (u - 1) % 4, 0:C + keys(n)[1] - keys(n)[0]])
                if 0 <= u - LAG < len(UNITS):
                    att_fifth(u - LAG)
                if block_at(u - LAG - 2) is not None:
                    att_low(block_at(u - LAG - 2))

            def residual(n0, t0, q, gain, after=None):
                clear(q)
                for s in range(KD):
                    lo(n0 + s + 2)
                    dve.wait_ge(strip_used, n0 + s + 1)
                    ps = pb[bank(t0 + s)][:, :]
                    dve.scalar_tensor_tensor(out=x[:, s, :], in0=ps, scalar=gain(s), in1=x[:, s, :], op0=ALU.mult, op1=ALU.add)\
                       .then_inc(out_taken, 1)
                    if s:
                        add(q, s - 1)
                        if after:
                            lowered(q, s - 1, x, after)
                add(q, KD - 1)
                if after:
                    lowered(q, KD - 1, x, after)

            residual(W_OUT, T_OUT, NH2, lambda m: mod[:, 16 + m:17 + m])

            invert(NH2)
            norm_low(NH2, x, lambda k: gain1[:, 16 + k:17 + k], None, None)
            dve.wait_ge(logits_done, 1)
            logits = pb[4][:, 0:NB * E].rearrange("p (i e) -> p i e", i=NB)
            dve.tensor_reduce(stat[:, 0:4], logits, AX_X, ALU.max).then_inc(lmax, 1)
            dve.wait_ge(lmax, 1)
            dve.tensor_scalar(stat[:, 4:8], stat[:, 0:4], -1.0, None, ALU.mult).then_inc(lmax, 1)
            dve.wait_ge(aff_exp, 4)
            dve.reciprocal(stat[:, 12:16], stat[:, 8:12]).then_inc(lmax, 1)
            dve.wait_ge(lmax, 3)
            for i in range(NB):
                dve.tensor_scalar(af[:, i, :], af[:, i, :], stat[:, 12 + i:13 + i], None, ALU.mult).then_inc(aff_ready, 1)
            dve.wait_ge(aff_turned, 1)
            dve.tensor_copy(work[:, 0, :], pb[5][0:E, :]).then_inc(top_step, 1)
            for r in range(SLOTS // 8):
                dve.wait_ge(top_step, 2 * r + 1)
                dve.max(top[:, r, :], work[:, r % 2, :]).then_inc(top_step, 1)
                dve.wait_ge(top_step, 2 * r + 2)
                dve.match_replace(work[:, (r + 1) % 2, :], top[:, r, :], work[:, r % 2, :], -1.0).then_inc(top_step, 1)
            dve.wait_ge(top_step, 17)
            dve.tensor_scalar(work[:, 1, :], work[:, 0, :], 0.0, None, ALU.is_lt).then_inc(top_step, 1)
            dve.wait_ge(top_step, 18)
            dve.tensor_tensor_scan(afT[:, :], work[:, 1, :], work[:, 1, :], 0.0, ALU.add, ALU.max).then_inc(top_step, 1)
            dve.wait_ge(top_step, 19)
            dve.tensor_tensor(pos[:, :], afT[:, :], work[:, 1, :], ALU.mult).then_inc(top_step, 1)
            dve.wait_ge(pos_turned, 1)
            dve.tensor_copy(posT[:, :, :], pb[5][:, 0:NB * E].rearrange("p (i e) -> p i e", i=NB)).then_inc(posT_ready, 1)
            dve.wait_ge(posT_ready, 1)
            dve.wait_ge(ssq_done, SS0[NFIN])

            def picks(it, p, weighted):
                for k in range(NB):
                    for j in range(2):
                        e = slice(2 * p + j, 2 * p + j + 1) if it is None else bass.ds(it * 2 + (2 * p + j), 1)
                        o = (pickg if weighted else pick)[:, k, 64 * j:64 * j + 64]
                        if weighted:
                            ins = dve.tensor_scalar(o, tab("slot"), posT[:, k, e], af[:, k, e], ALU.is_equal, ALU.mult)
                        else:
                            ins = dve.tensor_scalar(o, tab("slot"), posT[:, k, e], None, ALU.is_equal)
                ins.then_inc(pickg_ready if weighted else pick_ready, 1)

            def tokens_out(it, p):
                dve.wait_ge(gathered, count(it, p, 2, 2))
                dve.tensor_copy(xs[:, 512:1024], pb[7][:, :]).then_inc(xs_dve, 1)

            def tokens_turned(it, p):
                dve.wait_ge(xs_turned, count(it, p, 2, 2))
                dve.tensor_copy(xsT[:, 4:8, :], pb[3][:, :].rearrange("p (k s) -> p k s", k=4)).then_inc(xsT_dve, 1)

            def hidden(it, p):
                for half in range(2):
                    dve.wait_ge(sil_done, count(it, p, 2, half + 1))
                    c = half * 512
                    dve.tensor_tensor(hid[:, c:c + 512], sil[:, c:c + 512], pb[2 + half][:, :], ALU.mult).then_inc(hid_done, 1)

            def hidden_turned(it, p):
                dve.wait_ge(hid_turned, count(it, p, 2, 2))
                dve.tensor_copy(hidT[:, 4:8, :], pb[1][:, :].rearrange("p (k s) -> p k s", k=4)).then_inc(hidT_dve, 1)

            def expert_out(it, p):
                dve.wait_ge(exp_used, count(it, p, 24, 24))
                dve.tensor_copy(xs[:, 512:1024], pb[5][:, :]).then_inc(y_dve, 1)
                for k in range(KD):
                    dve.wait_ge(scattered, count(it, p, KD, k + 1))
                    dve.scalar_tensor_tensor(out=x[:, k, :], in0=pb[7 - k % 2][:, :], scalar=mod[:, 40 + k:41 + k], in1=x[:, k, :],
                                             op0=ALU.mult, op1=ALU.add).then_inc(x_added, 1)

            picks(None, 0, False)
            tokens_out(None, 0)
            tokens_turned(None, 0)
            with dve.Fori(0, PAIRS - 1) as i:
                dve.wait_ge(gathered, count(i, 0, 2, 2))
                picks(i, 1, False)
                hidden(i, 0)
                tokens_out(i, 1)
                hidden_turned(i, 0)
                tokens_turned(i, 1)
                picks(i, 0, True)
                expert_out(i, 0)
            hidden(None, PAIRS - 1)
            hidden_turned(None, PAIRS - 1)
            picks(None, PAIRS - 1, True)
            expert_out(None, PAIRS - 1)

            def plain(q, dst, gain):
                dve.wait_ge(rstd_done, q + 1)
                for k in range(KD):
                    dve.scalar_tensor_tensor(out=dst[:, k, :], in0=x[:, k, :], scalar=gain(k), in1=rstd_of[q][:, :],
                                             op0=ALU.mult, op1=ALU.mult).then_inc(h_raw, 1)

            clear(NFIN)
            for k in range(KD):
                add(NFIN, k)
            invert(NFIN)
            plain(NFIN, x, lambda k: col("g_final", k))
            clear(N1A)
            for k in range(KD):
                add(N1A, k)
                lowered(N1A, k, x, "ffn1a")

            def ffn(n0, t0, f, q):
                def inner(tile, it):
                    dve.wait_ge(strip_used, shifted(n0 + 2 * tile + 2, it))
                    b, s, c = bank(t0 + tile), tile % 2, f * KF + tile
                    dve.tensor_tensor(hraw[:, s, :], pb[b][:, :], rstd[:, :], ALU.mult).then_inc(gate_ready, 1)
                    dve.wait_ge(strip_lo, shifted(n0 + 2 * tile + 3, it))
                    dve.tensor_tensor(gf[:, s, :], pb[b + 1][:, :], rstd[:, :], ALU.mult).then_inc(out_taken, 1)
                    dve.wait_ge(out_taken, shifted(t0 + tile + 1, it, 2))
                    dve.wait_ge(silu_done, shifted(c + 1, it, 2))
                    dve.tensor_tensor(gf[:, s, :], gf[:, s, :], sg[:, s, :], ALU.mult).then_inc(g_raw, 1)
                    dve.wait_ge(g_hi, shifted(c + 1, it, 2))
                    g = tile if it is None else it * 2 + tile
                    dve.tensor_tensor(gL[:, g, :], gf[:, s, :], gH[:, g, :], ALU.subtract).then_inc(g_lo, 1)

                def tiles(e, it):
                    lo(n0 + e + 2, it)
                    lo(n0 + e + 3, it)
                    inner(e // 2, it)
                    lo(n0 + e + 4, it)
                    lo(n0 + e + 5, it)
                    inner(e // 2 + 1, it)

                invert(q)
                dve.wait_ge(rstd_done, q + 1)
                with dve.Fori(0, KF // 2 - 1) as i:
                    tiles(0, i)
                tiles(2 * KF - 4, None)
                d0, q1 = n0 + 2 * KF, q + 1
                if q1 < 12:
                    clear(q1)

                def outer(m, it):
                    dve.wait_ge(strip_used, shifted(d0 + 2 * m + 2, it))
                    g = m if it is None else it * 2 + m
                    dve.scalar_tensor_tensor(out=x[:, g, :], in0=pb[bank(t0 + KF + m)][:, :], scalar=0.5, in1=x[:, g, :],
                                             op0=ALU.mult, op1=ALU.add).then_inc(out_taken, 1)
                    if q1 < 12:
                        add(q1, m, it)
                        if FOLDED[q1]:
                            lowered(q1, m, x, GAIN[q1], it)

                def down(e, it):
                    lo(d0 + e + 2, it)
                    lo(d0 + e + 3, it)
                    outer(e // 2, it)
                    lo(d0 + e + 4, it)
                    lo(d0 + e + 5, it)
                    outer(e // 2 + 1, it)

                with dve.Fori(0, KD // 2 - 1) as i:
                    down(0, i)
                down(2 * KD - 4, None)

            ffn(*ffns[0])

            invert(NMA)
            plain(NMA, hp, lambda k: col("mixa", k))
            clear(N2A)
            steps = 0
            for g in range(4):
                w = 2 << g
                u = hp[:, 2 * g:2 * g + 2, :]
                cur = u
                if g == 0:
                    dve.wait_ge(h_raw, RAW0[NMA] + KD)
                for level in range(g + 1):
                    d = 1 << level
                    nxt = (s1, s2)[level % 2]
                    if steps:
                        dve.wait_ge(pool_step, steps)
                    dve.tensor_copy(nxt[:, :, 0:d], cur[:, :, 0:d]).then_inc(pool_step, 1)
                    dve.tensor_tensor(nxt[:, :, d:T], cur[:, :, d:T], cur[:, :, 0:T - d], ALU.add).then_inc(pool_step, 1)
                    steps += 2
                    cur = nxt
                dve.wait_ge(pool_step, steps)
                if g:
                    dve.wait_ge(pool_lo, g)
                dve.scalar_tensor_tensor(out=gf[:, :, :], in0=cur[:, :, :], scalar=1.0 / w, in1=u, op0=ALU.mult, op1=ALU.subtract)\
                   .then_inc(pool_step, 1)
                for j in range(2):
                    dve.tensor_tensor(stat[:, 16 * j:16 * j + w - 1], cur[:, j, 0:w - 1], tab("rcount", w - 1), ALU.mult).then_inc(pool_step, 1)
                dve.wait_ge(pool_step, steps + 3)
                for j in range(2):
                    dve.tensor_tensor(gf[:, j, 0:w - 1], stat[:, 16 * j:16 * j + w - 1], u[:, j, 0:w - 1], ALU.subtract).then_inc(pool_step, 1)
                steps += 5
                assert steps == POOL_STEPS[g]
                dve.wait_ge(pool_hi, g + 1)
                dve.tensor_tensor(hL[:, 2 * g:2 * g + 2, :], gf[:, :, :], hH[:, 2 * g:2 * g + 2, :], ALU.subtract).then_inc(pool_lo, 1)
                lo(POOL + g + 2)
                dve.wait_ge(strip_used, POOL + g + 1)
                for m in (2 * g, 2 * g + 1):
                    dve.scalar_tensor_tensor(out=x[:, m, :], in0=pb[bank(T_POOL + m)][:, :], scalar=col("pool_scale", m), in1=x[:, m, :],
                                             op0=ALU.mult, op1=ALU.add).then_inc(out_taken, 1)
                for m in (2 * g, 2 * g + 1):
                    add(N2A, m)

            for m in range(KD):
                lowered(N2A, m, x, "ffn2a")
            ffn(*ffns[1])
            ffn(*ffns[2])

            for s in range(9):
                lo(M_IN + s + 2)
                if s == 0:
                    invert(NMB)
                    dve.wait_ge(rstd_done, NMB + 1)
                    clear(NQL)
                if s == KQ + 1:
                    invert(NQL)
                dve.wait_ge(strip_used, M_IN + s + 1)
                dve.tensor_tensor(lat[:, s, :], pb[bank(T_MIN + s)][:, :], rstd[:, :], ALU.mult).then_inc(out_taken, 1)
                if s < KQ:
                    add(NQL, s)
                    lowered(NQL, s, lat, "q_norm")
                elif s > KQ:
                    if s == KQ + 1:
                        clear(NKL)
                    add(NKL, s - KQ - 1)
                if s == 5:
                    whole_turn = float(np.float32(6.28125))
                    rest = 2 * np.pi - 6.28125
                    second = float(np.float32(np.floor(rest * 2 ** 20) / 2 ** 20))
                    third = float(np.float32(rest - second))
                    magic = 1.5 * 2.0 ** 23
                    dve.wait_ge(pos_loaded, 16)
                    dve.tensor_copy(posf[:, :], posi[:, :]).then_inc(angle, 1)
                    dve.wait_ge(angle, 1)
                    dve.tensor_scalar(ang[:, :], posf[:, :], tab("inv_freq"), None, ALU.mult).then_inc(angle, 1)
                    dve.wait_ge(angle, 2)
                    dve.tensor_scalar(turns[:, :], ang[:, :], float(1 / (2 * np.pi)), magic, ALU.mult, ALU.add).then_inc(angle, 1)
                    dve.wait_ge(angle, 3)
                    dve.tensor_scalar(turns[:, :], turns[:, :], -magic, None, ALU.add).then_inc(angle, 1)
                    for m, part in enumerate((whole_turn, second, third)):
                        dve.wait_ge(angle, 4 + m)
                        dve.scalar_tensor_tensor(out=ang[:, :], in0=turns[:, :], scalar=-part, in1=ang[:, :], op0=ALU.mult, op1=ALU.add)\
                           .then_inc(angle, 1)
                    dve.wait_ge(angle, 7)
                    pi = float(np.nextafter(np.float32(np.pi), np.float32(0)))
                    dve.tensor_scalar(ang[:, :], ang[:, :], pi, -pi, ALU.min, ALU.max).then_inc(angle, 1)
                    dve.wait_ge(angle, 8)
                    dve.scalar_tensor_tensor(out=turns[:, :], in0=ang[:, :], scalar=-1.0, in1=ang[:, :], op0=ALU.mult, op1=ALU.max)\
                       .then_inc(angle, 1)
                    dve.wait_ge(angle, 9)
                    dve.tensor_scalar(turns[:, :], turns[:, :], -1.0, float(np.float32(np.pi / 2)), ALU.mult, ALU.add).then_inc(angle, 1)

            def head_invert(group):
                dve.wait_ge(hq_std, group + 1)
                dve.reciprocal(head_rstd[group][:, :], head_std[:, :]).then_inc(hq_rstd, 1)

            def head_scale(n):
                dve.wait_ge(spread, n + 1)
                ps = pb[6 + n % 2]
                if n < MH:
                    dve.scalar_tensor_tensor(out=qn[:, n, :], in0=qn[:, n, :], scalar=col("qh_nope"), in1=ps[:, :],
                                             op0=ALU.mult, op1=ALU.mult).then_inc(hq_out, 1)
                elif n < 12:
                    dve.tensor_tensor(qr[:, n - MH, :], qr[:, n - MH, :], ps[:, :], ALU.mult).then_inc(hq_out, 1)
                else:
                    h = n - 12
                    part = slice(64 * (h % 2), 64 * (h % 2) + 64)
                    dve.scalar_tensor_tensor(out=kn[:, h, :], in0=kn[:, h, :], scalar=col("kh_nope"), in1=ps[:, :],
                                             op0=ALU.mult, op1=ALU.mult).then_inc(hq_out, 1)
                    dve.tensor_tensor(kr[part, h, :], krope[part, :], ps[part, :], ALU.mult).then_inc(hq_out, 1)

            for s in range(12):
                lo(M_Q + s + 2)
                if s == 0:
                    dve.wait_ge(rstd_done, NQL + 1)
                    dve.wait_ge(out_taken, T_MIN + 9)
                    dve.tensor_scalar(krope[:, :], lat[:, 8, :], col("kh_rope"), None, ALU.mult).then_inc(gained, 1)
                dve.wait_ge(strip_used, M_Q + s + 1)
                dst = qr[:, s, :] if s < 4 else qn[:, s - 4, :]
                dve.tensor_tensor(dst, pb[bank(T_MQ + s)][:, :], rstd_q[:, :], ALU.mult).then_inc(out_taken, 1)
                if 1 <= s <= 4:
                    dve.wait_ge(hq_sq, s)
                    dve.wait_ge(out_taken, T_MQ + s)
                    dve.tensor_scalar(qr[:, s - 1, :], qr[:, s - 1, :], col("qh_rope"), None, ALU.mult).then_inc(gained, 1)
                if 2 <= s <= 6:
                    r = s - 2
                    dve.wait_ge(sines, 2)
                    rope_finish(r, krope[:, :] if r == 0 else qr[:, r - 1, :], pb[6 + r % 2][:, :], rope2[:, 1, :], rope2[:, 0, :],
                                rope_tmp[:, :], 5 + r, 0)
                if s == 2:
                    invert(NKL)
                if s == 3:
                    norm_low(NKL, lat[:, KQ:KD, :], lambda k: col("kv_norm", k), nH[:, KQ:KD, :], nL[:, KQ:KD, :])
            head_invert(0)
            dve.wait_ge(rope_done, 10)
            lo(M_K + 2)
            for n in range(6):
                head_scale(n)
            lo(M_K + 3)
            head_invert(1)
            for n in range(6, 12):
                head_scale(n)
            lo(M_OUT)
            lo(M_OUT + 1)
            dve.wait_ge(kr_cleared, 1)
            dve.wait_ge(out_taken, T_MV)
            for n in range(12, 20):
                head_scale(n)

            def soft_max(u):
                h, b = divmod(u, NB)
                w = (b + 1) * P
                m2 = stat[:, 32 + u % 4:33 + u % 4]
                dve.wait_ge(scored, 32 + u + 1)
                if u >= 4:
                    dve.wait_ge(p_turned, 32 + u - 3)
                else:
                    dve.wait_ge(mask_loaded, 16)
                dve.tensor_tensor_reduce(prob2[:, u % 4, 0:w], pb[S2[u % 4]][:, 0:w], cmask[:, T - w:T], 1.0, -3e38,
                                         ALU.add, ALU.max, m2).then_inc(masked, 1)
                dve.wait_ge(masked, 32 + u + 1)
                dve.tensor_scalar(stat[:, 16 + u % 4:17 + u % 4], m2, -SCALE2, None, ALU.mult).then_inc(bias_ready, 1)

            for u in range(MH * NB + LAG + 3):
                if u < MH * NB:
                    soft_max(u)
                if 1 <= u <= MH * NB:
                    scale_probs(32 + u - 1, prob2[:, (u - 1) % 4, 0:((u - 1) % NB + 1) * P])
                if head_at(u - LAG - 3) is not None:
                    h = head_at(u - LAG - 3)
                    dve.wait_ge(att_hi, NB + h + 1)
                    dve.tensor_tensor(oL[:, h, :], pb[4 + h % 2][:, :], oH[:, h, :], ALU.subtract).then_inc(att_lo, 1)

            residual(M_OUT, T_MOUT, N2B, lambda m: ones[:, 0:1], "ffn2b")
            ffn(*ffns[3])


def kernel(**inputs):
    import numpy as _np
    import concourse.bacc as _bacc
    from concourse import mybir as _mybir
    from concourse.bass_utils import run_bass_kernel_spmd as _run

    a = {k: _np.asarray(v) for k, v in inputs.items()}

    def features(v):
        return v.reshape(-1, P).T

    def tokens(v):
        n, d = v.shape
        return v.T.reshape(d // P, P, n).transpose(1, 0, 2).reshape(P, -1)

    def strips(w, per=1, halves=1):
        k, m = w.shape
        w = w.reshape(halves, k // P // halves, P, m // P // per, per, P)
        return w.transpose(3, 0, 2, 4, 1, 5).reshape(m // P // per * halves, P, -1)

    heads = _np.arange(H * HD).reshape(H, HD)
    paired = _np.concatenate([_np.concatenate([heads[i], heads[i + 4]]) for i in range(4)])
    att, kv = H * HD, 2 * HD
    cw = D - att
    cols_in = [_np.arange(att, att + kv), _np.arange(att + kv, att + 2 * kv), paired]
    c0 = att + 2 * kv
    for i in range(4):
        for part in (1, 2, 0):
            cols_in.append(c0 + part * cw + _np.arange(i * P, (i + 1) * P))
    cols_in = _np.concatenate(cols_in)
    rows_out = _np.concatenate([paired, _np.arange(att, D)])
    qcols = _np.arange(MH * (NOPE + ROPE)).reshape(MH, NOPE + ROPE)
    qcols = _np.concatenate([qcols[:, NOPE:].ravel(), qcols[:, :NOPE].ravel()])
    kvcols = _np.arange(MH * 2 * NOPE).reshape(MH, 2 * NOPE)
    lat_cols = _np.concatenate([_np.arange(D + ROPE), _np.arange(D, D + ROPE)])
    kv_up = a["mla_w_kv_up_2"][0]
    wv = kv_up[:, kvcols[:, NOPE:].ravel()].reshape(2, P, 2, 512).transpose(2, 1, 0, 3).reshape(2, P, 1024)

    by_tile = [a[n][0].reshape(PAIRS, 2, 8, P, 1024).transpose(0, 2, 3, 1, 4) for n in ("w_gate", "w_up", "w_down")]
    experts = _np.concatenate([_np.stack(by_tile[:2], 2).reshape(PAIRS, 16, P, 2, 1024), by_tile[2]], 1)

    vec = {
        "c": features(a["c"][0]), "cctx": features(a["c_ctx"]), "b_ada": features(a["b_ada"][0]),
        "g_mix": features(a["g_mix"][0]), "g_ffn": features(a["g_ffn"][0]),
        "conv_w": a["conv_w"][0].reshape(3, 4, P).transpose(2, 1, 0).reshape(P, 12),
        "sink": _np.broadcast_to(a["sink"][0][None], (P, H)),
        "ffn1a": features(a["ffn1_norm_2"][0]), "ffn1b": features(a["ffn1_norm_2"][1]),
        "ffn2a": features(a["ffn2_norm_2"][0]), "ffn2b": features(a["ffn2_norm_2"][1]),
        "mixa": features(a["mix_norm_2"][0]), "mixb": features(a["mix_norm_2"][1]),
        "pool_scale": features(a["pool_scale_2"][0]), "q_norm": features(a["mla_q_norm_2"][0]),
        "kv_norm": features(a["mla_kv_norm_2"][0]),
        "qh_nope": a["mla_q_head_norm_2"][0][:NOPE, None], "qh_rope": _np.tile(a["mla_q_head_norm_2"][0][NOPE:], 2)[:, None],
        "kh_nope": a["mla_k_head_norm_2"][0][:NOPE, None], "kh_rope": _np.tile(a["mla_k_head_norm_2"][0][NOPE:], 2)[:, None],
        "g_final": features(a["g_final"]),
    }
    tabs, window, causal, rope, select = shape_tables()
    arrays = {
        "cols": _np.concatenate([vec[n] for n, _ in _names], 1),
        "tabs": tabs, "window": window, "causal": causal, "select": select, "rope": rope,
        "positions": _np.broadcast_to(a["positions_2"], (P, T)),
        "ctx": tokens(a["ctx"][0]), "x": tokens(a["x"][0]),
        "w_ada": a["w_ada"][0],
        "w_in": strips(a["w_in"][0][:, cols_in]),
        "w_out": strips(a["w_out"][0][rows_out]),
        "w_router": a["w_router"][0].reshape(KD, P, E).transpose(1, 0, 2).reshape(P, -1),
        "experts": experts.reshape(PAIRS, 24, P, 2 * 1024),
        "pool_w": _np.stack([strips(a["pool_w_2"][0][g], per=2)[0] for g in range(4)]),
        "mla_in": strips(a["mla_w_in_2"][0][:, lat_cols]),
        "q_up": strips(a["mla_w_q_up_2"][0][:, qcols]),
        "kv_up": _np.concatenate([strips(kv_up[:, kvcols[:, :NOPE].ravel()], per=4), wv]),
        "mla_out": strips(a["mla_w_out_2"][0]),
    }
    for f in range(4):
        n, layer = ("ffn1", "ffn2")[f % 2], f // 2
        arrays[f"gate{f}"] = strips(a[f"{n}_w_gate_2"][layer])
        arrays[f"up{f}"] = strips(a[f"{n}_w_up_2"][layer])
        arrays[f"down{f}"] = strips(a[f"{n}_w_down_2"][layer], halves=2)

    nc = _bacc.Bacc("TRN2", target_bir_lowering=False, num_devices=1)
    given, handles = {}, {}
    for name, v in arrays.items():
        v = _np.ascontiguousarray(v)
        given[f"in_{name}"] = v
        handles[name] = nc.dram_tensor(f"in_{name}", v.shape, _mybir.dt.from_np(v.dtype), kind="ExternalInput").ap()
    for name in ("gate", "up", "down"):
        handles[name] = [handles[f"{name}{f}"] for f in range(4)]
    out = nc.dram_tensor("out", (P, KD * T), _mybir.dt.float32, kind="ExternalOutput").ap()
    build(nc, handles, out)
    r = _run(nc, [given], core_ids=[0])
    got = r.results[0]["out"].reshape(P, KD, T).transpose(2, 1, 0).reshape(1, T, D)
    return _np.ascontiguousarray(got)
```

```python
from contextlib import ExitStack

import numpy as np

import concourse.bass as bass
from concourse import mybir

F32 = mybir.dt.float32
F32R = mybir.dt.float32r
I32 = mybir.dt.int32
ALU = mybir.AluOpType
ACT = mybir.ActivationFunctionType
AX_X = mybir.AxisListType.X

P = 128
T = 512
C = 256
D = 1024
KD = D // P
H, HD = 8, 64
NB = T // P
E, SLOTS = 16, 64
PAIRS = E // 2
F2 = 2816
KF = F2 // P
HALF_KF = KF // 2
MH, NOPE, ROPE = 8, 128, 64
KQ, KKV = 6, 2
EPS = 1e-6
MASKED = -1e30
STAGE = 4
WIDE = HALF_KF * P
RING = 12

_names = [("c", KD), ("cctx", KD), ("b_ada", 48), ("g_mix", KD), ("g_ffn", KD), ("conv_w", 12), ("sink", H),
          ("ffn1a", KD), ("ffn2a", KD), ("ffn1b", KD), ("ffn2b", KD), ("mixa", KD), ("mixb", KD),
          ("pool_scale", KD), ("q_norm", KQ), ("kv_norm", KKV), ("qh_nope", 1), ("qh_rope", 1),
          ("kh_nope", 1), ("kh_rope", 1), ("g_final", KD)]
COL, NCOLS = {}, 0
for _n, _k in _names:
    COL[_n] = (NCOLS, _k)
    NCOLS += _k

_tables = [("ident", P), ("turn", P), ("lower", H), ("one_row", 15), ("two_rows", 14), ("slot", SLOTS), ("inv_freq", 1), ("rcount", 15)]
TAB, NTAB = {}, 0
for _n, _k in _tables:
    TAB[_n] = (NTAB, _k)
    NTAB += _k


def shape_tables():
    t = np.zeros((P, NTAB), np.float32)

    def put(name, v):
        t[:, TAB[name][0]:TAB[name][0] + TAB[name][1]] = v

    put("ident", np.eye(P))
    turn = np.zeros((P, P), np.float32)
    for g in range(0, P, 64):
        for d in range(32):
            turn[g + 32 + d, g + d] = -1.0
            turn[g + d, g + 32 + d] = 1.0
    put("turn", turn)
    put("lower", np.repeat((np.arange(P) < 64)[:, None], H, 1))
    one, two = np.zeros((P, 15), np.float32), np.zeros((P, 14), np.float32)
    one[:, 7] = 1
    two[:64, 6], two[64:, 7] = 1, 1
    put("one_row", one)
    put("two_rows", two)
    put("slot", np.arange(1, SLOTS + 1))
    inv = (np.float32(1) / np.power(np.float32(10000), np.arange(0, 64, 2, dtype=np.float32) / np.float32(64))).astype(np.float32)
    bits = inv.view(np.int32).copy()
    bits[[5, 27]] -= 2
    put("inv_freq", np.tile(bits.view(np.float32), 4)[:, None])
    put("rcount", 1.0 / np.arange(1, 16, dtype=np.float32))
    i, j = np.arange(P)[:, None], np.arange(P)[None, :]
    zero = np.zeros((P, P), np.float32)
    window = np.concatenate([np.where(j >= i, 0, MASKED), zero, np.where(j <= i, 0, MASKED)], 1).astype(np.float32)
    causal = np.concatenate([zero, zero, zero, np.where(j <= i, 0, MASKED)], 1).astype(np.float32)
    inv16 = (np.float32(10000.0) ** (-np.arange(16, dtype=np.float32) / np.float32(16))).astype(np.float32)
    tok = np.arange(T)
    ang = np.concatenate([(tok // 64).astype(np.float32)[:, None] * inv16, (tok % 64).astype(np.float32)[:, None] * inv16], -1)
    rope = np.concatenate([np.tile(np.cos(ang).T, (4, 1)), np.tile(np.sin(ang).T, (4, 1))], 1).astype(np.float32)
    select = np.zeros((MH, MH + MH // 2, P), np.float32)
    for h in range(MH):
        select[h, h] = 1
        select[h, MH + h // 2, 64 * (h % 2):64 * (h % 2) + 64] = 1
    return t, window, causal, rope, select.reshape(MH, -1)


def build(nc, A, out):
    st = ExitStack()
    with st:
        def sem(name):
            return st.enter_context(nc.semaphore(name))

        base = 16512

        def place(name, shape, dt, at):
            return nc.alloc_sbuf_tensor_at(name, shape, dt, offset=base + at)

        def up(n):
            return (n + 31) // 32 * 32

        KB = 1024
        TILE = T * 4
        X0, HH, HL, G = 0, 16 * KB, 32 * KB, 48 * KB
        ST = G + KF * 2 * TILE
        WH = ST + STAGE * WIDE * 4
        WL = WH + 2 * WIDE * 4
        TM = WL + 2 * WIDE * 4
        CO = TM + 11 * TILE
        x = place("x", [P, KD, T], F32, X0)
        hH = place("hH", [P, KD, T], F32R, HH)
        hL = place("hL", [P, KD, T], F32R, HL)
        stage = place("stage", [P, STAGE, WIDE], F32, ST)
        wH = place("wH", [P, 2, WIDE], F32R, WH)
        wL = place("wL", [P, 2, WIDE], F32R, WL)
        std = place("std", [P, T], F32, TM)
        rstd = place("rstd", [P, T], F32, TM + TILE)
        ssq = place("ssq", [P, T], F32, TM + 2 * TILE)
        sq = place("sq", [P, 2, T], F32, TM + 3 * TILE)
        hraw = place("hraw", [P, 2, T], F32, TM + 5 * TILE)
        sg = place("sg", [P, 2, T], F32, TM + 7 * TILE)
        gf = place("gf", [P, 2, T], F32, TM + 9 * TILE)
        cols = place("cols", [P, NCOLS], F32, CO)
        tabs = place("tabs", [P, NTAB], F32, CO + up(NCOLS * 4))
        c2 = CO + up(NCOLS * 4) + up(NTAB * 4)
        ones = place("ones", [P, P], F32, c2)
        eps = place("eps", [P, 1], F32, c2 + 512)
        mod = place("mod", [P, 64], F32, c2 + 544)
        gain1 = place("gain1", [P, 3 * KD], F32, c2 + 544 + 256)
        stat = place("stat", [P, 64], F32, c2 + 544 + 256 + 96)
        assert base + c2 + 544 + 256 + 96 + 256 <= 229368, base + c2 + 1152

        ctx = place("ctx", [P, KD, C], F32, G)
        cH = place("cH", [P, KD, C], F32R, G + 8 * KB)
        cL = place("cL", [P, KD, C], F32R, G + 16 * KB)
        PT = place("PT", [P, 2, 5, T], F32, G)
        adaw = place("adaw", [P, 4, 1024], F32, G + 24 * KB)
        prob = place("prob", [P, 4, 648], F32, G + 24 * KB)
        acc = place("acc", [P, 2, 1024], F32, G + 40 * KB)
        mod_row = place("mod_row", [2, 2048], F32, G + 48 * KB)
        qT = place("qT", [P, 4, T], F32, G + 56 * KB)
        kT = place("kT", [P, T + C], F32, G + 64 * KB)
        vT = place("vT", [P, T + C], F32, G + 67 * KB)
        V = place("V", [P, 6, P], F32, G + 70 * KB)
        conv = place("conv", [P, 4, T], F32, G + 73 * KB)
        rope = place("rope", [P, 2, T], F32, G + 81 * KB)
        window = place("window", [P, 3 * P], F32, G + 85 * KB)
        catH, catL = hH, hL
        ring = place("ring", [P, 2 * RING, 1024], F32, G + 24 * KB)
        h2 = place("h2", [P, KD, T], F32, HH)
        h2t = place("h2t", [P, NB, D], F32, HL)
        pos = place("pos", [E, T], F32, G)
        afT = place("afT", [E, T], F32, G + 2 * KB)
        work = place("work", [E, 2, T], F32, G + 4 * KB)
        xs = place("xs", [P, D], F32, G)
        xsT = place("xsT", [P, KD, P], F32, G + 4 * KB)
        sil = place("sil", [P, 1024], F32, G + 8 * KB)
        hid = place("hid", [P, 1024], F32, G + 12 * KB)
        hidT = place("hidT", [P, 8, P], F32, G + 16 * KB)
        pick = place("pick", [P, NB, P], F32, G + 20 * KB)
        pickg = place("pickg", [P, NB, P], F32, G + 22 * KB)
        pickgT = place("pickgT", [P, T], F32, TM + 9 * TILE)
        af = place("af", [P, NB, E], F32, TM + 4 * TILE)
        posT = place("posT", [P, NB, E], F32, TM + 4 * TILE + 256)
        top = place("top", [E, 8, 8], F32, TM + 4 * TILE + 512)
        wr = place("wr", [P, KD, E], F32, TM + 7 * TILE)
        gH = place("gH", [P, KF, T], F32R, G)
        gL = place("gL", [P, KF, T], F32R, G + KF * TILE)
        s1 = place("s1", [P, 2, T], F32, G)
        s2 = place("s2", [P, 2, T], F32, G + 2 * TILE)
        hp = place("hp", [P, KD, T], F32, G + 4 * TILE)
        wide = {g: [place(f"wide{g}{i}", [P, 2, T], F32, G + (12 + 4 * (g - 2) + 2 * i) * TILE) for i in range(2)] for g in (2, 3)}
        lat = place("lat", [P, 9, T], F32, G)
        kr = place("kr", [P, MH, T], F32, G)
        nH = place("nH", [P, KD, T], F32R, G + 18 * KB)
        nL = place("nL", [P, KD, T], F32R, G + 34 * KB)
        oH, oL = nH, nL
        qn = place("qn", [P, MH, T], F32, G + 50 * KB)
        qr = place("qr", [P, 4, T], F32, G + 66 * KB)
        pT2 = [place("pT2a", [P, NB, T], F32, G + 74 * KB), place("pT2b", [P, NB, T], F32, TM)]
        select = place("select", [MH, MH + MH // 2, P], F32, TM + 7 * TILE)
        rstd_q = place("rstd_q", [P, T], F32, TM + 10 * TILE)
        head_std = place("head_std", [MH, T], F32, TM)
        head_rstd = [place("head_rstd_q", [MH, T], F32, TM + TILE), place("head_rstd_k", [MH, T], F32, TM + 2 * TILE)]
        rope_tmp = place("rope_tmp", [P, T], F32, G + 78 * KB)
        rope2 = place("rope2", [P, 2, T], F32, G + 82 * KB)
        krope = place("krope", [P, T], F32, G + 86 * KB)
        kn = place("kn", [P, MH, T], F32, HH)
        V2 = place("V2", [P, NB, D], F32, HL)
        prob2 = place("prob2", [P, 4, T], F32, TM + 7 * TILE)
        cmask = place("cmask", [P, T], F32, TM + 6 * TILE)
        posi = place("posi", [P, T], I32, G + 74 * KB)
        posf = place("posf", [P, T], F32, G + 76 * KB)
        ang = place("ang", [P, T], F32, G + 78 * KB)
        turns = place("turns", [P, T], F32, G + 80 * KB)

        pb = [st.enter_context(nc.psum_tensor(f"pb{i}", [P, 512], F32)) for i in range(8)]

        def col(name, k=0):
            return cols[:, COL[name][0] + k:COL[name][0] + k + 1]

        def tab(name, n=None):
            a, k = TAB[name]
            return tabs[:, a:a + (n or k)]


        cols_loaded = sem("cols_loaded")
        small_loaded, x_loaded, ctx_loaded = sem("small_loaded"), sem("x_loaded"), sem("ctx_loaded")
        ones_set = sem("ones_set")
        ada_landed = [sem(f"ada_landed{i}") for i in range(4)]
        cond_ready, ada_used, ada_added = sem("cond_ready"), sem("ada_used"), sem("ada_added")
        mod_rowed = sem("mod_rowed")
        mod_summed, mod_ready, gain_ready = sem("mod_summed"), sem("mod_ready"), sem("gain_ready")
        strip_landed = [sem(f"strip_landed{i}") for i in range(STAGE)]
        strip_hi, strip_lo, strip_used = sem("strip_hi"), sem("strip_lo"), sem("strip_used")
        out_taken = sem("out_taken")
        sq_done, ssq_done, norm_summed = sem("sq_done"), sem("ssq_done"), sem("norm_summed")
        std_done, rstd_done = sem("std_done"), sem("rstd_done")
        x_normed, rstd_both = sem("x_normed"), sem("rstd_both")
        h_raw, h_hi, h_lo = sem("h_raw"), sem("h_hi"), sem("h_lo")
        gate_ready, g_raw = sem("gate_ready"), sem("g_raw")
        silu_done, g_hi, g_lo = sem("silu_done"), sem("g_hi"), sem("g_lo")
        turned, rope_part, rope_done = sem("turned"), sem("rope_part"), sem("rope_done")
        v_turned, v_ready, conv_part = sem("v_turned"), sem("v_ready"), sem("conv_part")
        cat_hi, cat_lo = sem("cat_hi"), sem("cat_lo")
        scored, row_max, masked, bias_ready = sem("scored"), sem("row_max"), sem("masked"), sem("bias_ready")
        ctx_copied, exp_done, inv_ready, p_ready = sem("ctx_copied"), sem("exp_done"), sem("inv_ready"), sem("p_ready")
        p_turned, pt_act, pt_dve, pv_done = sem("p_turned"), sem("pt_act"), sem("pt_dve"), sem("pv_done")
        att_hi, att_lo = sem("att_hi"), sem("att_lo")
        logits_summed, logits_copied = sem("logits_summed"), sem("logits_copied")
        wr_loaded, logits_done, lmax, aff_exp, aff_ready = sem("wr_loaded"), sem("logits_done"), sem("lmax"), sem("aff_exp"), sem("aff_ready")
        aff_turned, top_step, pos_turned, posT_ready = sem("aff_turned"), sem("top_step"), sem("pos_turned"), sem("posT_ready")
        h2_turned, h2t_ready = sem("h2_turned"), sem("h2t_ready")
        exp_landed = [sem(f"exp_landed{i}") for i in range(RING)]
        exp_used = sem("exp_used")
        pick_ready, pickg_ready, pg_turned, pgT_ready = sem("pick_ready"), sem("pickg_ready"), sem("pg_turned"), sem("pgT_ready")
        gathered, xs_act, xs_dve, xs_turned = sem("gathered"), sem("xs_act"), sem("xs_dve"), sem("xs_turned")
        xsT_act, xsT_dve, sil_done, hid_done = sem("xsT_act"), sem("xsT_dve"), sem("sil_done"), sem("hid_done")
        hid_turned, hidT_act, hidT_dve = sem("hid_turned"), sem("hidT_act"), sem("hidT_dve")
        y_act, y_dve, scattered, x_added = sem("y_act"), sem("y_dve"), sem("scattered"), sem("x_added")
        pool_step, wide_step, x_pooled = sem("pool_step"), sem("wide_step"), sem("x_pooled")
        pos_loaded, mask_loaded, angle, sines = sem("pos_loaded"), sem("mask_loaded"), sem("angle"), sem("sines")
        hq_sq, hq_summed, hq_std, hq_rstd, hq_out = sem("hq_sq"), sem("hq_summed"), sem("hq_std"), sem("hq_rstd"), sem("hq_out")
        kr_cleared, gained, select_loaded, spread = sem("kr_cleared"), sem("gained"), sem("select_loaded"), sem("spread")
        out_stored = sem("out_stored")

        W_IN, W_OUT, FFN1A = 0, 18, 26
        NFFN = 2 * KF + 2 * KD
        POOL = FFN1A + NFFN
        FFN2A = POOL + 4
        FFN1B = FFN2A + NFFN
        M_IN = FFN1B + NFFN
        M_Q = M_IN + 9
        M_K = M_Q + 12
        M_V = M_K + 2
        M_OUT = M_V + 2
        FFN2B = M_OUT + KD
        N_STRIPS = FFN2B + NFFN
        width = [KD * P] * FFN1A
        ffn_width = [KD * P] * (2 * KF) + [WIDE] * (2 * KD)
        width += ffn_width + [4 * P] * 4 + ffn_width + ffn_width
        width += [KD * P] * 9 + [KQ * P] * 12 + [KD * P] * 4 + [KD * P] * KD + ffn_width
        assert len(width) == N_STRIPS
        T_OUT, T_FFN1A = 18, 26
        T_POOL = T_FFN1A + KF + KD
        T_FFN2A = T_POOL + KD
        T_FFN1B = T_FFN2A + KF + KD
        T_MIN = T_FFN1B + KF + KD
        T_MQ = T_MIN + 9
        T_MK = T_MQ + 12
        T_MV = T_MK + 8
        T_MOUT = T_MV + 8
        T_FFN2B = T_MOUT + KD
        NX, NCTX, NH2, NFIN, N1A, NMA, N2A, N1B, NMB, NQL, NKL, N2B = range(12)
        KT = [KD] * 9 + [KQ, KKV, KD]
        WID = [T, C] + [T] * 10
        SQ0 = [sum(KT[:q]) for q in range(12)]
        SS0 = [sum(KT[:q]) + q for q in range(12)]
        IS_SPLIT = [q not in (NH2, N1A) for q in range(12)]
        FOLDED = [q in (NFIN, N1A, NMA, N2A, N1B, NMB, NQL, N2B) for q in range(12)]
        RAW0 = [sum(k for r, k in enumerate(KT[:q]) if not FOLDED[r]) for q in range(12)]
        HI0 = [sum(k for r, k in enumerate(KT[:q]) if r != N1A) for q in range(12)]
        LO0 = [sum(k for r, k in enumerate(KT[:q]) if IS_SPLIT[r]) for q in range(12)]
        SCALE1 = float(HD) ** -0.5
        SCALE2 = float(NOPE + ROPE) ** -0.5
        UNITS = [(n, a, j) for n in range(NB) for a in range(4) for j in range(2)]

        def keys(n):
            return max(0, n - 1) * P, min(NB, n + 2) * P

        def block_at(u):
            return u // 8 if 0 <= u < len(UNITS) and u % 8 == 7 else None

        GAIN = {N1A: "ffn1a", NMA: "mixa", N2A: "ffn2a", N1B: "ffn1b", NMB: "mixb", N2B: "ffn2b"}

        OUTS = [n if n <= 12 else 12 + 2 * (n - 12) for n in range(21)]

        def head_at(u):
            return u // NB if 0 <= u < MH * NB and u % NB == NB - 1 else None

        def count(it, before, per, n):
            return before * per + n if it is None else it * per + (before * per + n)

        def bank(tile):
            return 2 * (tile % 2)

        def shifted(n, it, by=4):
            return n if it is None else it * by + n

        S2 = (0, 1, 6, 7)
        LAG1, LAG = 2, 3
        POOL_BANKS = (0, 1, 2, 3, 4, 5, 7, 0)
        POOL_ORDER = (3, 2, 0, 1)
        ROT_AT = {1: 0, 3: 1, 4: 2, 5: 3, 6: 4}

        def b_units(u):
            return min(max(u - 8, 0), 16)

        rstd_of = [rstd[:, :]] * 12
        rstd_of[NCTX] = sg[:, 0, :]
        rstd_of[NQL] = rstd_q[:, :]
        rstd_of[NFIN] = sg[:, 0, :]
        both_gains = stat[:, 56:64]
        kv_tiles = {n: [4, 5] + list(range(keys(n)[0] // P, keys(n)[1] // P)) for n in range(NB)}
        ffns = [(FFN1A, T_FFN1A, 0, N1A), (FFN2A, T_FFN2A, 1, N2A), (FFN1B, T_FFN1B, 2, N1B), (FFN2B, T_FFN2B, 3, N2B)]

        block = st.enter_context(nc.Block())

        @block.sync
        def _(sp):
            sp.dma_start(cols[:, :], A["cols"]).then_inc(cols_loaded, 16)

            def ada(a):
                if 4 <= a < 20:
                    sp.wait_ge(ada_used, a - 3)
                elif a >= 20:
                    sp.wait_ge(ada_added, a - 19)
                k, b = (a // 2, a % 2) if a < 16 else (a % 8, a // 8)
                sp.dma_start(adaw[:, a % 4, :], A["w_ada"][k * P:k * P + P, b * 1024:b * 1024 + 1024])\
                  .then_inc(ada_landed[a % 4], 16)

            def strip(n, src, it=None):
                if n >= STAGE:
                    sp.wait_ge(strip_lo, shifted(n - STAGE + 1, it))
                sp.dma_start(stage[:, n % STAGE, 0:width[n]], src).then_inc(strip_landed[n % STAGE], 16)

            def ffn_tiles(n0, f, it):
                for j in range(2):
                    g = j if it is None else it * 2 + j
                    strip(n0 + 2 * j, A["gate"][f][g], it)
                    strip(n0 + 2 * j + 1, A["up"][f][g], it)

            def ffn(n0, f, start=0):
                down = A["down"][f]
                with sp.Fori(start, KF // 2) as i:
                    ffn_tiles(n0, f, i)
                d0 = n0 + 2 * KF
                with sp.Fori(0, KD // 2) as i:
                    for j in range(4):
                        strip(d0 + j, down[i * 4 + j], i)

            for a in range(16):
                ada(a)
                if a == 3:
                    sp.dma_start(x[:, :, :], A["x"].rearrange("p (k t) -> p k t", k=KD)).then_inc(x_loaded, 16)
                    sp.dma_start(tabs[:, :], A["tabs"]).then_inc(small_loaded, 16)
                if a == 7:
                    strip(W_IN, A["w_in"][0])
                    strip(W_IN + 1, A["w_in"][1])
                if a == 9:
                    sp.dma_start(ctx[:, :, :], A["ctx"].rearrange("p (k t) -> p k t", k=KD)).then_inc(ctx_loaded, 16)
            sp.dma_start(rope[:, :, :], A["rope"].rearrange("p (k t) -> p k t", k=2)).then_inc(small_loaded, 16)
            sp.dma_start(window[:, :], A["window"]).then_inc(small_loaded, 16)
            for n in range(18):
                if n >= 2:
                    strip(W_IN + n, A["w_in"][n])
                if n < 16:
                    ada(16 + 2 * n)
                    ada(17 + 2 * n)
            for n in range(8):
                strip(W_OUT + n, A["w_out"][n])
                if n == 3:
                    sp.wait_ge(rope_done, 5)
                    sp.wait_ge(cat_lo, 4)
                    sp.dma_start(wr[:, :, :], A["w_router"].rearrange("p (k e) -> p k e", k=KD)).then_inc(wr_loaded, 16)

            def experts(d, it):
                w = 2 * (d % RING)
                sp.dma_start(ring[:, w:w + 2, :], A["experts"][it, d].rearrange("p (e f) -> p e f", e=2)).then_inc(exp_landed[d % RING], 16)

            sp.wait_ge(pv_done, NB)
            sp.wait_ge(pt_act, 32)
            sp.wait_ge(att_lo, NB)
            sp.wait_ge(cat_lo, 4)
            for d in range(8):
                experts(d, 0)
            sp.wait_ge(strip_lo, FFN1A)
            sp.wait_ge(strip_used, FFN1A)
            for d in range(8, RING):
                experts(d, 0)
            with sp.Fori(0, PAIRS - 1) as i:
                for d in range(24):
                    sp.wait_ge(exp_used, i * 24 + (d + 1))
                    experts((d + RING) % 24, i + (d + RING) // 24)
            for d in range(24 - RING):
                sp.wait_ge(exp_used, (PAIRS - 1) * 24 + d + 1)
                experts(d + RING, PAIRS - 1)
            sp.wait_ge(exp_used, PAIRS * 24)
            ffn_tiles(FFN1A, 0, None)
            ffn(FFN1A, 0, start=1)
            for n in range(4):
                strip(POOL + n, A["pool_w"][n])
            ffn(FFN2A, 1)
            ffn(FFN1B, 2)
            for n in range(9):
                strip(M_IN + n, A["mla_in"][n])
            sp.wait_ge(strip_used, M_IN)
            sp.dma_start(posi[:, :], A["positions"]).then_inc(pos_loaded, 16)
            sp.dma_start(select[:, :, :], A["select"].rearrange("h (k p) -> h k p", p=P)).then_inc(select_loaded, 16)
            for n in range(12):
                strip(M_Q + n, A["q_up"][n])
            for n in range(4):
                strip(M_K + n, A["kv_up"][n])
            sp.wait_ge(h_lo, LO0[N2B])
            sp.dma_start(cmask[:, :], A["causal"]).then_inc(mask_loaded, 16)
            for n in range(8):
                strip(M_OUT + n, A["mla_out"][n])
            ffn(FFN2B, 3)
            for m in range(KD):
                sp.wait_ge(out_taken, T_FFN2B + KF + m + 1)
                sp.dma_start(out[:, m * T:(m + 1) * T], x[:, m, :]).then_inc(out_stored, 16)
            sp.wait_ge(out_stored, 16 * KD)

        @block.gpsimd
        def _(pool):
            pool.memset(ones[:, :], 1.0).then_inc(ones_set, 1)
            pool.memset(eps[:, :], EPS).then_inc(ones_set, 1)

            def squares(q):
                for k in range(KD):
                    pool.wait_ge(sq_done, SQ0[q] + k + 1)
                    pool.wait_ge(ssq_done, SS0[q] + k + 1)
                    pool.tensor_tensor(ssq[:, :], ssq[:, :], sq[:, (SQ0[q] + k) % 2, :], ALU.add).then_inc(ssq_done, 1)

            squares(NFIN)
            squares(N1A)
            steps = 0
            for n, g in enumerate(POOL_ORDER[:2]):
                pool.wait_ge(out_taken, T_POOL + 2 * n + 2)
                cur = hp[:, 2 * g:2 * g + 2, :]
                for level in range(g + 1):
                    d, nxt = 1 << level, wide[g][level % 2]
                    if level:
                        pool.wait_ge(wide_step, steps)
                    pool.tensor_copy(nxt[:, :, 0:d], cur[:, :, 0:d]).then_inc(wide_step, 1)
                    pool.tensor_tensor(nxt[:, :, d:T], cur[:, :, d:T], cur[:, :, 0:T - d], ALU.add).then_inc(wide_step, 1)
                    steps += 2
                    cur = nxt
            squares(N2A)
            pool.wait_ge(h_lo, LO0[N2B])
            pool.wait_ge(sq_done, SQ0[N2B])
            pool.memset(kr[:, :, :], 0.0).then_inc(kr_cleared, 1)

        @block.scalar
        def _(act):
            def hi(n, it=None):
                if n >= N_STRIPS:
                    return
                landed = 16 * (n // STAGE + 1)
                act.wait_ge(strip_landed[n % STAGE], shifted(landed, it, 16))
                if n >= 2:
                    act.wait_ge(strip_used, shifted(n - 1, it))
                act.activation(wH[:, n % 2, 0:width[n]], stage[:, n % STAGE, 0:width[n]], ACT.Copy).then_inc(strip_hi, 1)

            def square(q, k, src):
                if SS0[q] + k >= 2:
                    act.wait_ge(ssq_done, SS0[q] + (k if k >= 2 else 0))
                act.activation(sq[:, (SQ0[q] + k) % 2, 0:WID[q]], src, ACT.Square).then_inc(sq_done, 1)

            def root(q, features):
                act.wait_ge(norm_summed, q + 1)
                act.wait_ge(ones_set, 2)
                if q:
                    act.wait_ge(rstd_done, q)
                act.activation(std[:, 0:WID[q]], pb[6][:, 0:WID[q]], ACT.Sqrt, bias=eps[:, 0:1], scale=1.0 / features)\
                   .then_inc(std_done, 1)

            def norm_hi(q, dst, shift=None):
                for k in range(KT[q]):
                    act.wait_ge(h_raw, RAW0[q] + k + 1)
                    src = hraw[:, (RAW0[q] + k) % 2, 0:WID[q]]
                    if shift is None:
                        ins = act.activation(dst[:, k, :], src, ACT.Copy)
                    else:
                        ins = act.activation(dst[:, k, :], src, ACT.Identity, bias=mod[:, shift + k:shift + k + 1])
                    ins.then_inc(h_hi, 1)

            def prepare(q, k, src, gain, it=None):
                g = k if it is None else it * 2 + k
                act.wait_ge(ssq_done, shifted(SS0[q] + k, it, 2) if k or it is not None else SS0[q])
                act.activation(sq[:, (SQ0[q] + k) % 2, :], src[:, g, :], ACT.Square).then_inc(sq_done, 1)
                a = COL[gain][0]
                scale = cols[:, a + k:a + k + 1] if it is None else cols[:, bass.ds(it * 2 + (a + k), 1)]
                dst = (nH if q == NQL else hH)[:, g, :]
                act.activation(dst, src[:, g, :], ACT.Copy, scale=scale).then_inc(h_hi, 1)

            def ffn(n0, t0, f, q):
                def inner(tile, it):
                    act.wait_ge(gate_ready, shifted(f * KF + tile + 1, it, 2))
                    act.activation(sg[:, tile % 2, :], hraw[:, tile % 2, :], ACT.Silu).then_inc(silu_done, 1)
                    act.wait_ge(g_raw, shifted(f * KF + tile + 1, it, 2))
                    dst = gH[:, tile, :] if it is None else gH[:, it * 2 + tile, :]
                    act.activation(dst, gf[:, tile % 2, :], ACT.Copy).then_inc(g_hi, 1)

                def tiles(e, it):
                    hi(n0 + e + 2, it)
                    hi(n0 + e + 3, it)
                    inner(e // 2, it)
                    hi(n0 + e + 4, it)
                    hi(n0 + e + 5, it)
                    inner(e // 2 + 1, it)

                def first_tiles():
                    hi(n0 + 4)
                    hi(n0 + 5)
                    inner(0, None)
                    inner(1, None)

                root(q, D)
                if f == 0:
                    first_tiles()
                with act.Fori(1 if f == 0 else 0, KF // 2 - 1) as i:
                    tiles(0, i)
                tiles(2 * KF - 4, None)
                d0, q1 = n0 + 2 * KF, q + 1

                def added(m, it):
                    act.wait_ge(out_taken, shifted(t0 + KF + m + 1, it, 2))
                    if FOLDED[q1]:
                        prepare(q1, m, x, GAIN[q1], it)
                    else:
                        act.wait_ge(ssq_done, shifted(SS0[q1] + m, it, 2) if m or it is not None else SS0[q1])
                        src = x[:, m, :] if it is None else x[:, it * 2 + m, :]
                        act.activation(sq[:, (SQ0[q1] + m) % 2, :], src, ACT.Square).then_inc(sq_done, 1)

                def down(e, it):
                    hi(d0 + e + 2, it)
                    hi(d0 + e + 3, it)
                    if q1 < 12:
                        added(e // 2, it)
                    hi(d0 + e + 4, it)
                    hi(d0 + e + 5, it)
                    if q1 < 12:
                        added(e // 2 + 1, it)

                with act.Fori(0, KD // 2 - 1) as i:
                    down(0, i)
                down(2 * KD - 4, None)

            act.wait_ge(cols_loaded, 16)
            act.activation(stat[:, 0:16], cols[:, 0:16], ACT.Silu).then_inc(cond_ready, 1)
            act.wait_ge(x_loaded, 16)
            for k in range(KD):
                square(NX, k, x[:, k, :])
            act.wait_ge(ctx_loaded, 16)
            for k in range(KD):
                square(NCTX, k, ctx[:, k, :])
            root(NX, D)
            hi(0)
            hi(1)
            act.wait_ge(small_loaded, 48)
            for half in range(4):
                act.wait_ge(ada_used, 15 + half // 2)
                act.activation(mod_row[:, half * 512:(half + 1) * 512], pb[half][0:2, :], ACT.Copy).then_inc(mod_rowed, 1)
            root(NCTX, D)
            act.wait_ge(mod_ready, 2)
            norm_hi(NX, hH, shift=0)
            norm_hi(NCTX, cH, shift=48)
            for s in range(18):
                hi(s + 2)
            act.wait_ge(strip_used, 18)
            for k in range(4):
                act.wait_ge(out_taken, 9 + 3 * k)
                act.activation(catH[:, 4 + k, :], conv[:, k, :], ACT.Copy).then_inc(cat_hi, 1)

            def att_context(u):
                if u >= 4:
                    act.wait_ge(p_turned, u - 3)
                act.wait_ge(scored, u + 1)
                act.activation(prob[:, u % 4, 0:C], pb[2 * (u % 2) + 1][:, 0:C], ACT.Copy).then_inc(ctx_copied, 1)

            def att_exp(u):
                lo_, hi_ = keys(UNITS[u][0])
                act.wait_ge(ctx_copied, u + 1)
                act.wait_ge(bias_ready, u + 1)
                p = prob[:, u % 4, 0:C + hi_ - lo_ + 1]
                act.activation(p, p, ACT.Exp, bias=stat[:, 16 + u % 4:17 + u % 4], scale=SCALE1,
                               accum_out=stat[:, 20 + u % 4:21 + u % 4]).then_inc(exp_done, 1)

            def att_turned(u):
                n, a, j = UNITS[u]
                act.wait_ge(p_turned, u + 1)
                if n and a == j == 0:
                    act.wait_ge(pv_done, n)
                act.activation(PT[:, j, 0:4, a * P:(a + 1) * P],
                               pb[4 + 2 * (u % 2)][:, :].rearrange("p (k q) -> p k q", k=4), ACT.Copy).then_inc(pt_act, 1)

            def att_out(n):
                act.wait_ge(pv_done, n + 1)
                act.activation(catH[:, 0:4, n * P:(n + 1) * P], pb[7][:, :].rearrange("p (k q) -> p k q", k=4), ACT.Copy)\
                   .then_inc(att_hi, 1)

            for u in range(len(UNITS) + LAG1 + 2):
                if u < len(UNITS):
                    att_context(u)
                if 1 <= u <= len(UNITS):
                    att_exp(u - 1)
                if 0 <= u - LAG1 < len(UNITS):
                    att_turned(u - LAG1)
                if block_at(u - LAG1 - 2) is not None:
                    att_out(block_at(u - LAG1 - 2))

            def residual_squares(n0, t0, q, gain=None):
                for s in range(KD):
                    if n0 + s + 2 != FFN1A and n0 + s + 1 != FFN1A:
                        hi(n0 + s + 2)
                    act.wait_ge(out_taken, t0 + s + 1)
                    if gain:
                        prepare(q, s, x, gain)
                    else:
                        square(q, s, x[:, s, :])

            residual_squares(W_OUT, T_OUT, NH2)

            root(NH2, D)
            act.wait_ge(mod_ready, 6)
            norm_hi(NH2, h2, shift=24)
            for k in range(KD):
                act.wait_ge(h2_turned, k + 1)
                tt, half = k // 2, k % 2
                act.activation(h2t[:, tt, half * 512:(half + 1) * 512], pb[half][:, :], ACT.Copy).then_inc(h2t_ready, 1)
                if k == 1:
                    act.wait_ge(lmax, 2)
                    for i in range(NB):
                        act.activation(af[:, i, :], pb[4][:, i * E:(i + 1) * E], ACT.Exp, bias=stat[:, 4 + i:5 + i], scale=1.0,
                                       accum_out=stat[:, 8 + i:9 + i]).then_inc(aff_exp, 1)

            def tokens_out(it, p):
                act.wait_ge(gathered, count(it, p, 2, 1))
                act.activation(xs[:, 0:512], pb[6][:, :], ACT.Copy).then_inc(xs_act, 1)

            def tokens_turned(it, p):
                act.wait_ge(xs_turned, count(it, p, 2, 1))
                act.activation(xsT[:, 0:4, :], pb[2][:, :].rearrange("p (k s) -> p k s", k=4), ACT.Copy).then_inc(xsT_act, 1)

            def silu(it, p):
                act.wait_ge(exp_used, count(it, p, 24, 16))
                for half in range(2):
                    act.activation(sil[:, half * 512:(half + 1) * 512], pb[half][:, :], ACT.Silu).then_inc(sil_done, 1)

            def hidden_turned(it, p):
                act.wait_ge(hid_turned, count(it, p, 2, 1))
                act.activation(hidT[:, 0:4, :], pb[0][:, :].rearrange("p (k s) -> p k s", k=4), ACT.Copy).then_inc(hidT_act, 1)

            def expert_out(it, p):
                act.wait_ge(exp_used, count(it, p, 24, 24))
                act.activation(xs[:, 0:512], pb[4][:, :], ACT.Copy).then_inc(y_act, 1)
                act.wait_ge(pg_turned, count(it, p, 1, 1))
                act.activation(pickgT[:, :], pb[6][:, :], ACT.Copy).then_inc(pgT_ready, 1)

            tokens_out(None, 0)
            tokens_turned(None, 0)
            with act.Fori(0, PAIRS - 1) as i:
                silu(i, 0)
                tokens_out(i, 1)
                hidden_turned(i, 0)
                tokens_turned(i, 1)
                expert_out(i, 0)
            silu(None, PAIRS - 1)
            hidden_turned(None, PAIRS - 1)
            expert_out(None, PAIRS - 1)

            hi(FFN1A)
            hi(FFN1A + 1)
            act.wait_ge(gain_ready, 6)
            for k in range(KD):
                act.wait_ge(x_added, (PAIRS - 1) * KD + k + 1)
                square(NFIN, k, x[:, k, :])
                act.activation(hH[:, k, :], x[:, k, :], ACT.Copy, scale=both_gains[:, k:k + 1]).then_inc(h_hi, 1)
            hi(FFN1A + 2)
            root(NFIN, D)
            hi(FFN1A + 3)
            for k in range(KD):
                act.wait_ge(x_normed, k + 1)
                square(N1A, k, x[:, k, :])
            ffn(*ffns[0])

            root(NMA, D)
            for n in range(4):
                hi(POOL + n + 2)
            act.wait_ge(strip_used, POOL + 4)
            for m in range(KD):
                act.wait_ge(x_pooled, m + 1)
                prepare(N2A, m, x, "ffn2a")
            ffn(*ffns[1])
            ffn(*ffns[2])

            for s in range(9):
                hi(M_IN + s + 2)
                if s == 0:
                    root(NMB, D)
                if s == KQ + 1:
                    root(NQL, KQ * P)
                act.wait_ge(out_taken, T_MIN + s + 1)
                if s < KQ:
                    prepare(NQL, s, lat, "q_norm")
                elif s < KQ + KKV:
                    square(NKL, s - KQ, lat[:, s, :])
            for k in range(2):
                act.wait_ge(angle, 8 + 2 * k)
                act.activation(rope2[:, 1 - k, :], (ang if k == 0 else turns)[:, :], ACT.Sin).then_inc(sines, 1)

            def head_square(n, src):
                if n >= 2:
                    act.wait_ge(hq_summed, n - 1)
                act.activation(sq[:, n % 2, :], src, ACT.Square).then_inc(hq_sq, 1)

            def head_root(group):
                act.wait_ge(hq_summed, (12, 21)[group])
                act.wait_ge(hq_rstd if group else rstd_done, group or NKL + 1)
                act.activation(head_std[:, :], pb[4 + group][0:MH, :], ACT.Sqrt, bias=eps[0:MH, 0:1], scale=1.0 / (NOPE + ROPE))\
                   .then_inc(hq_std, 1)

            for s in range(12):
                hi(M_Q + s + 2)
                if s == 9:
                    norm_hi(NKL, nH[:, KQ:KD, :])
                act.wait_ge(out_taken, T_MQ + s + 1)
                if s == 0:
                    act.wait_ge(ssq_done, SS0[N2B])
                head_square(s, qr[:, s, :] if s < 4 else qn[:, s - 4, :])
                if s == 0:
                    root(NKL, KKV * P)
            head_square(12, lat[:, 8, :])
            for g in range(2):
                hi(M_K + g + 2)
                act.wait_ge(strip_used, M_K + g + 1)
                for h in range(4 * g, 4 * g + 4):
                    act.activation(kn[:, h, :], pb[h % 4][:, :], ACT.Copy).then_inc(out_taken, 1)
                if g == 0:
                    head_root(0)
                for h in range(4 * g, 4 * g + 4):
                    act.wait_ge(out_taken, T_MK + h + 1)
                    head_square(13 + h, kn[:, h, :])
            for g in range(2):
                if g == 0:
                    head_root(1)
                hi(M_V + g + 2)
                act.wait_ge(strip_used, M_V + g + 1)
                for i in range(NB):
                    act.activation(V2[:, i, 512 * g:512 * g + 512], pb[i][:, :], ACT.Copy).then_inc(out_taken, 1)

            def soft(u):
                h, b = divmod(u, NB)
                act.wait_ge(bias_ready, 32 + u + 1)
                p = prob2[:, u % 4, 0:(b + 1) * P]
                act.activation(p, p, ACT.Exp, bias=stat[:, 16 + u % 4:17 + u % 4], scale=SCALE2,
                               accum_out=stat[:, 20 + u % 4:21 + u % 4]).then_inc(exp_done, 1)

            def turn_out(u):
                h, b = divmod(u, NB)
                act.wait_ge(p_turned, 32 + u + 1)
                if b == 0 and h >= 2:
                    act.wait_ge(pv_done, NB + h - 1)
                act.activation(pT2[h % 2][:, 0:b + 1, b * P:(b + 1) * P],
                               pb[2 + u % 2][:, 0:(b + 1) * P].rearrange("p (k q) -> p k q", q=P), ACT.Copy).then_inc(pt_act, 1)

            def head_out(h):
                act.wait_ge(pv_done, NB + h + 1)
                act.activation(oH[:, h, :], pb[4 + h % 2][:, :], ACT.Copy).then_inc(att_hi, 1)

            for u in range(MH * NB + LAG + 2):
                if u < MH * NB:
                    soft(u)
                if 0 <= u - LAG < MH * NB:
                    turn_out(u - LAG)
                if head_at(u - LAG - 2) is not None:
                    head_out(head_at(u - LAG - 2))
            residual_squares(M_OUT, T_MOUT, N2B, "ffn2b")
            ffn(*ffns[3])

        @block.tensor
        def _(pe):
            def three(ps, lhs, rhs, first, last):
                (lh, ll), (rh, rl) = lhs, rhs
                pe.matmul(ps, lh, rh, start=first, stop=False)
                pe.matmul(ps, lh, rl, start=False, stop=False)
                return pe.matmul(ps, ll, rh, start=False, stop=last)

            def weights(n, c, w=P):
                return wH[:, n % 2, c:c + w], wL[:, n % 2, c:c + w]

            def norm_sum(q):
                pe.wait_ge(ssq_done, SS0[q] + KT[q] + 1)
                if q:
                    pe.wait_ge(std_done, q)
                else:
                    pe.wait_ge(ones_set, 2)
                pe.matmul(pb[6][:, 0:WID[q]], ones[:, :], ssq[:, 0:WID[q]], start=True, stop=True).then_inc(norm_summed, 1)

            def whole(n, tile, kt, high, low, lows_of=None, c0=0, used=True, at=None, free=None):
                pe.wait_ge(strip_lo, n + 1)
                if at is None:
                    pe.wait_ge(out_taken, tile - 1)
                elif at == 0:
                    pe.wait_ge(out_taken, free or tile)
                for k in range(kt):
                    if lows_of is not None:
                        pe.wait_ge(h_lo, lows_of + k + 1)
                    mm = three(pb[bank(tile) if at is None else at][:, :], weights(n, c0 + k * P), (high[:, k, :], low[:, k, :]),
                               k == 0, k == kt - 1)
                if used:
                    mm.then_inc(strip_used, 1)

            def mod_sum(b):
                pe.wait_ge(ada_added, 8 * (b - 1))
                pe.wait_ge(mod_ready, b)
                for m in range(KD):
                    mm = pe.matmul(pb[7][:, 8 * b + m:8 * b + m + 1], acc[:, b % 2, m * P:(m + 1) * P], ones[:, 0:1], start=True, stop=True)
                mm.then_inc(mod_summed, 1)

            pe.wait_ge(cond_ready, 1)
            for a in range(16):
                k, b = a // 2, a % 2
                pe.wait_ge(ada_landed[a % 4], 16 * (a // 4 + 1))
                for half in range(2):
                    mm = pe.matmul(pb[2 * b + half][0:2, :], stat[:, k:k + 9:8], adaw[:, a % 4, half * 512:(half + 1) * 512],
                                   start=(k == 0), stop=(k == KD - 1))
                mm.then_inc(ada_used, 1)
                if a == 11:
                    norm_sum(NX)
            norm_sum(NCTX)
            for m in range(2 * KD):
                if m % 4 == 0:
                    pe.wait_ge(mod_rowed, m // 4 + 1)
                mm = pe.transpose(pb[7][:, 2 * m:2 * m + 2], mod_row[:, m * P:(m + 1) * P], tab("ident", 2)[0:2, :])
            mm.then_inc(mod_summed, 2)
            for s in range(18):
                pe.wait_ge(strip_lo, s + 1)
                if s >= 2:
                    pe.wait_ge(out_taken, s - 1)
                for k in range(KD):
                    if s == 0:
                        pe.wait_ge(h_lo, LO0[NX] + k + 1)
                    mm = three(pb[bank(s)][:, :], weights(s, k * P), (hH[:, k, :], hL[:, k, :]), k == 0, k == KD - 1)
                if s < 2:
                    for k in range(KD):
                        if s == 0:
                            pe.wait_ge(h_lo, LO0[NCTX] + k + 1)
                        mm = three(pb[bank(s) + 1][:, 0:C], weights(s, k * P), (cH[:, k, :], cL[:, k, :]), k == 0, k == KD - 1)
                mm.then_inc(strip_used, 1)
                if s in ROT_AT:
                    r = ROT_AT[s]
                    src = kT[:, 0:T] if r == 0 else qT[:, r - 1, :]
                    pe.wait_ge(out_taken, s)
                    if r >= 2:
                        pe.wait_ge(rope_done, r - 1)
                    pe.matmul(pb[4 + r % 2][:, :], tab("turn"), src, start=True, stop=True).then_inc(turned, 1)
                if s in (4, 8, 12, 16):
                    mod_sum(1 + s // 4)
                if s == 9:
                    pe.wait_ge(rope_done, 5)
                    for i in range(6):
                        mm = pe.transpose(pb[4 + i // 4][:, (i % 4) * P:(i % 4 + 1) * P], vT[:, i * P:(i + 1) * P], tab("ident"))
                        if i in (3, 5):
                            mm.then_inc(v_turned, 1)

            def att_scores(u):
                n, a, j = UNITS[u]
                lo_, hi_ = keys(n)
                if u < 2:
                    pe.wait_ge(out_taken, 18)
                    pe.wait_ge(rope_done, 5)
                else:
                    pe.wait_ge(masked, u - 1)
                    pe.wait_ge(ctx_copied, u - 1)
                q = qT[64 * j:64 * j + 64, a, n * P:(n + 1) * P]
                pe.matmul(pb[2 * j][:, 0:hi_ - lo_], q, kT[64 * j:64 * j + 64, lo_:hi_], start=True, stop=True)
                pe.matmul(pb[2 * j + 1][:, 0:C], q, kT[64 * j:64 * j + 64, T:T + C], start=True, stop=True).then_inc(scored, 1)

            def att_turn(u):
                tiles = len(kv_tiles[UNITS[u][0]])
                pe.wait_ge(p_ready, u + 1)
                if u >= 2:
                    pe.wait_ge(pt_act, u - 1)
                if tiles == 5:
                    pe.wait_ge(v_ready, 2)
                    pe.wait_ge(pt_dve, b_units(u))
                for k in range(tiles):
                    dst = pb[4 + 2 * (u % 2)][:, k * P:(k + 1) * P] if k < 4 else pb[5][:, 0:P]
                    mm = pe.transpose(dst, prob[:, u % 4, k * P:(k + 1) * P], tab("ident"))
                mm.then_inc(p_turned, 1)

            def att_values(n):
                pe.wait_ge(pt_act, 8 * n + 8)
                pe.wait_ge(pt_dve, b_units(8 * n + 8))
                pe.wait_ge(v_ready, 2)
                if n == 0:
                    pe.wait_ge(mod_ready, 6)
                else:
                    pe.wait_ge(att_lo, n)
                tiles = len(kv_tiles[n])
                for k, v in enumerate(kv_tiles[n]):
                    for j in range(2):
                        mm = pe.matmul(pb[7][64 * j:64 * j + 64, :], V[:, v, 64 * j:64 * j + 64], PT[:, j, k, :],
                                       start=(k == 0), stop=(k == tiles - 1))
                mm.then_inc(pv_done, 1)

            for u in range(len(UNITS) + LAG1 + 1):
                if u < len(UNITS):
                    att_scores(u)
                if 0 <= u - LAG1 < len(UNITS):
                    att_turn(u - LAG1)
                if block_at(u - LAG1 - 1) is not None:
                    att_values(block_at(u - LAG1 - 1))

            pe.wait_ge(cat_lo, 4)
            pe.wait_ge(att_lo, NB)
            for s in range(KD):
                whole(W_OUT + s, T_OUT + s, KD, catH, catL)

            norm_sum(NH2)
            pe.wait_ge(wr_loaded, 16)
            for k in range(KD):
                pe.wait_ge(h_hi, HI0[NH2] + k + 1)
                mm = pe.matmul(pb[5][0:E, :], wr[:, k, :], h2[:, k, :], start=(k == 0), stop=(k == KD - 1))
            mm.then_inc(logits_summed, 1)
            for m in range(8):
                if m >= 2:
                    pe.wait_ge(h2t_ready, m - 1)
                for i in range(4):
                    mm = pe.transpose(pb[m % 2][:, i * P:(i + 1) * P], h2[:, 4 * (m % 2) + i, (m // 2) * P:(m // 2 + 1) * P], tab("ident"))
                mm.then_inc(h2_turned, 1)
                if m == 0:
                    pe.wait_ge(logits_copied, 1)
                    for i in range(NB):
                        mm = pe.transpose(pb[4][:, i * E:(i + 1) * E], afT[:, i * P:(i + 1) * P], tab("ident", E)[0:E, :])
                    mm.then_inc(logits_done, 1)
                if m == 3:
                    pe.wait_ge(aff_ready, NB)
                    for i in range(NB):
                        mm = pe.transpose(pb[5][0:E, i * P:(i + 1) * P], af[:, i, :], tab("ident"))
                    mm.then_inc(aff_turned, 1)
            pe.wait_ge(top_step, 20)
            for i in range(NB):
                mm = pe.transpose(pb[5][:, i * E:(i + 1) * E], pos[:, i * P:(i + 1) * P], tab("ident", E)[0:E, :])
            mm.then_inc(pos_turned, 1)
            pe.wait_ge(h2t_ready, 8)

            def gather(it, p):
                pe.wait_ge(pick_ready, count(it, p, 1, 1))
                for half in range(2):
                    for k in range(NB):
                        mm = pe.matmul(pb[6 + half][:, :], pick[:, k, :], h2t[:, k, half * 512:(half + 1) * 512],
                                       start=(k == 0), stop=(k == NB - 1))
                    mm.then_inc(gathered, 1)

            def turn_tokens(it, p):
                for half, copied in enumerate((xs_act, xs_dve)):
                    pe.wait_ge(copied, count(it, p, 1, 1))
                    for k in range(4):
                        c = (4 * half + k) * P
                        mm = pe.transpose(pb[2 + half][:, k * P:(k + 1) * P], xs[:, c:c + P], tab("ident"))
                    mm.then_inc(xs_turned, 1)

            def scatter(it, p, k):
                if k == 0:
                    pe.wait_ge(pgT_ready, count(it, p, 1, 1))
                    pe.wait_ge(y_act, count(it, p, 1, 1))
                if k == 4:
                    pe.wait_ge(y_dve, count(it, p, 1, 1))
                if k >= 2:
                    pe.wait_ge(x_added, count(it, p, KD, k - 1))
                pe.matmul(pb[7 - k % 2][:, :], xs[:, k * P:(k + 1) * P], pickgT[:, :], start=True, stop=True).then_inc(scattered, 1)

            def gate_up(it, p):
                for k in range(KD):
                    if k == 0:
                        pe.wait_ge(xsT_act, count(it, p, 1, 1))
                        pe.wait_ge(xsT_dve, count(it, p, 1, 1))
                    for g in range(2):
                        d = 2 * k + g
                        pe.wait_ge(exp_landed[d % RING], count(it, p, 16 * 24 // RING, 16 * (d // RING + 1)))
                        for half in range(2):
                            for j in range(2):
                                mm = pe.matmul(pb[2 * g + half][64 * j:64 * j + 64, :], xsT[:, k, 64 * j:64 * j + 64],
                                               ring[:, 2 * (d % RING) + j, half * 512:(half + 1) * 512],
                                               start=(k == 0), stop=(k == KD - 1))
                        mm.then_inc(exp_used, 1)
                    if it is not None and 2 <= k < 6:
                        scatter(it, p - 1, 2 * k - 4)
                        scatter(it, p - 1, 2 * k - 3)

            def turn_hidden(it, p):
                for half in range(2):
                    pe.wait_ge(hid_done, count(it, p, 2, half + 1))
                    for k in range(4):
                        c = (4 * half + k) * P
                        mm = pe.transpose(pb[half][:, k * P:(k + 1) * P], hid[:, c:c + P], tab("ident"))
                    mm.then_inc(hid_turned, 1)

            def down(it, p):
                for k in range(8):
                    if k == 0:
                        pe.wait_ge(hidT_act, count(it, p, 1, 1))
                    if k == 4:
                        pe.wait_ge(hidT_dve, count(it, p, 1, 1))
                    d = 16 + k
                    pe.wait_ge(exp_landed[d % RING], count(it, p, 16 * 24 // RING, 16 * (d // RING + 1)))
                    for half in range(2):
                        for j in range(2):
                            mm = pe.matmul(pb[4 + half][64 * j:64 * j + 64, :], hidT[:, k, 64 * j:64 * j + 64],
                                           ring[:, 2 * (d % RING) + j, half * 512:(half + 1) * 512],
                                           start=(k == 0), stop=(k == 7))
                    mm.then_inc(exp_used, 1)
                pe.wait_ge(pickg_ready, count(it, p, 1, 1))
                for k in range(NB):
                    mm = pe.transpose(pb[6][:, k * P:(k + 1) * P], pickg[:, k, :], tab("ident"))
                mm.then_inc(pg_turned, 1)

            gather(None, 0)
            turn_tokens(None, 0)
            gate_up(None, 0)
            with pe.Fori(0, PAIRS - 1) as i:
                gather(i, 1)
                turn_hidden(i, 0)
                turn_tokens(i, 1)
                down(i, 0)
                gate_up(i, 1)
                pe.wait_ge(x_added, count(i, 0, KD, KD))
            turn_hidden(None, PAIRS - 1)
            down(None, PAIRS - 1)
            for k in range(KD):
                scatter(None, PAIRS - 1, k)

            def ffn(n0, t0, f, q):
                lows = LO0[NFIN if f == 0 else q]

                def inner(tile, it, waits):
                    for part in range(2):
                        n = n0 + 2 * tile + part
                        pe.wait_ge(strip_lo, shifted(n + 1, it))
                        if part == 0:
                            pe.wait_ge(out_taken, shifted(t0 + tile - 1, it, 2))
                        for k in range(KD):
                            if waits and part == 0:
                                pe.wait_ge(h_lo, lows + k + 1)
                            mm = three(pb[bank(t0 + tile) + part][:, :], weights(n, k * P), (hH[:, k, :], hL[:, k, :]), k == 0, k == KD - 1)
                        mm.then_inc(strip_used, 1)

                def outer(m, it):
                    t = t0 + KF + m
                    for half in range(2):
                        n = n0 + 2 * KF + 2 * m + half
                        pe.wait_ge(strip_lo, shifted(n + 1, it))
                        pe.wait_ge(g_lo, f * KF + HALF_KF * (half + 1))
                        if half == 0:
                            pe.wait_ge(out_taken, shifted(t - 1, it, 2))
                        for k in range(HALF_KF):
                            g = half * HALF_KF + k
                            mm = three(pb[bank(t)][:, :], weights(n, k * P), (gH[:, g, :], gL[:, g, :]), g == 0, g == KF - 1)
                        mm.then_inc(strip_used, 1)

                inner(0, None, True)
                norm_sum(NFIN if f == 0 else q)
                inner(1, None, False)
                if f == 0:
                    norm_sum(q)
                with pe.Fori(0, KF // 2 - 1) as i:
                    inner(2, i, False)
                    inner(3, i, False)
                with pe.Fori(0, KD // 2) as i:
                    outer(0, i)
                    outer(1, i)

            ffn(*ffns[0])
            for n, g in enumerate(POOL_ORDER):
                for m in range(2):
                    j = 2 * n + m
                    whole(POOL + n, T_POOL + j, 2, hH[:, 2 * g:2 * g + 2, :], hL[:, 2 * g:2 * g + 2, :],
                          lows_of=LO0[NMA] + 6 if j == 0 else None, c0=2 * m * P, used=(m == 1), at=POOL_BANKS[j], free=T_POOL + 1 if j == 7 else None)
                    if j == 0:
                        norm_sum(NMA)
            ffn(*ffns[1])
            ffn(*ffns[2])

            for s in range(9):
                whole(M_IN + s, T_MIN + s, KD, hH, hL, lows_of=LO0[NMB] if s == 0 else None)
                if s == 0:
                    norm_sum(NMB)
                if s == KQ:
                    norm_sum(NQL)

            def turn(r, src):
                pe.wait_ge(gained, r + 1)
                if r >= 2:
                    pe.wait_ge(rope_done, 5 + r - 1)
                if r == 1:
                    pe.wait_ge(std_done, NKL + 1)
                pe.matmul(pb[7 - r % 2][:, :], tab("turn"), src, start=True, stop=True).then_inc(turned, 1)

            def head_sum(n):
                pe.wait_ge(hq_sq, n + 1)
                if n < 4:
                    rows = tab("two_rows")[:, 6 - 2 * n:14 - 2 * n]
                elif n == 12:
                    rows = tab("lower")
                else:
                    h = n - 4 if n < 12 else n - 13
                    rows = tab("one_row")[:, 7 - h:15 - h]
                pe.matmul(pb[4 if n < 12 else 5][0:MH, :], rows, sq[:, n % 2, :], start=n in (0, 12), stop=n in (11, 20))\
                  .then_inc(hq_summed, 1)

            def spread_rows(n):
                if n == 0:
                    pe.wait_ge(select_loaded, 16)
                pe.wait_ge(hq_rstd, 1 if n < 12 else 2)
                if n >= 2:
                    pe.wait_ge(hq_out, OUTS[n - 1])
                pe.matmul(pb[6 + n % 2][:, :], select[:, n if n < 12 else n - 12, :], head_rstd[n >= 12][:, :], start=True, stop=True)\
                  .then_inc(spread, 1)

            for s in range(12):
                whole(M_Q + s, T_MQ + s, KQ, nH, nL, lows_of=LO0[NQL] if s == 0 else None)
                if s == 0:
                    norm_sum(NKL)
                if 1 <= s <= 5:
                    r = s - 1
                    turn(r, krope[:, :] if r == 0 else qr[:, r - 1, :])
                if s:
                    head_sum(s - 1)

            def keys_of(g):
                for m in range(4):
                    whole(M_K + g, T_MK + 4 * g + m, KKV, nH[:, KQ:KD, :], nL[:, KQ:KD, :],
                          lows_of=LO0[NKL] if g == m == 0 else None, c0=2 * m * P, used=(m == 3), at=m)

            def values_of(g):
                n = M_V + g
                pe.wait_ge(strip_lo, n + 1)
                pe.wait_ge(out_taken, T_MV + 4 * g)
                for i in range(NB):
                    for k in range(KKV):
                        lhs = (nH[:, KQ + k, i * P:(i + 1) * P], nL[:, KQ + k, i * P:(i + 1) * P])
                        mm = three(pb[i][:, :], lhs, weights(n, k * 512, 512), k == 0, k == KKV - 1)
                mm.then_inc(strip_used, 1)

            keys_of(0)
            head_sum(11)
            head_sum(12)
            keys_of(1)
            for h in range(4):
                head_sum(13 + h)
            for n in range(6):
                spread_rows(n)
            for h in range(4, 8):
                head_sum(13 + h)
            values_of(0)
            for n in range(6, 12):
                spread_rows(n)
            values_of(1)
            for n in range(12, 20):
                spread_rows(n)

            def scores(u):
                h, b = divmod(u, NB)
                w = (b + 1) * P
                if u < 2:
                    pe.wait_ge(out_taken, T_MOUT)
                    pe.wait_ge(hq_out, OUTS[20])
                elif u >= 4:
                    pe.wait_ge(masked, 32 + u - 3)
                pe.matmul(pb[S2[u % 4]][:, 0:w], qn[:, h, b * P:(b + 1) * P], kn[:, h, 0:w], start=True, stop=False)
                pe.matmul(pb[S2[u % 4]][:, 0:w], qr[:, h // 2, b * P:(b + 1) * P], kr[:, h, 0:w], start=False, stop=True).then_inc(scored, 1)

            def turn_probs(u):
                h, b = divmod(u, NB)
                pe.wait_ge(p_ready, 32 + u + 1)
                pe.wait_ge(pt_act, 32 + u - 1)
                for k in range(b + 1):
                    mm = pe.transpose(pb[2 + u % 2][:, k * P:(k + 1) * P], prob2[:, u % 4, k * P:(k + 1) * P], tab("ident"))
                mm.then_inc(p_turned, 1)

            def values(h):
                pe.wait_ge(pt_act, 32 + NB * h + NB)
                if h >= 2:
                    pe.wait_ge(att_lo, NB + h - 1)
                for k in range(NB):
                    mm = pe.matmul(pb[4 + h % 2][:, k * P:T], V2[:, k, h * P:(h + 1) * P], pT2[h % 2][:, k, k * P:T],
                                   start=(k == 0), stop=(k == NB - 1))
                mm.then_inc(pv_done, 1)

            for u in range(MH * NB + LAG + 1):
                if u < MH * NB:
                    scores(u)
                if 0 <= u - LAG < MH * NB:
                    turn_probs(u - LAG)
                if head_at(u - LAG - 1) is not None:
                    values(head_at(u - LAG - 1))
            pe.wait_ge(att_lo, NB + MH)
            for s in range(KD):
                whole(M_OUT + s, T_MOUT + s, KD, oH, oL)
            ffn(*ffns[3])

        @block.vector
        def _(dve):
            def lo(n, it=None):
                if n >= N_STRIPS:
                    return
                dve.wait_ge(strip_hi, shifted(n + 1, it))
                w = width[n]
                dve.tensor_tensor(wL[:, n % 2, 0:w], stage[:, n % STAGE, 0:w], wH[:, n % 2, 0:w], ALU.subtract).then_inc(strip_lo, 1)

            def clear(q):
                if q:
                    dve.wait_ge(norm_summed, q)
                dve.memset(ssq[:, :], 0.0).then_inc(ssq_done, 1)

            def add(q, k, it=None):
                dve.wait_ge(sq_done, shifted(SQ0[q] + k + 1, it, 2))
                dve.wait_ge(ssq_done, shifted(SS0[q] + k + 1, it, 2))
                w = WID[q]
                dve.tensor_tensor(ssq[:, 0:w], ssq[:, 0:w], sq[:, (SQ0[q] + k) % 2, 0:w], ALU.add).then_inc(ssq_done, 1)

            def invert(q):
                dve.wait_ge(std_done, q + 1)
                dve.reciprocal(rstd_of[q][:, 0:WID[q]], std[:, 0:WID[q]]).then_inc(rstd_done, 1)

            def norm_low(q, src, gain, high, low, shift=None):
                w = WID[q]
                dve.wait_ge(rstd_done, q + 1)
                for k in range(KT[q] + 1):
                    if k < KT[q]:
                        if q or k >= 2:
                            dve.wait_ge(h_hi, HI0[q] + max(k - 1, 0))
                            dve.wait_ge(h_lo, LO0[q] + (max(k - 1, 0) if low is not None else 0))
                        dve.scalar_tensor_tensor(out=hraw[:, (RAW0[q] + k) % 2, 0:w], in0=src[:, k, :], scalar=gain(k),
                                                 in1=rstd_of[q][:, 0:w], op0=ALU.mult, op1=ALU.mult).then_inc(h_raw, 1)
                    if k and low is not None:
                        dve.wait_ge(h_hi, HI0[q] + k)
                        raw = hraw[:, (RAW0[q] + k - 1) % 2, 0:w]
                        if shift is None:
                            ins = dve.tensor_tensor(low[:, k - 1, :], raw, high[:, k - 1, :], ALU.subtract)
                        else:
                            ins = dve.scalar_tensor_tensor(out=low[:, k - 1, :], in0=raw, scalar=mod[:, shift + k - 1:shift + k],
                                                           in1=high[:, k - 1, :], op0=ALU.add, op1=ALU.subtract)
                        ins.then_inc(h_lo, 1)

            def lowered(q, k, src, gain, it=None):
                g = k if it is None else it * 2 + k
                a = COL[gain][0]
                scale = cols[:, a + k:a + k + 1] if it is None else cols[:, bass.ds(it * 2 + (a + k), 1)]
                high, low = (nH, nL) if q == NQL else (hH, hL)
                dve.wait_ge(h_hi, shifted(HI0[q] + k + 1, it, 2))
                dve.scalar_tensor_tensor(out=low[:, g, :], in0=src[:, g, :], scalar=scale, in1=high[:, g, :],
                                         op0=ALU.mult, op1=ALU.subtract).then_inc(h_lo, 1)

            def ada(a):
                b, k = divmod(a, KD)
                dve.wait_ge(ada_landed[a % 4], 16 * (a // 4 + 1))
                if k == 0 and b >= 4:
                    dve.wait_ge(mod_summed, b - 1)
                w, v = adaw[:, a % 4, :], stat[:, k:k + 1]
                if k == 0:
                    dve.wait_ge(cond_ready, 1)
                    dve.tensor_scalar(acc[:, b % 2, :], w, v, None, ALU.mult).then_inc(ada_added, 1)
                else:
                    dve.wait_ge(ada_added, a - 16)
                    dve.scalar_tensor_tensor(out=acc[:, b % 2, :], in0=w, scalar=v, in1=acc[:, b % 2, :],
                                             op0=ALU.mult, op1=ALU.add).then_inc(ada_added, 1)

            def mod_take(b):
                dve.wait_ge(mod_summed, b + 1)
                bias = cols[:, COL["b_ada"][0] + 8 * b:COL["b_ada"][0] + 8 * b + 8]
                dve.tensor_tensor(mod[:, 8 * b:8 * b + 8], pb[7][:, 8 * b:8 * b + 8], bias, ALU.add).then_inc(mod_ready, 1)

            def mod_gain(dst, scale_col, g, need):
                dve.wait_ge(mod_ready, need)
                dve.scalar_tensor_tensor(out=gain1[:, dst:dst + 8], in0=mod[:, scale_col:scale_col + 8], scalar=1.0,
                                         in1=cols[:, COL[g][0]:COL[g][0] + 8], op0=ALU.add, op1=ALU.mult).then_inc(gain_ready, 1)

            dve.wait_ge(cols_loaded, 16)
            sink = cols[:, COL["sink"][0]:COL["sink"][0] + H]
            dve.tensor_scalar(stat[:, 40:48], sink, -1.0, None, ALU.mult).then_inc(gain_ready, 1)
            dve.tensor_scalar(stat[:, 48:56], sink, 1.0 / SCALE1, None, ALU.mult).then_inc(gain_ready, 1)
            for q in (NX, NCTX):
                clear(q)
                for k in range(KD):
                    add(q, k)
            invert(NX)
            lo(0)
            lo(1)
            dve.wait_ge(small_loaded, 48)
            dve.wait_ge(mod_summed, 2)
            bias = cols[:, COL["b_ada"][0]:COL["b_ada"][0] + 16]
            for j, at in ((0, 0), (1, 48)):
                dve.tensor_tensor(mod[:, at:at + 16], pb[7][:, j:32:2], bias, ALU.add).then_inc(mod_ready, 1)
            mod_gain(0, 8, "g_mix", 2)
            mod_gain(8, 56, "g_mix", 2)
            dve.wait_ge(gain_ready, 4)
            norm_low(NX, x, lambda k: gain1[:, k:k + 1], hH, hL, shift=0)
            invert(NCTX)
            norm_low(NCTX, ctx, lambda k: gain1[:, 8 + k:9 + k], cH, cL, shift=48)

            def rope_finish(dst, rot, sine, cosine, tmp, r0):
                dve.wait_ge(turned, r0 + 1)
                if r0:
                    dve.wait_ge(rope_done, r0)
                dve.tensor_tensor(tmp, rot, sine, ALU.mult).then_inc(rope_part, 1)
                dve.tensor_tensor(dst, dst, cosine, ALU.mult).then_inc(rope_part, 1)
                dve.wait_ge(rope_part, 2 * r0 + 2)
                dve.tensor_tensor(dst, dst, tmp, ALU.add).then_inc(rope_done, 1)

            for s in range(18):
                if s < 16:
                    ada(16 + 2 * s)
                    ada(17 + 2 * s)
                lo(s + 2)
                dve.wait_ge(strip_used, s + 1)
                ps = pb[bank(s)][:, :]
                if s < 2:
                    dst = (kT, vT)[s]
                    dve.tensor_copy(dst[:, 0:T], ps)
                    dve.tensor_copy(dst[:, T:T + C], pb[bank(s) + 1][:, 0:C]).then_inc(out_taken, 1)
                elif s < 6:
                    dve.tensor_copy(qT[:, s - 2, :], ps).then_inc(out_taken, 1)
                else:
                    i, part = divmod(s - 6, 3)
                    w3 = [cols[:, COL["conv_w"][0] + 3 * i + j:COL["conv_w"][0] + 3 * i + j + 1] for j in range(3)]
                    y, u = gf[:, 0, :], sg[:, 1, :]
                    if part == 0:
                        dve.tensor_copy(sg[:, 0, :], ps).then_inc(out_taken, 1)
                    elif part == 1:
                        dve.wait_ge(out_taken, s)
                        dve.tensor_tensor(u, ps, sg[:, 0, :], ALU.mult).then_inc(out_taken, 1)
                        dve.wait_ge(out_taken, s + 1)
                        dve.tensor_scalar(y, u, w3[1], None, ALU.mult).then_inc(conv_part, 1)
                        dve.wait_ge(conv_part, 3 * i + 1)
                        dve.scalar_tensor_tensor(out=y[:, 1:T], in0=u[:, 0:T - 1], scalar=w3[0], in1=y[:, 1:T],
                                                 op0=ALU.mult, op1=ALU.add).then_inc(conv_part, 1)
                        dve.wait_ge(conv_part, 3 * i + 2)
                        dve.scalar_tensor_tensor(out=y[:, 0:T - 1], in0=u[:, 1:T], scalar=w3[2], in1=y[:, 0:T - 1],
                                                 op0=ALU.mult, op1=ALU.add).then_inc(conv_part, 1)
                    else:
                        dve.wait_ge(conv_part, 3 * i + 3)
                        dve.tensor_tensor(conv[:, i, :], ps, y, ALU.mult).then_inc(out_taken, 1)
                if s - 1 in ROT_AT:
                    r = ROT_AT[s - 1]
                    rope_finish(kT[:, 0:T] if r == 0 else qT[:, r - 1, :], pb[4 + r % 2][:, :], rope[:, 1, :], rope[:, 0, :],
                                gf[:, 1, :], r)
                if s in (6, 10, 14):
                    mod_take(s // 4 + 1)
                if s == 11:
                    dve.wait_ge(v_turned, 2)
                    dve.tensor_copy(V[:, 0:4, :], pb[4][:, :].rearrange("p (k d) -> p k d", k=4)).then_inc(v_ready, 1)
                    dve.tensor_copy(V[:, 4:6, :], pb[5][:, 0:C].rearrange("p (k d) -> p k d", k=2)).then_inc(v_ready, 1)
            mod_take(5)
            mod_gain(16, 32, "g_ffn", 6)
            for k in range(4):
                dve.wait_ge(cat_hi, k + 1)
                dve.tensor_tensor(catL[:, 4 + k, :], conv[:, k, :], catH[:, 4 + k, :], ALU.subtract).then_inc(cat_lo, 1)

            def att_soft(u):
                if u == len(UNITS):
                    invert_sum(u - 1)
                    scale_probs(u - 1, att_probs(u - 1))
                    return
                n, a, j = UNITS[u]
                w = keys(n)[1] - keys(n)[0]
                off = P if n == 0 else 0
                head = a + 4 * j
                m1, m2 = stat[:, 28 + u % 4:29 + u % 4], stat[:, 32 + u % 4:33 + u % 4]
                dve.wait_ge(ctx_copied, u + 1)
                if u >= 4:
                    dve.wait_ge(p_turned, u - 3)
                dve.reduce_max(m1, prob[:, u % 4, 0:C], AX_X).then_inc(row_max, 1)
                dve.tensor_copy(prob[:, u % 4, C + w:C + w + 1], stat[:, 48 + head:49 + head]).then_inc(row_max, 1)
                if u:
                    invert_sum(u - 1)
                dve.wait_ge(row_max, 2 * u + 2)
                dve.tensor_tensor_reduce(prob[:, u % 4, C:C + w], pb[2 * j][:, 0:w], window[:, off:off + w], 1.0, m1,
                                         ALU.add, ALU.max, m2).then_inc(masked, 1)
                if u:
                    scale_probs(u - 1, att_probs(u - 1))
                dve.wait_ge(masked, u + 1)
                dve.tensor_scalar(stat[:, 16 + u % 4:17 + u % 4], m2, -SCALE1, stat[:, 40 + head:41 + head],
                                  ALU.mult, ALU.min).then_inc(bias_ready, 1)

            def att_probs(u):
                n = UNITS[u][0]
                return prob[:, u % 4, 0:C + keys(n)[1] - keys(n)[0]]

            def invert_sum(v):
                dve.wait_ge(exp_done, v + 1)
                dve.reciprocal(stat[:, 24 + v % 4:25 + v % 4], stat[:, 20 + v % 4:21 + v % 4]).then_inc(inv_ready, 1)

            def scale_probs(v, p):
                dve.wait_ge(inv_ready, v + 1)
                dve.tensor_scalar(p, p, stat[:, 24 + v % 4:25 + v % 4], None, ALU.mult).then_inc(p_ready, 1)

            def att_fifth(u):
                n, a, j = UNITS[u]
                if len(kv_tiles[n]) == 5:
                    dve.wait_ge(p_turned, u + 1)
                    if a == j == 0:
                        dve.wait_ge(pv_done, n)
                    dve.tensor_copy(PT[:, j, 4, a * P:(a + 1) * P], pb[5][:, 0:P]).then_inc(pt_dve, 1)

            def att_low(n):
                dve.wait_ge(att_hi, n + 1)
                dve.tensor_tensor(catL[:, 0:4, n * P:(n + 1) * P], pb[7][:, :].rearrange("p (k q) -> p k q", k=4),
                                  catH[:, 0:4, n * P:(n + 1) * P], ALU.subtract).then_inc(att_lo, 1)

            for u in range(len(UNITS) + LAG1 + 3):
                if u <= len(UNITS):
                    att_soft(u)
                if 0 <= u - LAG1 < len(UNITS):
                    att_fifth(u - LAG1)
                if block_at(u - LAG1 - 2) is not None:
                    att_low(block_at(u - LAG1 - 2))

            def residual(n0, t0, q, gain, after=None):
                clear(q)
                for s in range(KD):
                    if n0 + s + 2 != FFN1A and n0 + s + 1 != FFN1A:
                        lo(n0 + s + 2)
                    dve.wait_ge(strip_used, n0 + s + 1)
                    ps = pb[bank(t0 + s)][:, :]
                    dve.scalar_tensor_tensor(out=x[:, s, :], in0=ps, scalar=gain(s), in1=x[:, s, :], op0=ALU.mult, op1=ALU.add)\
                       .then_inc(out_taken, 1)
                    if s:
                        add(q, s - 1)
                        if after:
                            lowered(q, s - 1, x, after)
                add(q, KD - 1)
                if after:
                    lowered(q, KD - 1, x, after)

            residual(W_OUT, T_OUT, NH2, lambda m: mod[:, 16 + m:17 + m])

            invert(NH2)
            norm_low(NH2, x, lambda k: gain1[:, 16 + k:17 + k], None, None)
            dve.wait_ge(logits_summed, 1)
            dve.tensor_copy(afT[:, :], pb[5][0:E, :]).then_inc(logits_copied, 1)
            dve.wait_ge(logits_done, 1)
            logits = pb[4][:, 0:NB * E].rearrange("p (i e) -> p i e", i=NB)
            dve.tensor_reduce(stat[:, 0:4], logits, AX_X, ALU.max).then_inc(lmax, 1)
            dve.wait_ge(lmax, 1)
            dve.tensor_scalar(stat[:, 4:8], stat[:, 0:4], -1.0, None, ALU.mult).then_inc(lmax, 1)
            dve.wait_ge(aff_exp, 4)
            dve.reciprocal(stat[:, 12:16], stat[:, 8:12]).then_inc(lmax, 1)
            dve.wait_ge(lmax, 3)
            for i in range(NB):
                dve.tensor_scalar(af[:, i, :], af[:, i, :], stat[:, 12 + i:13 + i], None, ALU.mult).then_inc(aff_ready, 1)
            dve.wait_ge(aff_turned, 1)
            dve.tensor_copy(work[:, 0, :], pb[5][0:E, :]).then_inc(top_step, 1)
            for r in range(SLOTS // 8):
                dve.wait_ge(top_step, 2 * r + 1)
                dve.max(top[:, r, :], work[:, r % 2, :]).then_inc(top_step, 1)
                dve.wait_ge(top_step, 2 * r + 2)
                dve.match_replace(work[:, (r + 1) % 2, :], top[:, r, :], work[:, r % 2, :], -1.0).then_inc(top_step, 1)
            dve.wait_ge(top_step, 17)
            dve.tensor_scalar(work[:, 1, :], work[:, 0, :], 0.0, None, ALU.is_lt).then_inc(top_step, 1)
            dve.wait_ge(top_step, 18)
            dve.tensor_tensor_scan(afT[:, :], work[:, 1, :], work[:, 1, :], 0.0, ALU.add, ALU.max).then_inc(top_step, 1)
            dve.wait_ge(top_step, 19)
            dve.tensor_tensor(pos[:, :], afT[:, :], work[:, 1, :], ALU.mult).then_inc(top_step, 1)
            dve.wait_ge(pos_turned, 1)
            dve.tensor_copy(posT[:, :, :], pb[5][:, 0:NB * E].rearrange("p (i e) -> p i e", i=NB)).then_inc(posT_ready, 1)
            dve.wait_ge(posT_ready, 1)
            dve.tensor_tensor(both_gains, cols[:, COL["g_final"][0]:COL["g_final"][0] + KD],
                              cols[:, COL["ffn1a"][0]:COL["ffn1a"][0] + KD], ALU.mult).then_inc(gain_ready, 1)

            def picks(it, p, weighted):
                for k in range(NB):
                    for j in range(2):
                        e = slice(2 * p + j, 2 * p + j + 1) if it is None else bass.ds(it * 2 + (2 * p + j), 1)
                        o = (pickg if weighted else pick)[:, k, 64 * j:64 * j + 64]
                        if weighted:
                            ins = dve.tensor_scalar(o, tab("slot"), posT[:, k, e], af[:, k, e], ALU.is_equal, ALU.mult)
                        else:
                            ins = dve.tensor_scalar(o, tab("slot"), posT[:, k, e], None, ALU.is_equal)
                ins.then_inc(pickg_ready if weighted else pick_ready, 1)

            def tokens_out(it, p):
                dve.wait_ge(gathered, count(it, p, 2, 2))
                dve.tensor_copy(xs[:, 512:1024], pb[7][:, :]).then_inc(xs_dve, 1)

            def tokens_turned(it, p):
                dve.wait_ge(xs_turned, count(it, p, 2, 2))
                dve.tensor_copy(xsT[:, 4:8, :], pb[3][:, :].rearrange("p (k s) -> p k s", k=4)).then_inc(xsT_dve, 1)

            def hidden(it, p):
                for half in range(2):
                    dve.wait_ge(sil_done, count(it, p, 2, half + 1))
                    c = half * 512
                    dve.tensor_tensor(hid[:, c:c + 512], sil[:, c:c + 512], pb[2 + half][:, :], ALU.mult).then_inc(hid_done, 1)

            def hidden_turned(it, p):
                dve.wait_ge(hid_turned, count(it, p, 2, 2))
                dve.tensor_copy(hidT[:, 4:8, :], pb[1][:, :].rearrange("p (k s) -> p k s", k=4)).then_inc(hidT_dve, 1)

            def expert_out(it, p, each=None):
                dve.wait_ge(exp_used, count(it, p, 24, 24))
                dve.tensor_copy(xs[:, 512:1024], pb[5][:, :]).then_inc(y_dve, 1)
                for k in range(KD):
                    dve.wait_ge(scattered, count(it, p, KD, k + 1))
                    dve.scalar_tensor_tensor(out=x[:, k, :], in0=pb[7 - k % 2][:, :], scalar=mod[:, 40 + k:41 + k], in1=x[:, k, :],
                                             op0=ALU.mult, op1=ALU.add).then_inc(x_added, 1)
                    if each:
                        if k == 2:
                            lo(FFN1A)
                            lo(FFN1A + 1)
                        if k:
                            each(k - 1)
                if each:
                    each(KD - 1)

            picks(None, 0, False)
            tokens_out(None, 0)
            tokens_turned(None, 0)
            with dve.Fori(0, PAIRS - 1) as i:
                dve.wait_ge(gathered, count(i, 0, 2, 2))
                picks(i, 1, False)
                hidden(i, 0)
                tokens_out(i, 1)
                hidden_turned(i, 0)
                tokens_turned(i, 1)
                picks(i, 0, True)
                expert_out(i, 0)
            hidden(None, PAIRS - 1)
            hidden_turned(None, PAIRS - 1)
            picks(None, PAIRS - 1, True)

            clear(NFIN)

            def both(k):
                dve.wait_ge(h_hi, HI0[NFIN] + k + 1)
                dve.scalar_tensor_tensor(out=hL[:, k, :], in0=x[:, k, :], scalar=both_gains[:, k:k + 1], in1=hH[:, k, :],
                                         op0=ALU.mult, op1=ALU.subtract).then_inc(h_lo, 1)

            expert_out(None, PAIRS - 1, each=both)
            lo(FFN1A + 2)
            invert(NFIN)
            lo(FFN1A + 3)
            dve.wait_ge(rstd_done, NFIN + 1)
            dve.wait_ge(h_lo, LO0[NFIN] + KD)
            clear(N1A)
            for k in range(KD):
                dve.scalar_tensor_tensor(out=x[:, k, :], in0=x[:, k, :], scalar=col("g_final", k), in1=rstd_of[NFIN],
                                         op0=ALU.mult, op1=ALU.mult).then_inc(x_normed, 1)

            def ffn(n0, t0, f, q):
                def inner(tile, it):
                    dve.wait_ge(strip_used, shifted(n0 + 2 * tile + 2, it))
                    b, s, c = bank(t0 + tile), tile % 2, f * KF + tile
                    dve.tensor_tensor(hraw[:, s, :], pb[b][:, :], rstd[:, :], ALU.mult).then_inc(gate_ready, 1)
                    dve.wait_ge(strip_lo, shifted(n0 + 2 * tile + 3, it))
                    dve.tensor_tensor(gf[:, s, :], pb[b + 1][:, :], rstd[:, :], ALU.mult).then_inc(out_taken, 1)
                    dve.wait_ge(out_taken, shifted(t0 + tile + 1, it, 2))
                    dve.wait_ge(silu_done, shifted(c + 1, it, 2))
                    dve.tensor_tensor(gf[:, s, :], gf[:, s, :], sg[:, s, :], ALU.mult).then_inc(g_raw, 1)
                    dve.wait_ge(g_hi, shifted(c + 1, it, 2))
                    g = tile if it is None else it * 2 + tile
                    dve.tensor_tensor(gL[:, g, :], gf[:, s, :], gH[:, g, :], ALU.subtract).then_inc(g_lo, 1)

                def tiles(e, it):
                    lo(n0 + e + 2, it)
                    lo(n0 + e + 3, it)
                    inner(e // 2, it)
                    lo(n0 + e + 4, it)
                    lo(n0 + e + 5, it)
                    inner(e // 2 + 1, it)

                def first_tiles():
                    lo(n0 + 4)
                    lo(n0 + 5)
                    inner(0, None)
                    inner(1, None)

                invert(q)
                dve.wait_ge(rstd_done, q + 1)
                if f == 0:
                    dve.tensor_tensor(rstd[:, :], rstd[:, :], rstd_of[NFIN], ALU.mult).then_inc(rstd_both, 1)
                    dve.wait_ge(rstd_both, 1)
                    first_tiles()
                with dve.Fori(1 if f == 0 else 0, KF // 2 - 1) as i:
                    tiles(0, i)
                tiles(2 * KF - 4, None)
                d0, q1 = n0 + 2 * KF, q + 1
                if q1 < 12:
                    clear(q1)

                def outer(m, it):
                    dve.wait_ge(strip_used, shifted(d0 + 2 * m + 2, it))
                    g = m if it is None else it * 2 + m
                    dve.scalar_tensor_tensor(out=x[:, g, :], in0=pb[bank(t0 + KF + m)][:, :], scalar=0.5, in1=x[:, g, :],
                                             op0=ALU.mult, op1=ALU.add).then_inc(out_taken, 1)
                    if q1 < 12:
                        add(q1, m, it)
                        if FOLDED[q1]:
                            lowered(q1, m, x, GAIN[q1], it)

                def down(e, it):
                    lo(d0 + e + 2, it)
                    lo(d0 + e + 3, it)
                    outer(e // 2, it)
                    lo(d0 + e + 4, it)
                    lo(d0 + e + 5, it)
                    outer(e // 2 + 1, it)

                with dve.Fori(0, KD // 2 - 1) as i:
                    down(0, i)
                down(2 * KD - 4, None)

            ffn(*ffns[0])

            invert(NMA)
            dve.wait_ge(rstd_done, NMA + 1)
            clear(N2A)

            def pool_product(n):
                lo(POOL + n + 2)
                dve.wait_ge(strip_used, POOL + n + 1)
                for m in range(2):
                    dve.tensor_tensor(hp[:, 2 * POOL_ORDER[n] + m, :], pb[POOL_BANKS[2 * n + m]][:, :], rstd[:, :], ALU.mult).then_inc(out_taken, 1)

            def window_sums(g, steps):
                cur = hp[:, 2 * g:2 * g + 2, :]
                dve.wait_ge(out_taken, T_POOL + 2 * g + 6)
                for level in range(g + 1):
                    d, nxt = 1 << level, (s1, s2)[level % 2]
                    if steps:
                        dve.wait_ge(pool_step, steps)
                    dve.tensor_copy(nxt[:, :, 0:d], cur[:, :, 0:d]).then_inc(pool_step, 1)
                    dve.tensor_tensor(nxt[:, :, d:T], cur[:, :, d:T], cur[:, :, 0:T - d], ALU.add).then_inc(pool_step, 1)
                    steps += 2
                    cur = nxt
                dve.wait_ge(pool_step, steps)
                return cur, steps

            def pool_mean(g, cur, steps):
                w, u = 2 << g, hp[:, 2 * g:2 * g + 2, :]
                if g:
                    dve.wait_ge(x_pooled, 2 * g)
                dve.scalar_tensor_tensor(out=gf[:, :, :], in0=cur[:, :, :], scalar=1.0 / w, in1=u, op0=ALU.mult, op1=ALU.subtract)\
                   .then_inc(pool_step, 1)
                for j in range(2):
                    dve.tensor_tensor(stat[:, 16 * j:16 * j + w - 1], cur[:, j, 0:w - 1], tab("rcount", w - 1), ALU.mult).then_inc(pool_step, 1)
                dve.wait_ge(pool_step, steps + 3)
                for j in range(2):
                    dve.tensor_tensor(gf[:, j, 0:w - 1], stat[:, 16 * j:16 * j + w - 1], u[:, j, 0:w - 1], ALU.subtract).then_inc(pool_step, 1)
                dve.wait_ge(pool_step, steps + 5)
                for j in range(2):
                    m = 2 * g + j
                    dve.scalar_tensor_tensor(out=x[:, m, :], in0=gf[:, j, :], scalar=col("pool_scale", m), in1=x[:, m, :],
                                             op0=ALU.mult, op1=ALU.add).then_inc(x_pooled, 1)
                return steps + 5

            for n in range(4):
                pool_product(n)
            steps = 0
            for g in range(4):
                if g < 2:
                    cur, steps = window_sums(g, steps)
                else:
                    dve.wait_ge(wide_step, 14 if g == 2 else 8)
                    cur = wide[g][g % 2]
                steps = pool_mean(g, cur, steps)
                if g:
                    for m in (2 * g - 2, 2 * g - 1):
                        lowered(N2A, m, x, "ffn2a")
            for m in (6, 7):
                lowered(N2A, m, x, "ffn2a")
            ffn(*ffns[1])
            ffn(*ffns[2])

            for s in range(9):
                lo(M_IN + s + 2)
                if s == 0:
                    invert(NMB)
                    dve.wait_ge(rstd_done, NMB + 1)
                    clear(NQL)
                if s == KQ + 1:
                    invert(NQL)
                dve.wait_ge(strip_used, M_IN + s + 1)
                dve.tensor_tensor(lat[:, s, :], pb[bank(T_MIN + s)][:, :], rstd[:, :], ALU.mult).then_inc(out_taken, 1)
                if s < KQ:
                    add(NQL, s)
                    lowered(NQL, s, lat, "q_norm")
                elif s > KQ:
                    if s == KQ + 1:
                        clear(NKL)
                    add(NKL, s - KQ - 1)
                if s == 5:
                    whole_turn = float(np.float32(6.28125))
                    rest = 2 * np.pi - 6.28125
                    second = float(np.float32(np.floor(rest * 2 ** 20) / 2 ** 20))
                    third = float(np.float32(rest - second))
                    magic = 1.5 * 2.0 ** 23
                    dve.wait_ge(pos_loaded, 16)
                    dve.tensor_copy(posf[:, :], posi[:, :]).then_inc(angle, 1)
                    dve.wait_ge(angle, 1)
                    dve.tensor_scalar(ang[:, :], posf[:, :], tab("inv_freq"), None, ALU.mult).then_inc(angle, 1)
                    dve.wait_ge(angle, 2)
                    dve.tensor_scalar(turns[:, :], ang[:, :], float(1 / (2 * np.pi)), magic, ALU.mult, ALU.add).then_inc(angle, 1)
                    dve.wait_ge(angle, 3)
                    dve.tensor_scalar(turns[:, :], turns[:, :], -magic, None, ALU.add).then_inc(angle, 1)
                    for m, part in enumerate((whole_turn, second, third)):
                        dve.wait_ge(angle, 4 + m)
                        dve.scalar_tensor_tensor(out=ang[:, :], in0=turns[:, :], scalar=-part, in1=ang[:, :], op0=ALU.mult, op1=ALU.add)\
                           .then_inc(angle, 1)
                    dve.wait_ge(angle, 7)
                    pi = float(np.nextafter(np.float32(np.pi), np.float32(0)))
                    dve.tensor_scalar(ang[:, :], ang[:, :], pi, -pi, ALU.min, ALU.max).then_inc(angle, 1)
                    dve.wait_ge(angle, 8)
                    dve.scalar_tensor_tensor(out=turns[:, :], in0=ang[:, :], scalar=-1.0, in1=ang[:, :], op0=ALU.mult, op1=ALU.max)\
                       .then_inc(angle, 1)
                    dve.wait_ge(angle, 9)
                    dve.tensor_scalar(turns[:, :], turns[:, :], -1.0, float(np.float32(np.pi / 2)), ALU.mult, ALU.add).then_inc(angle, 1)

            def head_invert(group):
                dve.wait_ge(hq_std, group + 1)
                dve.reciprocal(head_rstd[group][:, :], head_std[:, :]).then_inc(hq_rstd, 1)

            def head_scale(n):
                dve.wait_ge(spread, n + 1)
                ps = pb[6 + n % 2]
                if n < MH:
                    dve.scalar_tensor_tensor(out=qn[:, n, :], in0=qn[:, n, :], scalar=col("qh_nope"), in1=ps[:, :],
                                             op0=ALU.mult, op1=ALU.mult).then_inc(hq_out, 1)
                elif n < 12:
                    dve.tensor_tensor(qr[:, n - MH, :], qr[:, n - MH, :], ps[:, :], ALU.mult).then_inc(hq_out, 1)
                else:
                    h = n - 12
                    part = slice(64 * (h % 2), 64 * (h % 2) + 64)
                    dve.scalar_tensor_tensor(out=kn[:, h, :], in0=kn[:, h, :], scalar=col("kh_nope"), in1=ps[:, :],
                                             op0=ALU.mult, op1=ALU.mult).then_inc(hq_out, 1)
                    dve.tensor_tensor(kr[part, h, :], krope[part, :], ps[part, :], ALU.mult).then_inc(hq_out, 1)

            for s in range(12):
                lo(M_Q + s + 2)
                if s == 0:
                    dve.wait_ge(rstd_done, NQL + 1)
                    dve.wait_ge(out_taken, T_MIN + 9)
                    dve.tensor_scalar(krope[:, :], lat[:, 8, :], col("kh_rope"), None, ALU.mult).then_inc(gained, 1)
                dve.wait_ge(strip_used, M_Q + s + 1)
                dst = qr[:, s, :] if s < 4 else qn[:, s - 4, :]
                dve.tensor_tensor(dst, pb[bank(T_MQ + s)][:, :], rstd_q[:, :], ALU.mult).then_inc(out_taken, 1)
                if 1 <= s <= 4:
                    dve.wait_ge(hq_sq, s)
                    dve.wait_ge(out_taken, T_MQ + s)
                    dve.tensor_scalar(qr[:, s - 1, :], qr[:, s - 1, :], col("qh_rope"), None, ALU.mult).then_inc(gained, 1)
                if 2 <= s <= 6:
                    r = s - 2
                    dve.wait_ge(sines, 2)
                    rope_finish(krope[:, :] if r == 0 else qr[:, r - 1, :], pb[7 - r % 2][:, :], rope2[:, 1, :], rope2[:, 0, :],
                                rope_tmp[:, :], 5 + r)
                if s == 7:
                    invert(NKL)
                if s == 9:
                    norm_low(NKL, lat[:, KQ:KD, :], lambda k: col("kv_norm", k), nH[:, KQ:KD, :], nL[:, KQ:KD, :])
            head_invert(0)
            dve.wait_ge(rope_done, 10)
            lo(M_K + 2)
            for n in range(6):
                head_scale(n)
            lo(M_K + 3)
            head_invert(1)
            for n in range(6, 12):
                head_scale(n)
            lo(M_OUT)
            lo(M_OUT + 1)
            dve.wait_ge(kr_cleared, 1)
            dve.wait_ge(out_taken, T_MV)
            for n in range(12, 20):
                head_scale(n)

            def soft_max(u):
                h, b = divmod(u, NB)
                w = (b + 1) * P
                m2 = stat[:, 32 + u % 4:33 + u % 4]
                dve.wait_ge(scored, 32 + u + 1)
                if u >= 4:
                    dve.wait_ge(p_turned, 32 + u - 3)
                else:
                    dve.wait_ge(mask_loaded, 16)
                dve.tensor_tensor_reduce(prob2[:, u % 4, 0:w], pb[S2[u % 4]][:, 0:w], cmask[:, T - w:T], 1.0, -3e38,
                                         ALU.add, ALU.max, m2).then_inc(masked, 1)
                dve.wait_ge(masked, 32 + u + 1)
                dve.tensor_scalar(stat[:, 16 + u % 4:17 + u % 4], m2, -SCALE2, None, ALU.mult).then_inc(bias_ready, 1)

            for u in range(MH * NB + LAG + 3):
                if u < MH * NB:
                    soft_max(u)
                if 1 <= u <= MH * NB:
                    invert_sum(32 + u - 1)
                    scale_probs(32 + u - 1, prob2[:, (u - 1) % 4, 0:((u - 1) % NB + 1) * P])
                if head_at(u - LAG - 3) is not None:
                    h = head_at(u - LAG - 3)
                    dve.wait_ge(att_hi, NB + h + 1)
                    dve.tensor_tensor(oL[:, h, :], pb[4 + h % 2][:, :], oH[:, h, :], ALU.subtract).then_inc(att_lo, 1)

            residual(M_OUT, T_MOUT, N2B, lambda m: ones[:, 0:1], "ffn2b")
            ffn(*ffns[3])


def kernel(**inputs):
    import numpy as _np
    import concourse.bacc as _bacc
    from concourse import mybir as _mybir
    from concourse.bass_utils import run_bass_kernel_spmd as _run

    a = {k: _np.asarray(v) for k, v in inputs.items()}

    def features(v):
        return v.reshape(-1, P).T

    def tokens(v):
        n, d = v.shape
        return v.T.reshape(d // P, P, n).transpose(1, 0, 2).reshape(P, -1)

    def strips(w, per=1, halves=1):
        k, m = w.shape
        w = w.reshape(halves, k // P // halves, P, m // P // per, per, P)
        return w.transpose(3, 0, 2, 4, 1, 5).reshape(m // P // per * halves, P, -1)

    heads = _np.arange(H * HD).reshape(H, HD)
    paired = _np.concatenate([_np.concatenate([heads[i], heads[i + 4]]) for i in range(4)])
    att, kv = H * HD, 2 * HD
    cw = D - att
    cols_in = [_np.arange(att, att + kv), _np.arange(att + kv, att + 2 * kv), paired]
    c0 = att + 2 * kv
    for i in range(4):
        for part in (1, 2, 0):
            cols_in.append(c0 + part * cw + _np.arange(i * P, (i + 1) * P))
    cols_in = _np.concatenate(cols_in)
    rows_out = _np.concatenate([paired, _np.arange(att, D)])
    qcols = _np.arange(MH * (NOPE + ROPE)).reshape(MH, NOPE + ROPE)
    qcols = _np.concatenate([qcols[:, NOPE:].ravel(), qcols[:, :NOPE].ravel()])
    kvcols = _np.arange(MH * 2 * NOPE).reshape(MH, 2 * NOPE)
    lat_cols = _np.concatenate([_np.arange(D + ROPE), _np.arange(D, D + ROPE)])
    kv_up = a["mla_w_kv_up_2"][0]
    wv = kv_up[:, kvcols[:, NOPE:].ravel()].reshape(2, P, 2, 512).transpose(2, 1, 0, 3).reshape(2, P, 1024)

    by_tile = [a[n][0].reshape(PAIRS, 2, 8, P, 1024).transpose(0, 2, 3, 1, 4) for n in ("w_gate", "w_up", "w_down")]
    experts = _np.concatenate([_np.stack(by_tile[:2], 2).reshape(PAIRS, 16, P, 2, 1024), by_tile[2]], 1)

    vec = {
        "c": features(a["c"][0]), "cctx": features(a["c_ctx"]), "b_ada": features(a["b_ada"][0]),
        "g_mix": features(a["g_mix"][0]), "g_ffn": features(a["g_ffn"][0]),
        "conv_w": a["conv_w"][0].reshape(3, 4, P).transpose(2, 1, 0).reshape(P, 12),
        "sink": _np.broadcast_to(a["sink"][0][None], (P, H)),
        "ffn1a": features(a["ffn1_norm_2"][0]), "ffn1b": features(a["ffn1_norm_2"][1]),
        "ffn2a": features(a["ffn2_norm_2"][0]), "ffn2b": features(a["ffn2_norm_2"][1]),
        "mixa": features(a["mix_norm_2"][0]), "mixb": features(a["mix_norm_2"][1]),
        "pool_scale": features(a["pool_scale_2"][0]), "q_norm": features(a["mla_q_norm_2"][0]),
        "kv_norm": features(a["mla_kv_norm_2"][0]),
        "qh_nope": a["mla_q_head_norm_2"][0][:NOPE, None], "qh_rope": _np.tile(a["mla_q_head_norm_2"][0][NOPE:], 2)[:, None],
        "kh_nope": a["mla_k_head_norm_2"][0][:NOPE, None], "kh_rope": _np.tile(a["mla_k_head_norm_2"][0][NOPE:], 2)[:, None],
        "g_final": features(a["g_final"]),
    }
    tabs, window, causal, rope, select = shape_tables()
    arrays = {
        "cols": _np.concatenate([vec[n] for n, _ in _names], 1),
        "tabs": tabs, "window": window, "causal": causal, "select": select, "rope": rope,
        "positions": _np.broadcast_to(a["positions_2"], (P, T)),
        "ctx": tokens(a["ctx"][0]), "x": tokens(a["x"][0]),
        "w_ada": a["w_ada"][0],
        "w_in": strips(a["w_in"][0][:, cols_in]),
        "w_out": strips(a["w_out"][0][rows_out]),
        "w_router": a["w_router"][0].reshape(KD, P, E).transpose(1, 0, 2).reshape(P, -1),
        "experts": experts.reshape(PAIRS, 24, P, 2 * 1024),
        "pool_w": _np.stack([strips(a["pool_w_2"][0][g], per=2)[0] for g in (3, 2, 0, 1)]),
        "mla_in": strips(a["mla_w_in_2"][0][:, lat_cols]),
        "q_up": strips(a["mla_w_q_up_2"][0][:, qcols]),
        "kv_up": _np.concatenate([strips(kv_up[:, kvcols[:, :NOPE].ravel()], per=4), wv]),
        "mla_out": strips(a["mla_w_out_2"][0]),
    }
    for f in range(4):
        n, layer = ("ffn1", "ffn2")[f % 2], f // 2
        arrays[f"gate{f}"] = strips(a[f"{n}_w_gate_2"][layer])
        arrays[f"up{f}"] = strips(a[f"{n}_w_up_2"][layer])
        arrays[f"down{f}"] = strips(a[f"{n}_w_down_2"][layer], halves=2)

    nc = _bacc.Bacc("TRN2", target_bir_lowering=False, num_devices=1)
    given, handles = {}, {}
    for name, v in arrays.items():
        v = _np.ascontiguousarray(v)
        given[f"in_{name}"] = v
        handles[name] = nc.dram_tensor(f"in_{name}", v.shape, _mybir.dt.from_np(v.dtype), kind="ExternalInput").ap()
    for name in ("gate", "up", "down"):
        handles[name] = [handles[f"{name}{f}"] for f in range(4)]
    out = nc.dram_tensor("out", (P, KD * T), _mybir.dt.float32, kind="ExternalOutput").ap()
    build(nc, handles, out)
    r = _run(nc, [given], core_ids=[0])
    got = r.results[0]["out"].reshape(P, KD, T).transpose(2, 1, 0).reshape(1, T, D)
    return _np.ascontiguousarray(got)
```
